# Optimizing a Trainium2 kernel written in Bass

```python
import jax, jax.numpy as jnp
from jax import lax
import numpy as np

D_MODEL = 1024
BATCH = 1
SEQ = 256
DEPTH = 2

HEAD_DIM = 64
A_HEADS = 8
A_KV_HEADS = 2
B_GROUPS = ((128, 1), (512, 4), (2048, 16))
B_HEADS_PER_GROUP = 4
B_HEADS = len(B_GROUPS) * B_HEADS_PER_GROUP
GRID_W = 64
ROPE_THETA = 10000.0
Q_BLOCK = 128
N_EXPERTS = 16
N_GROUPS = 4
EXPERTS_PER_GROUP = N_EXPERTS // N_GROUPS
TOP_K = 2
D_EXPERT = 256
LN_EPS = 1e-5
RMS_EPS = 1e-6
DN_ALPHA = (2.0 * DEPTH) ** 0.25
DN_BETA = (8.0 * DEPTH) ** -0.25

A_Q = A_HEADS * HEAD_DIM
A_KV = A_KV_HEADS * HEAD_DIM
B_W = B_HEADS * HEAD_DIM
B_OUT = B_HEADS_PER_GROUP * HEAD_DIM
N_IN = A_Q + 2 * A_KV + 3 * B_W + 2 * D_MODEL
IN_SPLITS = (A_Q, A_Q + A_KV, A_Q + 2 * A_KV, A_Q + 2 * A_KV + B_W,
             A_Q + 2 * A_KV + 2 * B_W, A_Q + 2 * A_KV + 3 * B_W)


def _layer_norm(x, g=None, b=None):
    xf = x.astype(jnp.float32)
    mu = jnp.mean(xf, -1, keepdims=True)
    var = jnp.mean(jnp.square(xf - mu), -1, keepdims=True)
    y = (xf - mu) * lax.rsqrt(var + LN_EPS)
    if g is not None:
        y = y * g.astype(jnp.float32) + b.astype(jnp.float32)
    return y.astype(x.dtype)

def _rms_norm(x, g):
    xf = x.astype(jnp.float32)
    y = xf * lax.rsqrt(jnp.mean(jnp.square(xf), -1, keepdims=True) + RMS_EPS)
    return (y * g.astype(jnp.float32)).astype(x.dtype)

def _axial_rope_tables(seq):
    rows = seq // GRID_W
    row = jnp.repeat(jnp.arange(rows), GRID_W).astype(jnp.float32)
    col = jnp.tile(jnp.arange(GRID_W), rows).astype(jnp.float32)
    axis_dim = HEAD_DIM // 2
    inv = ROPE_THETA ** (-jnp.arange(0, axis_dim, 2, dtype=jnp.float32) / axis_dim)
    ang = jnp.concatenate([row[:, None] * inv, col[:, None] * inv], -1)
    return jnp.cos(ang), jnp.sin(ang)

def _apply_rope(x, cos, sin):
    xf = x.astype(jnp.float32).reshape(x.shape[:-1] + (HEAD_DIM // 2, 2))
    x0, x1 = xf[..., 0], xf[..., 1]
    c = cos[None, :, None, :]
    s = sin[None, :, None, :]
    out = jnp.stack([x0 * c - x1 * s, x0 * s + x1 * c], -1).reshape(x.shape)
    return out.astype(x.dtype)

def _alibi_slopes(n):
    return jnp.exp2(-8.0 * jnp.arange(1, n + 1, dtype=jnp.float32) / n)

def _global_gqa(q, k, v):
    b, s = q.shape[0], q.shape[1]
    rep = A_HEADS // A_KV_HEADS
    nblk = s // Q_BLOCK
    scale = HEAD_DIM ** -0.5
    qb = q.reshape(b, nblk, Q_BLOCK, A_KV_HEADS, rep, HEAD_DIM).transpose(1, 0, 2, 3, 4, 5)

    def block(qi):
        sc = jnp.einsum('bqgrd,bkgd->bgrqk', qi, k).astype(jnp.float32) * scale
        p = jax.nn.softmax(sc, axis=-1)
        return jnp.einsum('bgrqk,bkgd->bqgrd', p.astype(v.dtype), v)

    o = lax.map(block, qb)
    return o.transpose(1, 0, 2, 3, 4, 5).reshape(b, s, A_Q)

def _dilated_group(q, k, v, window, dilation, slopes):
    b, s, h = q.shape[0], q.shape[1], q.shape[2]
    reach = window // (2 * dilation)
    offs = dilation * jnp.arange(-reach, reach + 1)
    nblk = s // Q_BLOCK
    scale = HEAD_DIM ** -0.5
    qb = q.reshape(b, nblk, Q_BLOCK, h, HEAD_DIM).transpose(1, 0, 2, 3, 4)
    starts = jnp.arange(nblk) * Q_BLOCK
    bias = -slopes[:, None] * jnp.abs(offs).astype(jnp.float32)[None, :]

    def block(args):
        qi, t0 = args
        pos = t0 + jnp.arange(Q_BLOCK)[:, None] + offs[None, :]
        valid = (pos >= 0) & (pos < s)
        idx = jnp.clip(pos, 0, s - 1)
        kg = jnp.take(k, idx, axis=1)
        vg = jnp.take(v, idx, axis=1)
        sc = jnp.einsum('bqhd,bqkhd->bhqk', qi, kg).astype(jnp.float32) * scale + bias[None, :, None, :]
        sc = jnp.where(valid[None, None], sc, -jnp.inf)
        lse = jax.nn.logsumexp(sc, axis=-1)
        p = jnp.exp(sc - lse[..., None])
        o = jnp.einsum('bhqk,bqkhd->bqhd', p.astype(v.dtype), vg)
        return o, lse.transpose(0, 2, 1)

    o, lse = lax.map(block, (qb, starts))
    o = o.transpose(1, 0, 2, 3, 4).reshape(b, s, h, HEAD_DIM)
    lse = lse.transpose(1, 0, 2, 3).reshape(b, s, h)
    return o, lse

def _mixer(h, w_in, qn_g, kn_g, w_pa, w_pb, w_o, cos, sin, slopes):
    b, s, _ = h.shape
    proj = h @ w_in
    qa, ka, va, qd, kd, vd, gates = jnp.split(proj, IN_SPLITS, axis=-1)
    qa = _apply_rope(_rms_norm(qa.reshape(b, s, A_HEADS, HEAD_DIM), qn_g), cos, sin)
    ka = _apply_rope(_rms_norm(ka.reshape(b, s, A_KV_HEADS, HEAD_DIM), kn_g), cos, sin)
    va = va.reshape(b, s, A_KV_HEADS, HEAD_DIM)
    out_a = _global_gqa(qa, ka, va)
    qd = qd.reshape(b, s, B_HEADS, HEAD_DIM)
    kd = kd.reshape(b, s, B_HEADS, HEAD_DIM)
    vd = vd.reshape(b, s, B_HEADS, HEAD_DIM)
    outs, lses = [], []
    for g, (window, dilation) in enumerate(B_GROUPS):
        sl = slice(g * B_HEADS_PER_GROUP, (g + 1) * B_HEADS_PER_GROUP)
        o, l = _dilated_group(qd[:, :, sl], kd[:, :, sl], vd[:, :, sl], window, dilation, slopes[sl])
        outs.append(o)
        lses.append(l)
    wts = jax.nn.softmax(jnp.stack(lses, 0), axis=0)
    out_b = jnp.sum(wts[..., None].astype(h.dtype) * jnp.stack(outs, 0), 0).reshape(b, s, B_OUT)
    g_a, g_b = jnp.split(jax.nn.sigmoid(gates), 2, axis=-1)
    merged = g_a * (out_a @ w_pa) + g_b * (out_b @ w_pb)
    return merged @ w_o

def _moe(h, w_router, router_bias, w_gate, w_up, w_down):
    b, s, d = h.shape
    t = h.reshape(b * s, d)
    scores = jax.nn.sigmoid((t @ w_router).astype(jnp.float32))
    sel = scores + router_bias.astype(jnp.float32)
    grp_score = jnp.sum(lax.top_k(sel.reshape(-1, N_GROUPS, EXPERTS_PER_GROUP), TOP_K)[0], -1)
    best = jnp.argmax(grp_score, axis=-1)
    in_group = (jnp.arange(N_EXPERTS) // EXPERTS_PER_GROUP)[None, :] == best[:, None]
    _, idx = lax.top_k(jnp.where(in_group, sel, -jnp.inf), TOP_K)
    top_s = jnp.take_along_axis(scores, idx, axis=-1)
    gate = top_s / jnp.sum(top_s, -1, keepdims=True)
    combine = jnp.sum(jax.nn.one_hot(idx, N_EXPERTS, dtype=jnp.float32) * gate[..., None], 1)
    hg = jnp.einsum('td,edf->tef', t, w_gate)
    hu = jnp.einsum('td,edf->tef', t, w_up)
    act = jax.nn.silu(hg) * hu * combine[..., None].astype(t.dtype)
    y = jnp.einsum('tef,efd->td', act, w_down)
    return y.reshape(b, s, d)

def first_inputs(seed: int = 0) -> dict:
    key = jax.random.key(seed)
    ks = jax.random.split(key, 24)
    f32 = jnp.float32
    n = lambda k, shape, sc: jax.random.normal(k, shape, f32) * sc
    d = D_MODEL
    return {
        "x": n(ks[0], (BATCH, SEQ, d), 1.0),
        "c": n(ks[1], (BATCH, d), 1.0),
        "w_ada": n(ks[2], (DEPTH, d, 6 * d), 0.5 * d ** -0.5),
        "b_ada": n(ks[3], (DEPTH, 6 * d), 0.02),
        "w_in": n(ks[4], (DEPTH, d, N_IN), d ** -0.5),
        "q_norm_g": 1.0 + n(ks[5], (DEPTH, HEAD_DIM), 0.02),
        "k_norm_g": 1.0 + n(ks[6], (DEPTH, HEAD_DIM), 0.02),
        "w_branch_a": n(ks[7], (DEPTH, A_Q, d), A_Q ** -0.5),
        "w_branch_b": n(ks[8], (DEPTH, B_OUT, d), B_OUT ** -0.5),
        "w_out": n(ks[9], (DEPTH, d, d), DN_BETA * d ** -0.5),
        "ln1_g": 1.0 + n(ks[10], (DEPTH, d), 0.02),
        "ln1_b": n(ks[11], (DEPTH, d), 0.02),
        "w_router": n(ks[12], (d, N_EXPERTS), d ** -0.5),
        "router_bias": n(ks[13], (N_EXPERTS,), 0.01),
        "w_exp_gate": n(ks[14], (DEPTH, N_EXPERTS, d, D_EXPERT), d ** -0.5),
        "w_exp_up": n(ks[15], (DEPTH, N_EXPERTS, d, D_EXPERT), d ** -0.5),
        "w_exp_down": n(ks[16], (DEPTH, N_EXPERTS, D_EXPERT, d), DN_BETA * D_EXPERT ** -0.5),
        "ln2_g": 1.0 + n(ks[17], (DEPTH, d), 0.02),
        "ln2_b": n(ks[18], (DEPTH, d), 0.02),
    }

def first_block(x, c, w_ada, b_ada, w_in, q_norm_g, k_norm_g, w_branch_a, w_branch_b, w_out,
              ln1_g, ln1_b, w_router, router_bias, w_exp_gate, w_exp_up, w_exp_down, ln2_g, ln2_b):
    s = x.shape[1]
    cos, sin = _axial_rope_tables(s)
    slopes = _alibi_slopes(B_HEADS)
    cond = jax.nn.silu(c)
    for l in range(DEPTH):
        mod = cond @ w_ada[l] + b_ada[l]
        sh1, sc1, g1, sh2, sc2, g2 = [m[:, None, :] for m in jnp.split(mod, 6, axis=-1)]
        h = _layer_norm(x) * (1.0 + sc1) + sh1
        mix = _mixer(h, w_in[l], q_norm_g[l], k_norm_g[l], w_branch_a[l], w_branch_b[l],
                     w_out[l], cos, sin, slopes)
        x = _layer_norm(DN_ALPHA * x + g1 * mix, ln1_g[l], ln1_b[l])
        h = _layer_norm(x) * (1.0 + sc2) + sh2
        ffn = _moe(h, w_router, router_bias, w_exp_gate[l], w_exp_up[l], w_exp_down[l])
        x = _layer_norm(DN_ALPHA * x + g2 * ffn, ln2_g[l], ln2_b[l])
    return x


N_MEM = 256
N_BRANCH = 4
BRANCH_WIDTH = D_MODEL // N_BRANCH
IN_WIDTH = 9 * BRANCH_WIDTH
RET_HEADS = BRANCH_WIDTH // HEAD_DIM
RET_CHUNK = 128
POOL_WINDOWS = (2, 4, 8, 16)
POOL_GROUPS = len(POOL_WINDOWS)
POOL_GROUP_DIM = BRANCH_WIDTH // POOL_GROUPS
NA_HEADS = BRANCH_WIDTH // HEAD_DIM
NA_WIN_ROWS = 8
NA_WIN_COLS = 16
NA_QBLOCK_COLS = 16
NA_KBLOCK_COLS = 2 * NA_QBLOCK_COLS
MEM_HEADS = BRANCH_WIDTH // HEAD_DIM
FF_HIDDEN = -(-8 * D_MODEL // (3 * 256)) * 256
NEG_INF = -1e30
EPS = 1e-6


def rms_norm(x, g):
    xf = x.astype(jnp.float32)
    y = xf * lax.rsqrt(jnp.mean(xf * xf, axis=-1, keepdims=True) + EPS)
    return (y * g.astype(jnp.float32)).astype(x.dtype)

def split_heads(t, n_heads):
    b, s, _ = t.shape
    return t.reshape(b, s, n_heads, -1).transpose(0, 2, 1, 3)

def merge_heads(t):
    b, h, s, d = t.shape
    return t.transpose(0, 2, 1, 3).reshape(b, s, h * d)

def rotary(t, pos):
    half = t.shape[-1] // 2
    inv = ROPE_THETA ** (-jnp.arange(half, dtype=jnp.float32) / half)
    ang = pos[:, None] * inv[None, :]
    cos, sin = jnp.cos(ang), jnp.sin(ang)
    tf = t.astype(jnp.float32)
    t1, t2 = tf[..., :half], tf[..., half:]
    return jnp.concatenate([t1 * cos - t2 * sin, t1 * sin + t2 * cos], axis=-1).astype(t.dtype)

def retention_dir(q, k, v, log_gamma, include_diag):
    b, h, s, d = q.shape
    c = RET_CHUNK
    n = s // c
    dt = q.dtype
    qc, kc, vc = (t.reshape(b, h, n, c, d) for t in (q, k, v))
    idx = jnp.arange(c, dtype=jnp.float32)
    diff = idx[:, None] - idx[None, :]
    mask = (diff >= 0) if include_diag else (diff > 0)
    lg = log_gamma.astype(jnp.float32)[:, None]
    d_intra = jnp.where(mask[None], jnp.exp(jnp.where(mask, diff, 0.0)[None] * lg[:, :, None]), 0.0)
    scores = jnp.einsum('bhncd,bhnmd->bhncm', qc, kc) * d_intra[None, :, None].astype(dt)
    intra = jnp.einsum('bhncm,bhnme->bhnce', scores, vc)
    k_decay = jnp.exp((c - 1 - idx)[None, :] * lg).astype(dt)
    kv = jnp.einsum('bhncd,bhnce->nbhde', kc * k_decay[None, :, None, :, None], vc)
    chunk_decay = jnp.exp(c * lg[:, 0]).astype(dt)[None, :, None, None]

    def step(state, kv_n):
        return chunk_decay * state + kv_n, state

    _, states = lax.scan(step, jnp.zeros_like(kv[0]), kv)
    q_decay = jnp.exp((idx + 1)[None, :] * lg).astype(dt)
    cross = jnp.einsum('bhncd,nbhde->bhnce', qc * q_decay[None, :, None, :, None], states)
    return (intra + cross).reshape(b, h, s, d)

def bidirectional_retention(q, k, v, log_gamma_fwd, log_gamma_bwd):
    fwd = retention_dir(q, k, v, log_gamma_fwd, True)
    flip = lambda t: jnp.flip(t, axis=2)
    bwd = flip(retention_dir(flip(q), flip(k), flip(v), log_gamma_bwd, False))
    return fwd + bwd

def multiscale_pool(v, w_group, scale):
    b, s, cw = v.shape
    vg = v.reshape(b, s, POOL_GROUPS, POOL_GROUP_DIM)
    cs = jnp.cumsum(vg.astype(jnp.float32), axis=1)
    cs = jnp.concatenate([jnp.zeros_like(cs[:, :1]), cs], axis=1)
    t = np.arange(s)[:, None]
    half = np.array(POOL_WINDOWS)[None, :] // 2
    lo = np.clip(t - half, 0, s)
    hi = np.clip(t + half, 0, s)
    g_idx = np.arange(POOL_GROUPS)[None, :]
    win_sum = cs[:, hi, g_idx] - cs[:, lo, g_idx]
    count = jnp.asarray((hi - lo)[None, :, :, None], dtype=jnp.float32)
    pooled = (win_sum / count).astype(v.dtype) - vg
    mixed = jnp.einsum('bsgc,gce->bsge', pooled, w_group)
    return mixed.reshape(b, s, cw) * scale

def neighbourhood_attention(q, k, v, rpb):
    b, h, s, d = q.shape
    rows = s // GRID_W
    wr = min(NA_WIN_ROWS, rows)
    n_cb = GRID_W // NA_QBLOCK_COLS
    r = np.arange(rows)
    row_idx = np.clip(r - wr // 2, 0, rows - wr)[:, None] + np.arange(wr)[None, :]
    cb = np.arange(n_cb)
    kcol_idx = np.clip(cb * NA_QBLOCK_COLS - NA_WIN_COLS // 2, 0, GRID_W - NA_KBLOCK_COLS)[:, None] \
        + np.arange(NA_KBLOCK_COLS)[None, :]
    qcol = cb[:, None] * NA_QBLOCK_COLS + np.arange(NA_QBLOCK_COLS)[None, :]
    qwin = np.clip(qcol - NA_WIN_COLS // 2, 0, GRID_W - NA_WIN_COLS)
    col_mask = (kcol_idx[:, None, :] >= qwin[:, :, None]) & (kcol_idx[:, None, :] < qwin[:, :, None] + NA_WIN_COLS)
    row_off = row_idx - r[:, None]
    col_off = np.clip(kcol_idx[:, None, :] - qcol[:, :, None], -(NA_WIN_COLS - 1), NA_WIN_COLS - 1)
    bias = rpb[:, row_off[:, None, None, :, None] + NA_WIN_ROWS - 1,
               col_off[None, :, :, None, :] + NA_WIN_COLS - 1]
    bias = jnp.where(col_mask[None, None, :, :, None, :], bias.astype(jnp.float32), NEG_INF)

    qg = q.reshape(b, h, rows, n_cb, NA_QBLOCK_COLS, d)
    k_grid = k.reshape(b, h, rows, GRID_W, d)
    v_grid = v.reshape(b, h, rows, GRID_W, d)
    ri = row_idx[:, None, :, None]
    ci = kcol_idx[None, :, None, :]
    kg = k_grid[:, :, ri, ci]
    vg = v_grid[:, :, ri, ci]
    sc = jnp.einsum('bhrnqd,bhrnwkd->bhrnqwk', qg, kg).astype(jnp.float32) * (d ** -0.5) + bias[None]
    p = jax.nn.softmax(sc, axis=(-2, -1))
    o = jnp.einsum('bhrnqwk,bhrnwkd->bhrnqd', p.astype(v.dtype), vg)
    return o.reshape(b, h, s, d)

def memory_attention(q, mk, mv):
    sc = jnp.einsum('bhsd,bhmd->bhsm', q, mk).astype(jnp.float32) * (q.shape[-1] ** -0.5)
    p = jax.nn.softmax(sc, axis=-1)
    return jnp.einsum('bhsm,bhmd->bhsd', p.astype(mv.dtype), mv)

def hybrid_layer(x, mem, norm_mix_g, norm_mem_g, w_in, w_gate, ret_decay_fwd, ret_decay_bwd,
                 ret_norm_g, pool_w, pool_scale, na_q_norm_g, na_k_norm_g, na_rpb,
                 mem_q_norm_g, mem_k_norm_g, w_mem_kv, w_branch, w_out, norm_ffn_g,
                 w_ffn_in, w_ffn_out):
    b, s, dm = x.shape
    h = rms_norm(x, norm_mix_g)
    proj = h @ w_in
    rq, rk, rv, rg, pv, nq, nk, nv, mq = jnp.split(proj, 9, axis=-1)

    pos = jnp.arange(s, dtype=jnp.float32)
    rq_h = rotary(split_heads(rq, RET_HEADS), pos) * (HEAD_DIM ** -0.5)
    rk_h = rotary(split_heads(rk, RET_HEADS), pos)
    ret = bidirectional_retention(rq_h, rk_h, split_heads(rv, RET_HEADS),
                                  jax.nn.log_sigmoid(ret_decay_fwd.astype(jnp.float32)),
                                  jax.nn.log_sigmoid(ret_decay_bwd.astype(jnp.float32)))
    ret = merge_heads(rms_norm(ret, ret_norm_g.reshape(RET_HEADS, 1, HEAD_DIM))) * jax.nn.silu(rg)

    pool = multiscale_pool(pv, pool_w, pool_scale)

    na = merge_heads(neighbourhood_attention(rms_norm(split_heads(nq, NA_HEADS), na_q_norm_g),
                                             rms_norm(split_heads(nk, NA_HEADS), na_k_norm_g),
                                             split_heads(nv, NA_HEADS), na_rpb))

    mk, mv = jnp.split(rms_norm(mem, norm_mem_g) @ w_mem_kv, 2, axis=-1)
    mo = merge_heads(memory_attention(rms_norm(split_heads(mq, MEM_HEADS), mem_q_norm_g),
                                      rms_norm(split_heads(mk, MEM_HEADS), mem_k_norm_g),
                                      split_heads(mv, MEM_HEADS)))

    branches = jnp.stack([ret, pool, na, mo], axis=2)
    up = jnp.einsum('bsnc,ncd->bsnd', branches, w_branch)
    gates = jax.nn.sigmoid(h @ w_gate).reshape(b, s, N_BRANCH, dm)
    merged = jnp.einsum('bsnd,bsnd->bsd', gates, up)
    x = x + merged @ w_out

    a, g = jnp.split(rms_norm(x, norm_ffn_g) @ w_ffn_in, 2, axis=-1)
    return x + (jax.nn.silu(a) * g) @ w_ffn_out

def second_inputs(seed: int = 0) -> dict:
    key = jax.random.key(seed)
    ks = jax.random.split(key, 22)
    f32 = jnp.float32
    L, D, BW = DEPTH, D_MODEL, BRANCH_WIDTH

    def nrm(k, shape, scale):
        return jax.random.normal(k, shape, f32) * scale

    base_logit = jnp.log(2.0 ** (5.0 + jnp.arange(RET_HEADS, dtype=f32)) - 1.0)
    return {
        "x": nrm(ks[0], (BATCH, SEQ, D), 1.0),
        "mem": nrm(ks[1], (BATCH, N_MEM, D), 1.0),
        "norm_mix_g": 1.0 + nrm(ks[2], (L, D), 0.02),
        "norm_mem_g": 1.0 + nrm(ks[3], (L, D), 0.02),
        "w_in": nrm(ks[4], (L, D, IN_WIDTH), D ** -0.5),
        "w_gate": nrm(ks[5], (L, D, N_BRANCH * D), D ** -0.5),
        "ret_decay_fwd": base_logit[None, :] + nrm(ks[6], (L, RET_HEADS), 0.1),
        "ret_decay_bwd": base_logit[None, :] + nrm(ks[7], (L, RET_HEADS), 0.1),
        "ret_norm_g": 1.0 + nrm(ks[8], (L, BW), 0.02),
        "pool_w": nrm(ks[9], (L, POOL_GROUPS, POOL_GROUP_DIM, POOL_GROUP_DIM), POOL_GROUP_DIM ** -0.5),
        "pool_scale": 1.0 + nrm(ks[10], (L, BW), 0.02),
        "na_q_norm_g": 1.0 + nrm(ks[11], (L, HEAD_DIM), 0.02),
        "na_k_norm_g": 1.0 + nrm(ks[12], (L, HEAD_DIM), 0.02),
        "na_rpb": nrm(ks[13], (L, NA_HEADS, 2 * NA_WIN_ROWS - 1, 2 * NA_WIN_COLS - 1), 0.02),
        "mem_q_norm_g": 1.0 + nrm(ks[14], (L, HEAD_DIM), 0.02),
        "mem_k_norm_g": 1.0 + nrm(ks[15], (L, HEAD_DIM), 0.02),
        "w_mem_kv": nrm(ks[16], (L, D, 2 * BW), D ** -0.5),
        "w_branch": nrm(ks[17], (L, N_BRANCH, BW, D), BW ** -0.5),
        "w_out": nrm(ks[18], (L, D, D), D ** -0.5),
        "norm_ffn_g": 1.0 + nrm(ks[19], (L, D), 0.02),
        "w_ffn_in": nrm(ks[20], (L, D, 2 * FF_HIDDEN), D ** -0.5),
        "w_ffn_out": nrm(ks[21], (L, FF_HIDDEN, D), FF_HIDDEN ** -0.5),
    }

def second_block(x, mem, norm_mix_g, norm_mem_g, w_in, w_gate, ret_decay_fwd, ret_decay_bwd,
              ret_norm_g, pool_w, pool_scale, na_q_norm_g, na_k_norm_g, na_rpb,
              mem_q_norm_g, mem_k_norm_g, w_mem_kv, w_branch, w_out, norm_ffn_g,
              w_ffn_in, w_ffn_out):
    for l in range(DEPTH):
        x = hybrid_layer(x, mem, norm_mix_g[l], norm_mem_g[l], w_in[l], w_gate[l],
                         ret_decay_fwd[l], ret_decay_bwd[l], ret_norm_g[l], pool_w[l],
                         pool_scale[l], na_q_norm_g[l], na_k_norm_g[l], na_rpb[l],
                         mem_q_norm_g[l], mem_k_norm_g[l], w_mem_kv[l], w_branch[l],
                         w_out[l], norm_ffn_g[l], w_ffn_in[l], w_ffn_out[l])
    return x


def setup_inputs(seed=0):
    out = dict(first_inputs(seed))
    for name, value in second_inputs(seed + 1).items():
        if name != "x":
            out[name + "_2"] = value
    return out


def reference(
    x, c, w_ada, b_ada, w_in, q_norm_g, k_norm_g, w_branch_a, w_branch_b, w_out, ln1_g, ln1_b,
    w_router, router_bias, w_exp_gate, w_exp_up, w_exp_down, ln2_g, ln2_b, mem_2, norm_mix_g_2,
    norm_mem_g_2, w_in_2, w_gate_2, ret_decay_fwd_2, ret_decay_bwd_2, ret_norm_g_2, pool_w_2,
    pool_scale_2, na_q_norm_g_2, na_k_norm_g_2, na_rpb_2, mem_q_norm_g_2, mem_k_norm_g_2,
    w_mem_kv_2, w_branch_2, w_out_2, norm_ffn_g_2, w_ffn_in_2, w_ffn_out_2,
):
    x = first_block(
        x, c, w_ada, b_ada, w_in, q_norm_g, k_norm_g, w_branch_a, w_branch_b, w_out, ln1_g,
        ln1_b, w_router, router_bias, w_exp_gate, w_exp_up, w_exp_down, ln2_g, ln2_b,
    )
    return second_block(
        x, mem_2, norm_mix_g_2, norm_mem_g_2, w_in_2, w_gate_2, ret_decay_fwd_2,
        ret_decay_bwd_2, ret_norm_g_2, pool_w_2, pool_scale_2, na_q_norm_g_2, na_k_norm_g_2,
        na_rpb_2, mem_q_norm_g_2, mem_k_norm_g_2, w_mem_kv_2, w_branch_2, w_out_2, norm_ffn_g_2,
        w_ffn_in_2, w_ffn_out_2,
    )


_drawn_inputs = setup_inputs


def setup_inputs(seed=0):
    import zlib

    import numpy as np

    out = dict(_drawn_inputs(seed))
    spreads = {}
    factors = {'b_ada': 2.77,
     'q_norm_g': 8.0,
     'k_norm_g': 8.0,
     'norm_mem_g_2': 8.0,
     'ret_norm_g_2': 6.711,
     'pool_scale_2': 4.303,
     'na_q_norm_g_2': 8.0,
     'na_k_norm_g_2': 8.0,
     'na_rpb_2': 64.0,
     'mem_q_norm_g_2': 8.0,
     'mem_k_norm_g_2': 8.0,
     'norm_ffn_g_2': 2.978}
    for name, (base, spread) in spreads.items():
        noise = np.random.default_rng([zlib.crc32(name.encode()), seed]).standard_normal(out[name].shape)
        drawn = base * np.exp(spread * noise) if base else spread * noise
        out[name] = __import__('jax').numpy.asarray(drawn.astype(out[name].dtype))
    for name, factor in factors.items():
        out[name] = (out[name] * factor).astype(out[name].dtype)
    return out
```

```python
import math
from collections import deque
from contextlib import ExitStack

import numpy as np
import concourse.bass as bass
from concourse import mybir

F32 = mybir.dt.float32
F32R = mybir.dt.float32r
ALU = mybir.AluOpType
ACT = mybir.ActivationFunctionType
AX = mybir.AxisListType

P = 128
D = 1024
S = 256
HD = 64
L = 2
NE = 16
FF = 2816
ALPHA = (2.0 * L) ** 0.25
LN_EPS = 1e-5
RMS_EPS = 1e-6
W_IN1 = 5120
NRAW = 4
NSPL = 3

COLS = {}
ROWS = {}
CONS = {}


def _spans(table, items):
    at = 0
    for name, n in items:
        table[name] = (at, at + n)
        at += n
    return at


N_COLS = _spans(COLS, [("c", 8), ("b_ada", 96), ("mix_g", 16), ("mem_g", 16), ("ffn_g", 16),
                       ("pool_s", 4), ("router", 128), ("pool_w", 256)])
N_ROWS = _spans(ROWS, [("qn", 128), ("kn", 128), ("naq", 128), ("nak", 128), ("mq", 128), ("mk", 128),
                       ("ret", 512), ("rb", 16), ("dec", 16)])
N_CONS = _spans(CONS, [("ident", 128), ("cos1", 64), ("sin1", 64), ("cos2", 64), ("sin2", 64),
                       ("mask", 256)])


def shape_constants():
    f = np.float32
    t = np.arange(S)
    cons = np.zeros((P, N_CONS), f)

    def put(name, a):
        cons[:, CONS[name][0]:CONS[name][1]] = a

    def tiles(a):
        return a.reshape(2, P, -1).transpose(1, 0, 2).reshape(P, -1)

    put("ident", np.eye(P, dtype=f))
    inv = (f(10000.0) ** (-np.arange(0, 32, 2, dtype=f) / f(32))).astype(f)
    row, col = (t // 64).astype(f), (t % 64).astype(f)
    ang = np.concatenate([row[:, None] * inv, col[:, None] * inv], -1).astype(f)
    put("cos1", tiles(np.cos(ang)))
    put("sin1", tiles(np.sin(ang)))
    inv = (f(10000.0) ** (-np.arange(32, dtype=f) / f(32))).astype(f)
    ang = (t.astype(f)[:, None] * inv[None, :]).astype(f)
    put("cos2", tiles(np.cos(ang)))
    put("sin2", tiles(np.sin(ang)))
    qc, kc = np.arange(P) % 64, t % 64
    win = np.clip(qc - 8, 0, 48)
    ok = (kc[None, :] >= win[:, None]) & (kc[None, :] < win[:, None] + 16)
    put("mask", np.where(ok, f(0), f(-1e30)))

    dist = np.abs(t[:, None] - t[None, :])
    alibi = np.zeros((S, 3, S), f)
    for g, dil in enumerate((1, 4, 16)):
        seen = (dist % dil == 0) & (dist <= 64 * dil)
        alibi[:, g] = np.where(seen, dist, 1e30)
    alibi = tiles(alibi.reshape(S, -1))

    pool = np.zeros((S, 4, S), f)
    for g, w in enumerate((2, 4, 8, 16)):
        lo, hi = np.clip(t - w // 2, 0, S), np.clip(t + w // 2, 0, S)
        inside = (t[:, None] >= lo[None, :]) & (t[:, None] < hi[None, :])
        pool[:, g] = inside / (hi - lo)[None, :] - np.eye(S)
    pool = tiles(pool.reshape(S, -1))

    k, q = t[:, None], t[None, :]
    decay = np.stack([tiles(np.maximum(q - k, 0).astype(f)), tiles(np.maximum(k - q, 0).astype(f))], 1)
    return {"cons": cons, "alibi": np.ascontiguousarray(alibi), "pool_m": np.ascontiguousarray(pool.astype(f)),
            "decay_m": np.ascontiguousarray(decay.reshape(P, -1).astype(f))}


class Queues:

    def __init__(self):
        self.q = {n: [] for n in ("pe", "act", "dve", "pool", "sp")}
        self.n = {}
        self.seen = {n: {} for n in self.q}

    def wait(self, eng, deps):
        for d in deps:
            if d is None:
                continue
            if isinstance(d, list):
                self.wait(eng, d)
                continue
            s, v = d
            if self.seen[eng].get(s, 0) < v:
                self.seen[eng][s] = v
                self.q[eng].append(("wait", s, v))

    def op(self, eng, fn, *deps, sig=True):
        self.wait(eng, deps)
        if sig:
            self.n[eng] = self.n.get(eng, 0) + 1
        self.q[eng].append(("op", fn, (eng, 1) if sig else None))
        return (eng, self.n.get(eng, 0))

    def dma(self, eng, sem, out, src, *deps):
        self.wait(eng, deps)
        self.n[sem] = self.n.get(sem, 0) + 16
        self.q[eng].append(("op", lambda e: e.dma_start(out, src), (sem, 16)))
        return (sem, self.n[sem])


def plan(nc, T, dr, units, real):
    Q = Queues()
    op, dma = Q.op, Q.dma

    n_unit = len(units)
    st = {"dma": 0, "spl": 0, "use": 0}
    landed, released, prepared = {}, {}, {}
    spl_free = [None] * NSPL
    spl_ids = [i for i, u in enumerate(units) if u[3]]
    spl_no = {u: k for k, u in enumerate(spl_ids)}
    held = {}

    def pump():
        if not real:
            return
        while True:
            moved = False
            i = st["dma"]
            if i < n_unit and (i < NRAW or (i - NRAW) in released):
                src, a, b, _ = units[i]
                dst = T["raw"][i % NRAW][:, 0:a * b].rearrange("p (a b) -> p a b", a=a)
                landed[i] = dma("sp", f"s_raw{i % NRAW}", dst, src, released.get(i - NRAW))
                st["dma"] += 1
                moved = True
            k = st["spl"]
            if k < len(spl_ids):
                i = spl_ids[k]
                if i in landed and (k < NSPL or held.get(k - NSPL)):
                    _, a, b, _ = units[i]
                    j = k % NSPL
                    raw = T["raw"][i % NRAW][:, 0:a * b]
                    hi, lo = T["whi"][j][:, 0:a * b], T["wlo"][j][:, 0:a * b]
                    t1 = op("act", lambda e, hi=hi, raw=raw: e.activation(hi, raw, ACT.Copy),
                            landed[i], held.get(k - NSPL))
                    t2 = op("dve", lambda e, hi=hi, lo=lo, raw=raw:
                            e.tensor_tensor(lo, raw, hi.bitcast(F32), ALU.subtract), t1)
                    released[i] = [t1, t2]
                    prepared[i] = [t1, t2]
                    st["spl"] += 1
                    moved = True
            if not moved:
                return

    def unit(src, a, b, split=True):
        i = st["use"]
        st["use"] += 1
        if not real:
            units.append((src, a, b, split))
            return (i, None, None, None)
        pump()
        if split:
            j = spl_no[i] % NSPL
            hi = T["whi"][j][:, 0:a * b].rearrange("p (a b) -> p a b", a=a)
            lo = T["wlo"][j][:, 0:a * b].rearrange("p (a b) -> p a b", a=a)
            return (i, hi, lo, prepared[i])
        raw = T["raw"][i % NRAW][:, 0:a * b].rearrange("p (a b) -> p a b", a=a)
        return (i, raw, None, landed[i])

    def done(u, tok):
        i = u[0]
        if real:
            if units[i][3]:
                held[spl_no[i]] = tok
            else:
                released[i] = tok
            pump()

    if not real:
        full = op

        def op(eng, fn, *deps, sig=True):
            return None

        def dma(*a):
            return None

    ring = deque((b, None) for b in range(8))

    def take():
        b, free = ring.popleft()
        return b, T["ps"][b], free

    def put(b, tok):
        ring.append((b, tok))

    def col(name, j=0, n=1):
        a = COLS[name][0] + j
        return T["cols"][:, a:a + n]

    def row(name, j, n):
        a = ROWS[name][0] + j
        return T["rows"][:, a:a + n]

    def con(name):
        a, b = CONS[name]
        return T["cons"][:, a:b]

    ident = con("ident")
    small_at = [0]

    def small(n):
        if small_at[0] + n > T["small"].shape[1]:
            small_at[0] = 0
        a = small_at[0]
        small_at[0] += n
        return T["small"][:, a:a + n]

    H = (T["Hh"], T["Hl"])
    B = (T["Bh"], T["Bl"])
    x, T1, T2, G, AR = T["x"], T["T1"], T["T2"], T["G"], T["AR"]

    def arena(a, n, **k):
        v = AR[:, a:a + n]
        return v

    def mm(out, lhsT, rhs, start, stop, *deps, sig=False):
        return op("pe", lambda e: e.matmul(out, lhsT, rhs, start=start, stop=stop), *deps, sig=sig)

    def mm3(out, lhsT, rhs, start, stop, *deps, sig=False):
        (lh, ll), (rh, rl) = lhsT, rhs
        mm(out, lh, rh, start, False, *deps)
        mm(out, lh, rl, False, False)
        return mm(out, ll, rh, False, stop, sig=sig)

    def tr(out, src, *deps, sig=False):
        return op("pe", lambda e: e.transpose(out, src, ident), *deps, sig=sig)

    def act(out, src, func, *deps, **k):
        return op("act", lambda e: e.activation(out, src, func, **k), *deps)

    def tt(out, a, b, o, *deps, eng="dve"):
        return op(eng, lambda e: e.tensor_tensor(out, a, b, o), *deps)

    def ts(out, a, s1, s2, o0, o1, *deps, eng="dve"):
        if o1 is None:
            return op(eng, lambda e: e.tensor_scalar(out, a, s1, None, o0), *deps)
        return op(eng, lambda e: e.tensor_scalar(out, a, s1, s2, o0, o1), *deps)

    def stt(out, a, s, b, o0, o1, *deps):
        return op("dve", lambda e: e.scalar_tensor_tensor(out=out, in0=a, scalar=s, in1=b, op0=o0, op1=o1), *deps)

    def red(out, a, o, *deps):
        return op("dve", lambda e: e.tensor_reduce(out, a, AX.X, o), *deps)

    def copy(out, a, *deps, eng="act"):
        if eng == "act":
            return act(out, a, ACT.Copy, *deps)
        return op(eng, lambda e: e.tensor_copy(out, a), *deps)

    def split(hi, lo, src, *deps):
        t1 = act(hi, src, ACT.Copy, *deps)
        t2 = tt(lo, src, hi.bitcast(F32), ALU.subtract, t1, *deps)
        return [t1, t2]

    def rsqrt(ap, n, scale, eps, *deps):
        t = ts(ap, ap, scale, eps, ALU.mult, ALU.add, *deps)
        return op("pool", lambda e: e.tensor_tensor(ap, ap, T["mhalf"][:, 0:n], ALU.pow), t, tok["mhalf"])

    def proj_T(u, rhs, n_k, blk0, out, *deps, k0=0):
        last = None
        for j in range(2):
            for k in range(n_k):
                c = (blk0 + j) * P
                last = mm3(out[:, j * S:(j + 1) * S],
                           (u[1][:, k, c:c + P], u[2][:, k, c:c + P]) if real else (0, 0),
                           (rhs[0][:, k0 + k, :], rhs[1][:, k0 + k, :]), k == 0, k == n_k - 1,
                           u[3], *deps, sig=(j == 1 and k == n_k - 1))
        return last

    def proj_tok256(u, lhs, out, *deps):
        last = None
        for t in range(2):
            for k in range(8):
                last = mm3(out[:, t * S:(t + 1) * S],
                           (lhs[0][:, k, t * P:(t + 1) * P], lhs[1][:, k, t * P:(t + 1) * P]),
                           (u[1][:, k, :], u[2][:, k, :]) if real else (0, 0), k == 0, k == 7,
                           u[3], *deps, sig=(t == 1 and k == 7))
        return last

    def w_unit8(w, c0, n=256):
        return w[:, c0:c0 + n].rearrange("(k p) c -> p k c", p=P)

    def tok_proj(w, c0, lhs, *deps):
        u = unit(w_unit8(w, c0), 8, S)
        b, ps, free = take()
        t = proj_tok256(u, lhs, ps, free, *deps)
        done(u, t)
        return b, ps, t

    def T_proj(w, c0, rhs, *deps):
        u = unit(w_unit8(w, c0), 8, S)
        b, ps, free = take()
        t = proj_T(u, rhs, 8, 0, ps, free, *deps)
        done(u, t)
        return b, ps, t

    def tok_proj512(w, rhs_cols, n_kt, lhs, *deps):
        bs = [take() for _ in range(2)]
        last = None
        n_u = n_kt // 4
        for a in range(n_u):
            u = unit(w[a * 512:(a + 1) * 512, rhs_cols:rhs_cols + 512].rearrange("(k p) c -> p k c", p=P), 4, 512)
            toks = []
            for t in range(2):
                for k in range(4):
                    kk = 4 * a + k
                    last = mm3(bs[t][1][:, :],
                               (lhs[0][:, kk, t * P:(t + 1) * P], lhs[1][:, kk, t * P:(t + 1) * P]),
                               (u[1][:, k, :], u[2][:, k, :]) if real else (0, 0),
                               kk == 0, kk == n_kt - 1, u[3], bs[t][2], *deps, sig=(k == 3))
                toks.append(last)
            done(u, last)
        return bs, toks

    tok = {}
    tok["mhalf"] = op("pool", lambda e: e.memset(T["mhalf"][:, :], -0.5))
    tok["cons"] = dma("act", "s_cons", T["cons"][:, :], dr["cons"])
    tok["cols"] = dma("act", "s_cols", T["cols"][:, :], dr["cols"])
    tok["x"] = dma("act", "s_x", x[:, :, :], dr["x"].rearrange("(t p) d -> p t d", p=P))
    tok["rows"] = dma("act", "s_rows", T["rows"][:, :], dr["rows"].partition_broadcast(P))

    csil = T["csil"]
    t_c = act(csil[:, :], col("c", 0, 8), ACT.Silu, tok["cols"])
    modT = T["modT"]
    mod_tok = {}

    def mod_part(l, part):
        b, ps, free = take()
        last = None
        for a in range(4):
            u = unit(w_unit8(dr["w_ada"][l], part * D + a * S), 8, S, split=False)
            for j in range(2):
                for k in range(8):
                    last = mm(ps[:, 2 * a + j:2 * a + j + 1], u[1][:, k, j * P:(j + 1) * P] if real else 0,
                              csil[:, k:k + 1], k == 0, k == 7, u[3], t_c, free, sig=(j == 1 and k == 7))
            done(u, last)
        m = modT[:, 48 * l + 8 * part:48 * l + 8 * part + 8]
        t = tt(m, ps[:, 0:8], col("b_ada", 48 * l + 8 * part, 8), ALU.add, last, tok["cols"])
        put(b, t)
        if part in (1, 4):
            t = ts(m, m, 1.0, None, ALU.add, None, t)
        mod_tok[(l, part)] = t

    def mod_cols(l, part):
        return modT[:, 48 * l + 8 * part:48 * l + 8 * part + 8]

    def mod_bcast(l, part, out, *deps):
        b, ps, free = take()
        m = mod_cols(l, part)
        t = op("pe", lambda e, o=ps[0:8, 0:P]: e.transpose(o, m, ident), mod_tok[(l, part)], free, tok["cons"])
        t = copy(T["crow"][0:8, 0:P], ps[0:8, 0:P], t)
        put(b, t)
        toks = []
        for h in range(2):
            b, ps, free = take()
            last = None
            for j in range(4):
                kk = 4 * h + j
                last = mm(ps[:, j * P:(j + 1) * P], ident[0:8, kk:kk + 1].broadcast_to([8, P]),
                          T["crow"][0:8, 0:P], True, True, t, free, sig=(j == 3))
            e = copy(out[:, h * 512:(h + 1) * 512], ps[:, :], last, *deps)
            put(b, e)
            toks.append(e)
        return toks

    def ln(src, dst, *deps):
        sb = small(12)
        for h in range(2):
            t = op("dve", lambda e, h=h: e.bn_stats(sb[:, 6 * h:6 * h + 6], src[:, 512 * h:512 * h + 512]), *deps)
        mv = small(2)
        t = op("dve", lambda e: e.bn_aggr(mv, sb), t)
        t = rsqrt(mv[:, 1:2], 1, 1.0, LN_EPS, t)
        return ts(dst, src, mv[:, 0:1], mv[:, 1:2], ALU.subtract, ALU.mult, t)

    def rms(src, dst, junk, *deps):
        ss = small(1)
        t = act(junk, src, ACT.Square, *deps, accum_out=ss)
        t = rsqrt(ss, 1, 1.0 / D, RMS_EPS, t)
        return ts(dst, src, ss, None, ALU.mult, None, t)

    def to_H(src, scale, bias, src_toks, *deps):
        toks = []
        for kp in range(4):
            b, ps, free = take()
            last = None
            for j in range(2):
                for t in range(2):
                    k = 2 * kp + j
                    last = tr(ps[:, j * S + t * P:j * S + (t + 1) * P], src[:, t, k * P:(k + 1) * P],
                              src_toks[t], free, tok["cons"], sig=(j == 1 and t == 1))
            es = []
            for j in range(2):
                k = 2 * kp + j
                o, i = T2[:, k * S:(k + 1) * S], ps[:, j * S:(j + 1) * S]
                if bias is None and kp % 2:
                    e = act(o, i, ACT.Copy, last, *deps, scale=scale[:, k:k + 1])
                elif bias is None:
                    e = ts(o, i, scale[:, k:k + 1], None, ALU.mult, None, last, *deps)
                elif kp % 2:
                    e = act(o, i, ACT.Identity, last, *deps, scale=scale[:, k:k + 1], bias=bias[:, k:k + 1])
                else:
                    e = ts(o, i, scale[:, k:k + 1], bias[:, k:k + 1], ALU.mult, ALU.add, last, *deps)
                es.append(e)
            put(b, es)
            v = T2[:, 2 * kp * S:(2 * kp + 2) * S].rearrange("p (k s) -> p k s", k=2)
            toks += es + split(H[0][:, 2 * kp:2 * kp + 2, :], H[1][:, 2 * kp:2 * kp + 2, :], v, es)
        return toks

    def head_rms(src, dst, g, tmp, n, *deps):
        t0 = act(tmp, src, ACT.Square, *deps)
        ss = small(n)
        t = red(ss, tmp, ALU.add, t0)
        t = rsqrt(ss, n, 1.0 / HD, RMS_EPS, t)
        t_src = tt(dst, src, ss.unsqueeze(2).broadcast_to([P, n, HD]), ALU.mult, t, *deps)
        t = tt(dst, dst, g, ALU.mult, t_src, tok["rows"], eng="pool")
        return t, t_src

    def rotate(x0, x1, o0, o1, c, s, t4, *deps):
        a = tt(t4[0], x0, c, ALU.mult, *deps, tok["cons"], eng="pool")
        b = tt(t4[1], x1, s, ALU.mult, *deps, eng="pool")
        cc = tt(t4[2], x0, s, ALU.mult, *deps, eng="pool")
        d = tt(t4[3], x1, c, ALU.mult, *deps, eng="pool")
        e = tt(o0, t4[0], t4[1], ALU.subtract, b, d, eng="pool")
        f = tt(o1, t4[2], t4[3], ALU.add, d, eng="pool")
        return f

    def head_softmax(Sb, n, qscale, toks_in, src=None, *deps):
        frm = Sb if src is None else src
        mx = small(2)
        t = red(mx, frm, ALU.max, toks_in, *deps)
        t = ts(mx, mx, -qscale, None, ALU.mult, None, t)
        sm = small(2)
        es = [act(Sb[:, i, :], frm[:, i, :], ACT.Exp, t, bias=mx[:, i:i + 1], scale=qscale,
                  accum_out=sm[:, i:i + 1]) for i in range(2)]
        t = op("dve", lambda e: e.reciprocal(sm, sm), es)
        rs = [ts(Sb[:, i, :], Sb[:, i, :], sm[:, i:i + 1], None, ALU.mult, None, t) for i in range(2)]
        return es, rs

    def probs_T(Sb, n_g, PT, toks, free_pt):
        outs = []
        for g in range(n_g):
            b, ps, free = take()
            last = None
            for kt in range(2):
                for qt in range(2):
                    last = tr(ps[:, kt * S + qt * P:kt * S + (qt + 1) * P],
                              Sb[:, qt, g * S + kt * P:g * S + (kt + 1) * P], toks[qt], free,
                              sig=(kt == 1 and qt == 1))
            e = copy(PT[:, g * 512:(g + 1) * 512], ps[:, :], last, free_pt, eng="act" if g % 2 == 0 else "dve")
            put(b, e)
            outs.append(e)
        return outs, last

    pair = {}

    def pv(h, n_g, PT, v, toks, dst_blk, v_tok):
        half = h % 2
        if half == 0:
            pair["b"] = take()
        b, ps, free = pair["b"]
        last = None
        n = 2 * n_g
        for g in range(n_g):
            for kt in range(2):
                i = 2 * g + kt
                last = mm(ps[64 * half:64 * half + 64, 0:S], v(g, kt), PT[:, i * S:(i + 1) * S],
                          i == 0, i == n - 1, toks, free, v_tok, sig=(i == n - 1))
        res = last
        if half == 1:
            t1 = act(B[0][:, dst_blk, :], ps[:, 0:S], ACT.Copy, last, free_B[0])
            t2 = tt(B[1][:, dst_blk, :], ps[:, 0:S], B[0][:, dst_blk, :].bitcast(F32), ALU.subtract, t1, free_B[0])
            put(b, [t1, t2])
            B_tok[dst_blk] = [t1, t2]
        return res

    free_B = [None]
    B_tok = {}

    def pipeline(heads, filler, per=1):
        n = len(heads)
        for i in range(n + 2):
            if i < n:
                heads[i][0]()
            for _ in range(per):
                next(filler, None)
            if 0 <= i - 2 < n:
                heads[i - 2][2]()
            if 0 <= i - 1 < n:
                heads[i - 1][1]()
        for _ in filler:
            pass

    def ffn(n, ug, uu, ud, comb, h_toks, *deps):
        acc = [take() for _ in range(4)]
        act_done = {}
        pe_done = {}
        y = []

        def down(i):
            u = unit(*ud(i))
            last = None
            for t in range(2):
                for c in range(2):
                    for f in range(2):
                        a = (i % 4) * 2 + f
                        last = mm3(acc[2 * t + c][1][:, :],
                                   (B[0][:, a, t * P:(t + 1) * P], B[1][:, a, t * P:(t + 1) * P]),
                                   (u[1][:, f, c * 512:(c + 1) * 512], u[2][:, f, c * 512:(c + 1) * 512])
                                   if real else (0, 0),
                                   i == 0 and f == 0, i == n - 1 and f == 1, u[3], act_done[i],
                                   acc[2 * t + c][2], sig=(f == 1))
                    if i == n - 1:
                        y.append(last)
            done(u, last)
            pe_done[i] = last

        for i in range(n + 1):
            if i < n:
                ug_ = unit(*ug(i))
                bg, pg, fg = take()
                tg = proj_T(ug_, H, 8, 0, pg, fg, h_toks)
                done(ug_, tg)
                uu_ = unit(*uu(i))
                bu, pu, fu = take()
                tu = proj_T(uu_, H, 8, 0, pu, fu)
                done(uu_, tu)
                s = T1[:, (i % 2) * 512:(i % 2) * 512 + 512]
                e = act(s, pg[:, :], ACT.Silu, tg, act_done.get(i - 2), *deps)
                put(bg, e)
                e = tt(s, s, pu[:, :], ALU.mult, e, tu)
                put(bu, e)
                if comb is not None:
                    s3 = s.rearrange("p (f t) -> p f t", f=2)
                    cb, ct = comb(i)
                    e = tt(s3, s3, cb.unsqueeze(1).broadcast_to([P, 2, S]), ALU.mult, e, ct, eng="pool")
                a = (i % 4) * 2
                hi, lo = B[0][:, a:a + 2, :], B[1][:, a:a + 2, :]
                s3 = s.rearrange("p (f t) -> p f t", f=2)
                act_done[i] = split(hi, lo, s3, e, pe_done.get(i - 4), free_B[0])
            if i >= 1:
                down(i - 1)
        free_B[0] = pe_done[n - 1]
        return acc, y, tu

    def first_layer(l, x_toks):
        w = dr["w_in"][l]
        xn = T1[:, :].rearrange("p (t d) -> p t d", t=2)
        t_n = [ln(x[:, t, :], xn[:, t, :], x_toks[t], free_T1[0]) for t in range(2)]
        h_toks = to_H(xn, mod_cols(l, 1), mod_cols(l, 0), t_n, mod_tok[(l, 0)], mod_tok[(l, 1)],
                      free_H[0], free_T2[0])

        qd, kd = arena(0, 1536), arena(1536, 1536)
        qd3 = qd.rearrange("p (b s) -> p b s", s=S)
        kd3 = kd.rearrange("p (b s) -> p b s", s=S)
        vd = arena(3072, 1536).rearrange("p (t c) -> p t c", t=2)
        PT = arena(4608, 1536)
        qaT = arena(6144, 1024).rearrange("p (j s) -> p j s", j=4)
        kaT = arena(7168, 256)
        va = arena(7424, 256).rearrange("p (t c) -> p t c", t=2)
        ka = arena(7680, 256).rearrange("p (t c) -> p t c", t=2)
        qa = arena(4608, 1024).rearrange("p (t c) -> p t c", t=2)
        fa = free_AR[0]

        bs, ts_ = tok_proj512(w, 0, 8, H, h_toks)
        qa_t = []
        for t in range(2):
            tmp = T1[:, 512 * t:512 * t + 512].rearrange("p (h d) -> p h d", d=HD)
            dst = qa[:, t, :].rearrange("p (h d) -> p h d", d=HD)
            gq = row("qn", 64 * l, 64).unsqueeze(1).broadcast_to([P, 8, HD])
            tc_ = copy(qa[:, t, :].rearrange("p (j a d) -> p j a d", a=2, j=4),
                       bs[t][1][:, :].rearrange("p (a j d) -> p j a d", a=2, j=4), ts_[t], fa)
            put(bs[t][0], tc_)
            tq, _ = head_rms(dst, dst, gq, tmp, 8, tc_, h_toks)
            c = con("cos1")[:, 32 * t:32 * t + 32].unsqueeze(1).broadcast_to([P, 8, 32])
            s = con("sin1")[:, 32 * t:32 * t + 32].unsqueeze(1).broadcast_to([P, 8, 32])
            v = dst.rearrange("p h (i two) -> p h i two", two=2)
            t4 = [T1[:, 1024 + 256 * i:1280 + 256 * i].rearrange("p (h i) -> p h i", h=8) for i in range(4)]
            qa_t.append(rotate(v[:, :, :, 0], v[:, :, :, 1], v[:, :, :, 0], v[:, :, :, 1], c, s, t4, tq,
                               qa_t[-1] if qa_t else None))
        b, ps, t_p = tok_proj(w, 512, H, h_toks)
        p3 = ps[:, :].rearrange("p (t c) -> p t c", t=2)
        t1 = copy(ka, p3[:, :, 0:128], t_p, fa)
        t_va = copy(va, p3[:, :, 128:256], t_p, fa)
        put(b, [t1, t_va])
        kav = ka.rearrange("p t (h d) -> p (t h) d", d=HD)
        gk = row("kn", 64 * l, 64).unsqueeze(1).broadcast_to([P, 4, HD])
        tk, _ = head_rms(kav, kav, gk, T2[:, 0:256].rearrange("p (h d) -> p h d", d=HD), 4, t1, h_toks)
        for t in range(2):
            c = con("cos1")[:, 32 * t:32 * t + 32].unsqueeze(1).broadcast_to([P, 2, 32])
            s = con("sin1")[:, 32 * t:32 * t + 32].unsqueeze(1).broadcast_to([P, 2, 32])
            v = ka[:, t, :].rearrange("p (h i two) -> p h i two", h=2, two=2)
            t4 = [T2[:, 512 + 256 * t + 64 * i:576 + 256 * t + 64 * i].rearrange("p (h i) -> p h i", h=2)
                  for i in range(4)]
            tk = rotate(v[:, :, :, 0], v[:, :, :, 1], v[:, :, :, 0], v[:, :, :, 1], c, s, t4, tk)
        t_vd, t_qd, t_kd = [], [], []
        for i in range(3):
            b, ps, t_p = tok_proj(w, 2304 + S * i, H)
            e = copy(vd[:, :, S * i:S * i + S], ps[:, :].rearrange("p (t c) -> p t c", t=2), t_p, fa,
                     eng="dve" if i % 2 else "act")
            put(b, e)
            t_vd.append(e)
        for dst, c0, lst in ((qd, 768, t_qd), (kd, 1536, t_kd)):
            for i in range(3):
                b, ps, t_p = T_proj(w, c0 + S * i, H)
                e = copy(dst[:, 512 * i:512 * i + 512], ps[:, :], t_p, fa, eng="dve" if i % 2 else "act")
                put(b, e)
                lst.append(e)
        t_qa = []
        for jp in range(2):
            b, ps, free = take()
            last = None
            for j in range(2):
                for t in range(2):
                    jj = 2 * jp + j
                    v = qa[:, t, jj * P:(jj + 1) * P]
                    last = tr(ps[:, j * S + t * P:j * S + t * P + P], v, qa_t[t], free, sig=(j == 1 and t == 1))
            e = copy(qaT[:, 2 * jp:2 * jp + 2, :], ps[:, :].rearrange("p (j s) -> p j s", j=2), last, fa)
            put(b, e)
            t_qa.append(e)
        b, ps, free = take()
        for t in range(2):
            last = tr(ps[:, t * P:t * P + P], ka[:, t, :], tk, free, sig=(t == 1))
        t_ka = copy(kaT, ps[:, 0:S], last, fa)
        put(b, t_ka)

        G3 = G[:, :].rearrange("p (b s) -> p b s", s=S)
        g_tok = []

        def gates():
            for i in range(8):
                b, ps, t_p = T_proj(w, 3072 + S * i, H)
                e = copy(G3[:, 2 * i:2 * i + 2, :], ps[:, :].rearrange("p (b s) -> p b s", b=2), t_p, free_G[0],
                         eng="dve" if i % 2 else "act")
                put(b, e)
                g_tok.append(e)
                free_H[0] = t_p
                yield

        if l == 0:
            tok["alibi"] = dma("pool", "s_tab", T["TB"][:, 0:1536], dr["alibi"])
        t_al = tok["alibi"]
        al = T["TB"][:, 0:1536].rearrange("p (t g s) -> p t g s", t=2, g=3)
        bufs = [T1[:, 0:1536], T2[:, 0:1536]]
        state = {}
        pt_free = [[fa, t_qa]]
        al_used = []

        def dilated(j, i):
            Sb = bufs[i % 2].rearrange("p (t n) -> p t n", t=2)

            def s1():
                toks = []
                for g in range(3):
                    n = 4 * g + j
                    b, ps, free = take()
                    last = None
                    o = 64 * (n % 2)
                    for qt in range(2):
                        last = mm(ps[:, qt * S:(qt + 1) * S], qd3[o:o + 64, n // 2, qt * P:(qt + 1) * P],
                                  kd3[o:o + 64, n // 2, :], True, True, free, t_qd, t_kd, sig=(qt == 1))
                    slope = float(np.float32(2.0) ** np.float32(-8.0 * (n + 1) / 12))
                    a3 = al[:, :, g, :]
                    e = stt(Sb[:, :, g * S:(g + 1) * S], a3, -8.0 * slope,
                            ps[:, :].rearrange("p (t s) -> p t s", t=2), ALU.mult, ALU.add, last, t_al,
                            state.get(i - 2), qa_t, tk, h_toks)
                    put(b, e)
                    toks.append(e)
                al_used.append(toks[-1])
                state[("p", i)] = head_softmax(Sb, 768, 0.125, toks)[1]

            def s2():
                state[("t", i)], state[i] = probs_T(Sb, 3, PT, state[("p", i)], pt_free[0])

            def s3():
                r = pv(j, 3, PT, lambda g, kt: vd[:, kt, (4 * g + j) * HD:(4 * g + j + 1) * HD],
                       state[("t", i)], 4 + j // 2, t_vd)
                pt_free[0] = r

            return s1, s2, s3

        pipeline([dilated(j, j) for j in range(4)], gates(), per=2)
        free_TB[0] = al_used

        def globl(h, i):
            Sb = bufs[i % 2][:, 512 * (i // 2 % 3):512 * (i // 2 % 3) + 512].rearrange("p (t n) -> p t n", t=2)
            pt = PT[:, 512 * (i % 3):512 * (i % 3) + 512]

            def s1():
                b, ps, free = take()
                last = None
                o = 64 * (h // 4)
                for qt in range(2):
                    last = mm(ps[:, qt * S:(qt + 1) * S], qaT[o:o + 64, h % 4, qt * P:(qt + 1) * P],
                              kaT[o:o + 64, :], True, True, free, t_qa, t_ka, sig=(qt == 1))
                es, state[("p", i)] = head_softmax(Sb, S, 0.125, last, ps[:, :].rearrange("p (t s) -> p t s", t=2),
                                                   state.get(i - 2), state.get(i - 6))
                put(b, es)

            def s2():
                state[("t", i)], state[i] = probs_T(Sb, 1, pt, state[("p", i)], pt_free[0])

            def s3():
                pt_free[0] = pv(h, 1, pt, lambda g, kt: va[:, kt, 64 * (h // 4):64 * (h // 4) + 64],
                                state[("t", i)], h // 2, t_va)

            return s1, s2, s3

        def mods():
            for part in (2, 4, 3, 5):
                if l == 0:
                    mod_part(0, part)
                yield
            if l == 0:
                mod_part(1, 1)
                yield
                mod_part(1, 0)
                yield
                yield
            else:
                yield

        mg = mods() if l == 0 else later_mods()
        pipeline([globl(h, 4 + h) for h in range(8)], mg)
        free_AR[0] = pt_free[0]

        sg = []
        for i in range(4):
            v = G[:, 1024 * (3 - i):1024 * (4 - i)]
            sg.append(act(v, v, ACT.Sigmoid, g_tok))
        u = unit(dr["w_pb"][l].rearrange("(k p) c -> p k c", p=P), 2, D)
        last = None
        tb = []
        for m in range(4):
            b, ps, free = take()
            last = proj_T(u, B, 2, 2 * m, ps, free, B_tok[4], B_tok[5], k0=4)
            v = G[:, 2048 + 512 * m:2048 + 512 * m + 512]
            e = tt(v, v, ps[:, :], ALU.mult, last, sg)
            put(b, e)
            tb.append(e)
        done(u, last)
        m_toks = []
        for uu in range(2):
            u = unit(dr["w_pa"][l][:, uu * 512:uu * 512 + 512].rearrange("(k p) c -> p k c", p=P), 4, 512)
            for mm_ in range(2):
                m = 2 * uu + mm_
                b, ps, free = take()
                last = proj_T(u, B, 4, 2 * mm_, ps, free, [B_tok[i] for i in range(4)])
                v = G[:, 512 * m:512 * m + 512]
                vb = G[:, 2048 + 512 * m:2048 + 512 * m + 512]
                e = tt(v, v, ps[:, :], ALU.mult, last, sg)
                put(b, e)
                e = tt(v, v, vb, ALU.add, e, tb[m], eng="pool")
                v3 = v.rearrange("p (k s) -> p k s", k=2)
                m_toks += split(H[0][:, 2 * m:2 * m + 2, :], H[1][:, 2 * m:2 * m + 2, :], v3, e, free_H[0])
            done(u, last)
        free_B[0] = last
        B_tok.clear()
        gb = mod_bcast(l, 2, G[:, 0:1024], m_toks)
        lg = dma("pool", "s_lng", G[:, 1024:2048], dr["ln1_g"][l].partition_broadcast(P), m_toks)
        lb = dma("pool", "s_lnb", G[:, 2048:3072], dr["ln1_b"][l].partition_broadcast(P), m_toks)
        ys = [[None, None], [None, None]]
        for c in range(2):
            bs, ts_ = tok_proj512(dr["w_out"][l], 512 * c, 8, H, m_toks)
            for t in range(2):
                ys[t][c] = (bs[t][0], bs[t][1], ts_[t])
            free_H[0] = ts_[1]
        x_toks = residual_ln(ys, G[:, 0:1024], G[:, 1024:2048], G[:, 2048:3072], gb, lg, lb,
                             lambda t: T1[:, 1024 * t:1024 * t + 1024], [state[11], state[10], state[9], state[8]])
        free_G[0] = x_toks

        t_n = [ln(x[:, t, :], xn[:, t, :], x_toks[t], x_toks) for t in range(2)]
        h_toks = to_H(xn, mod_cols(l, 4), mod_cols(l, 3), t_n, mod_tok[(l, 3)], mod_tok[(l, 4)], free_H[0],
                      [state[11], state[10]])
        t_comb = router(h_toks)
        g2 = mod_bcast(l, 5, T1[:, 1024:2048], h_toks)
        lg = dma("pool", "s_lng", T2[:, 0:1024], dr["ln2_g"][l].partition_broadcast(P), h_toks, t_comb)
        lb = dma("pool", "s_lnb", T2[:, 1024:2048], dr["ln2_b"][l].partition_broadcast(P), h_toks, t_comb)
        CB = G[:, :].rearrange("p (e s) -> p e s", s=S)
        acc, y, tu = ffn(NE,
                         lambda i: (w_unit8(dr["w_g"][l, i], 0), 8, S),
                         lambda i: (w_unit8(dr["w_u"][l, i], 0), 8, S),
                         lambda i: (dr["w_d"][l, i].rearrange("(k p) c -> p k c", p=P), 2, D),
                         lambda i: (CB[:, i, :], t_comb), h_toks, h_toks)
        free_H[0] = tu
        ys = [[(acc[2 * t + c][0], acc[2 * t + c][1], y[2 * t + c]) for c in range(2)] for t in range(2)]
        x_toks = residual_ln(ys, T1[:, 1024:2048], T2[:, 0:1024], T2[:, 1024:2048], g2, lg, lb,
                             lambda t: G[:, 1024 * t:1024 * t + 1024], [y])
        free_G[0] = x_toks
        free_T1[0] = x_toks
        free_T2[0] = x_toks
        return x_toks

    def later_mods():
        for part in (2, 4, 3, 5):
            mod_part(1, part)
            yield

    free_TB = [None]
    free_T1, free_T2, free_G, free_H, free_AR = [None], [None], [None], [None], [None]

    def residual_ln(ys, gate, lng, lnb, g_tok, lg_tok, lb_tok, tmp, deps):
        out = []
        for t in range(2):
            v = tmp(t)
            es = []
            for c in range(2):
                b, ps, ty = ys[t][c]
                e = tt(v[:, 512 * c:512 * c + 512], ps[:, :], gate[:, 512 * c:512 * c + 512], ALU.mult, ty,
                       g_tok, deps)
                put(b, e)
                es.append(e)
            e = stt(x[:, t, :], x[:, t, :], ALPHA, v, ALU.mult, ALU.add, es)
            e = ln(x[:, t, :], v, e)
            e = tt(v, v, lng, ALU.mult, e, lg_tok)
            e = tt(x[:, t, :], v, lnb, ALU.add, e, lb_tok, eng="pool" if t == 0 else "dve")
            out.append(e)
        return out

    def router(h_toks):
        Hf = T2[:, :].rearrange("p (k s) -> p k s", k=8)
        b, ps, free = take()
        last = None
        for t in range(2):
            for k in range(8):
                last = mm(ps[:, 16 * t:16 * t + 16], Hf[:, k, t * P:(t + 1) * P],
                          col("router", 16 * k, 16), k == 0, k == 7, h_toks, free, sig=(t == 1 and k == 7))
        R = T["R"]

        def r(a, n):
            return R[:, a:a + n]

        sc, sel = r(0, 32), r(32, 32)
        e = act(sc, ps[:, 0:32], ACT.Sigmoid, last)
        put(b, e)
        rb = row("rb", 0, 16).unsqueeze(1).broadcast_to([P, 2, 16])
        e_sc = e
        e = tt(sel.rearrange("p (t e) -> p t e", t=2), sc.rearrange("p (t e) -> p t e", t=2), rb, ALU.add, e,
               tok["rows"])
        s4 = sel.rearrange("p (g e) -> p g e", e=4)
        rank, cmp_ = r(64, 32), r(96, 32)
        rk4, c4 = rank.rearrange("p (g e) -> p g e", e=4), cmp_.rearrange("p (g e) -> p g e", e=4)
        e = op("dve", lambda e_: e_.memset(rank, 0.0), e)
        pr = r(128, 8 * 6)
        n = 0
        ps_t = []
        for a in range(4):
            for b_ in range(a + 1, 4):
                sa, sb = s4[:, :, a:a + 1], s4[:, :, b_:b_ + 1]
                ps_t.append(tt(pr[:, 8 * n:8 * n + 8].unsqueeze(2), sa, sb, ALU.add, e))
                e = tt(c4[:, :, 0:1], sb, sa, ALU.is_gt, e)
                e = tt(rk4[:, :, a:a + 1], rk4[:, :, a:a + 1], c4[:, :, 0:1], ALU.add, e)
                e = tt(c4[:, :, 1:2], sa, sb, ALU.is_ge, e)
                e = tt(rk4[:, :, b_:b_ + 1], rk4[:, :, b_:b_ + 1], c4[:, :, 1:2], ALU.add, e)
                n += 1
        gs = r(176, 8)
        e = red(gs, pr.rearrange("p (n g) -> p g n", n=6), ALU.max, ps_t, e)
        g4 = gs.rearrange("p (t g) -> p t g", g=4)
        gr = r(184, 8)
        gr4 = gr.rearrange("p (t g) -> p t g", g=4)
        e = op("dve", lambda e_: e_.memset(gr, 0.0), e)
        c2 = cmp_.rearrange("p (t g) -> p t g", t=2)
        for a in range(4):
            for b_ in range(a + 1, 4):
                e = tt(c2[:, :, 0:1], g4[:, :, b_:b_ + 1], g4[:, :, a:a + 1], ALU.is_gt, e)
                e = tt(gr4[:, :, a:a + 1], gr4[:, :, a:a + 1], c2[:, :, 0:1], ALU.add, e)
                e = tt(c2[:, :, 1:2], g4[:, :, a:a + 1], g4[:, :, b_:b_ + 1], ALU.is_ge, e)
                e = tt(gr4[:, :, b_:b_ + 1], gr4[:, :, b_:b_ + 1], c2[:, :, 1:2], ALU.add, e)
        e = ts(gr, gr, 0.5, None, ALU.is_lt, None, e)
        e = ts(rank, rank, 1.5, None, ALU.is_lt, None, e)
        e = tt(rk4, rk4, gr.unsqueeze(2).broadcast_to([P, 8, 4]), ALU.mult, e)
        e = tt(rank, rank, sc, ALU.mult, e)
        tot = r(192, 2)
        e = red(tot, rank.rearrange("p (t e) -> p t e", t=2), ALU.add, e)
        e = op("dve", lambda e_: e_.reciprocal(tot, tot), e)
        e = tt(rank.rearrange("p (t e) -> p t e", t=2), rank.rearrange("p (t e) -> p t e", t=2),
               tot.unsqueeze(2).broadcast_to([P, 2, 16]), ALU.mult, e)
        b, ps, free = take()
        for t in range(2):
            last = op("pe", lambda e_, t=t, ps=ps: e_.transpose(ps[0:16, t * P:(t + 1) * P], rank[:, 16 * t:16 * t + 16], ident),
                      e, free)
        e = copy(T["crow"][0:16, :], ps[0:16, 0:S], last)
        put(b, e)
        outs = []
        for m in range(8):
            b, ps, free = take()
            for j in range(2):
                k = 2 * m + j
                last = mm(ps[:, j * S:(j + 1) * S], ident[0:16, k:k + 1].broadcast_to([16, P]),
                          T["crow"][0:16, :], True, True, e, free, sig=(j == 1))
            c = copy(G[:, 512 * m:512 * m + 512], ps[:, :], last, free_G[0], eng="act" if m % 2 else "dve")
            put(b, c)
            outs.append(c)
        return outs

    gam = T["gam"]

    def decays():
        z, a, u, w, d, r_, m = (T["R"][:, 16 * i:16 * i + 16] for i in range(7))
        src = row("dec", 0, 16)
        e = ts(z, src, -1.0, None, ALU.mult, None, tok["rows"])
        e = tt(a, z, src, ALU.min, e)
        e = act(u, a, ACT.Exp, e)
        e1 = ts(w, u, 1.0, None, ALU.add, None, e)
        e2 = act(m, w, ACT.Ln, e1)
        e = ts(d, w, -1.0, None, ALU.add, None, e1)
        e = ts(r_, d, 1e-30, None, ALU.max, None, e)
        e = op("dve", lambda e_: e_.reciprocal(r_, r_), e)
        e = tt(r_, r_, u, ALU.mult, e)
        e = tt(r_, r_, m, ALU.mult, e, e2)
        e = stt(m, d, 0.0, u, ALU.is_equal, ALU.mult, e)
        e = tt(r_, r_, m, ALU.add, e)
        e = ts(a, src, 0.0, None, ALU.min, None, e)
        return tt(gam[:, :], a, r_, ALU.subtract, e)

    def to_T(src, dst, toks, *deps):
        b, ps, free = take()
        last = None
        for blk in range(2):
            for t in range(2):
                last = tr(ps[:, blk * S + t * P:blk * S + t * P + P], src[:, t, blk * P:(blk + 1) * P], toks, free,
                          sig=(blk == 1 and t == 1))
        if dst is None:
            return b, ps, last
        e = copy(dst, ps[:, :], last, *deps)
        put(b, e)
        return e

    def second_layer(l, x_toks, t_gam):
        w = dr["w_in2"][l]
        xn = T1[:, :].rearrange("p (t d) -> p t d", t=2)

        def t2(a):
            return arena(a * 512, 512)

        fa = free_AR[0]
        tiles = {}
        names = ["rq", "rk", "rv", "rg", "rqT", "rkT", "pv", "nq", "nk", "nv", "nqT", "nkT", "mq", "mqT",
                 "mk", "mkT", "mv"]
        for i, n in enumerate(names):
            tiles[n] = t2(i)

        def v3(n):
            return tiles[n].rearrange("p (t c) -> p t c", t=2)

        def vh(ap):
            return ap.rearrange("p (h d) -> p h d", d=HD)

        t_nab = dma("pool", "s_tab", T["TB"][:, :], dr["na_b"][:, l].rearrange("p t h s -> p (t h s)"), free_TB[0])
        um = unit(dr["mem"].rearrange("(t p) d -> p t d", p=P), 2, D, split=False)
        t_n = []
        for t in range(2):
            m = um[1][:, t, :] if real else T1[:, 0:D]
            t_n.append(rms(m, xn[:, t, :], T2[:, 1024 * t:1024 * t + 1024], um[3], free_T1[0], free_T2[0]))
        done(um, t_n)
        h_toks = to_H(xn, col("mem_g", 8 * l, 8), None, t_n, free_H[0], tok["cols"], t_n)
        bk, pk, tk = tok_proj(dr["w_kv"][l], 0, H, h_toks)
        bv, pvs, tv = tok_proj(dr["w_kv"][l], S, H)
        t_mem = t_n + h_toks
        t_n = [rms(x[:, t, :], xn[:, t, :], T2[:, 1024 * t:1024 * t + 1024], x_toks[t], t_mem) for t in range(2)]
        h2 = to_H(xn, col("mix_g", 8 * l, 8), None, t_n, tv, t_n)

        hr_last = [None]

        def hr(src_ps, name, g, t_in):
            t, ts_ = head_rms(vh(src_ps), vh(tiles[name]), row(g, 64 * l, 64).unsqueeze(1).broadcast_to([P, 8, HD]),
                              vh(T1[:, 512:1024]), 8, t_in, fa, h2, hr_last[0])
            hr_last[0] = ts_
            return t, ts_

        t_mk, t_s = hr(pk[:, :], "mk", "mk", tk)
        put(bk, t_s)
        t_mv = copy(tiles["mv"], pvs[:, :], tv, fa)
        put(bv, t_mv)

        b, ps, t_p = tok_proj(w, 3 * S, H, h2)
        t_rg = act(tiles["rg"], ps[:, :], ACT.Silu, t_p, fa)
        put(b, t_rg)
        rot = {}
        prev = None
        for n, name in enumerate(("rq", "rk")):
            b, ps, t_p = tok_proj(w, n * S, H)
            e = copy(tiles[name], ps[:, :], t_p, fa)
            put(b, e)
            for t in range(2):
                c = con("cos2")[:, 32 * t:32 * t + 32].unsqueeze(1).broadcast_to([P, 4, 32])
                s = con("sin2")[:, 32 * t:32 * t + 32].unsqueeze(1).broadcast_to([P, 4, 32])
                v = v3(name)[:, t, :].rearrange("p (h two i) -> p h two i", two=2, i=32)
                t4 = [T1[:, 1024 + 128 * i:1152 + 128 * i].rearrange("p (h i) -> p h i", h=4) for i in range(4)]
                prev = rotate(v[:, :, 0, :], v[:, :, 1, :], v[:, :, 0, :], v[:, :, 1, :], c, s, t4, e, prev, h2)
            rot[name] = prev
        b, ps, t_p = tok_proj(w, 2 * S, H)
        t_rv = copy(tiles["rv"], ps[:, :], t_p, fa, eng="dve")
        put(b, t_rv)
        ud = unit(dr["decay_m"].rearrange("p (a s) -> p a s", s=512), 2, 512, split=False)
        DT = T2
        t_D = []
        for h in range(4):
            o = DT[:, 512 * h:512 * h + 512]
            a_, b_ = (ud[1][:, 0, :], ud[1][:, 1, :]) if real else (o, o)
            e = ts(o, a_, gam[:, 4 * l + h:4 * l + h + 1], None, ALU.mult, None, ud[3], t_gam, h2)
            e = stt(o, b_, gam[:, 8 + 4 * l + h:8 + 4 * l + h + 1], o, ALU.mult, ALU.add, e)
            e_dec = e
            t_D.append(act(o, o, ACT.Exp, e))
        done(ud, e_dec)
        b, ps, t_p = tok_proj(w, 4 * S, H)
        t_pv = copy(tiles["pv"], ps[:, :], t_p, fa)
        put(b, t_pv)
        t_rq = to_T(v3("rq"), tiles["rqT"], rot["rq"], fa)
        t_rk = to_T(v3("rk"), tiles["rkT"], rot["rk"], fa)

        qt_tok = {}

        def nh(name, c0, g):
            b, ps, t_p = tok_proj(w, c0, H)
            qt_tok[name], t_s = hr(ps[:, :], name, g, t_p)
            put(b, t_s)

        nh("nq", 5 * S, "naq")
        rqT = tiles["rqT"].rearrange("p (b s) -> p b s", b=2)
        rkT = tiles["rkT"].rearrange("p (b s) -> p b s", b=2)
        bo, po, fo = take()
        t_sd = {}
        t_ret = {}

        def ret_s(h):
            b, ps, free = take()
            o = 64 * (h % 2)
            last = None
            for kt in range(2):
                last = mm(ps[:, kt * S:(kt + 1) * S], rkT[o:o + 64, h // 2, kt * P:(kt + 1) * P],
                          rqT[o:o + 64, h // 2, :], True, True, t_rq, t_rk, free, sig=(kt == 1))
            d = DT[:, 512 * h:512 * h + 512]
            t_sd[h] = stt(d, ps[:, :], 0.125, d, ALU.mult, ALU.mult, last, t_D[h])
            put(b, t_sd[h])

        def ret_o(h):
            for qt in range(2):
                for kt in range(2):
                    o = qt * S + h * HD
                    t_ret[h] = mm(po[:, o:o + HD],
                                  DT[:, 512 * h + kt * S + qt * P:512 * h + kt * S + qt * P + P],
                                  v3("rv")[:, kt, h * HD:(h + 1) * HD], kt == 0, kt == 1, t_sd[h], t_rv, fo,
                                  sig=(kt == 1 and qt == 1))

        ret_s(0)
        ret_s(1)
        nh("nk", 6 * S, "nak")
        ret_o(0)
        ret_s(2)
        ret_o(1)
        ret_s(3)
        b, ps, t_p = tok_proj(w, 7 * S, H)
        t_nv = copy(tiles["nv"], ps[:, :], t_p, fa, eng="dve")
        put(b, t_nv)
        ret_o(2)
        ret_o(3)
        ret_all = list(t_ret.values())
        rt = tiles["rq"]
        tmp = vh(T1[:, 512:1024])
        t0 = act(tmp, vh(po[:, :]), ACT.Square, ret_all, hr_last[0])
        ss = small(8)
        t = red(ss, tmp, ALU.add, t0)
        hr_last[0] = t
        t = rsqrt(ss, 8, 1.0 / HD, RMS_EPS, t)
        t = tt(vh(rt), vh(po[:, :]), ss.unsqueeze(2).broadcast_to([P, 8, HD]), ALU.mult, t, t_rq)
        put(bo, t)
        r3 = rt.rearrange("p (t c) -> p t c", t=2)
        t = tt(r3, r3, row("ret", S * l, S).unsqueeze(1).broadcast_to([P, 2, S]), ALU.mult, t, eng="pool")
        t_r = tt(rt, rt, tiles["rg"], ALU.mult, t, t_rg, eng="pool")
        nh("mq", 8 * S, "mq")
        t_nq = to_T(v3("nq"), tiles["nqT"], qt_tok["nq"], fa)
        t_nk = to_T(v3("nk"), tiles["nkT"], qt_tok["nk"], fa)
        t_mkT = to_T(v3("mk"), tiles["mkT"], t_mk, fa)

        up = unit(dr["pool_m"].rearrange("p (a s) -> p a s", s=S), 8, S, split=False)
        b, ps, free = take()
        last = None
        for g in range(4):
            for kt in range(2):
                last = mm(ps[64 * (g % 2):64 * (g % 2) + 64, (g // 2) * S:(g // 2) * S + S],
                          v3("pv")[:, kt, g * HD:(g + 1) * HD], up[1][:, 4 * kt + g, :] if real else 0,
                          kt == 0, kt == 1, up[3], t_pv, free, sig=(g == 3 and kt == 1))
        done(up, last)
        pl = tiles["rk"]
        t = copy(pl, ps[:, :], last, t_rk)
        put(b, t)
        b, ps, free = take()
        for g in range(4):
            o = 64 * (g % 2)
            a = 128 * l + 64 * (g // 2)
            c0 = COLS["pool_w"][0] + a
            last = mm(ps[o:o + 64, (g // 2) * S:(g // 2) * S + S], T["cols"][o:o + 64, c0:c0 + 64],
                      pl[o:o + 64, (g // 2) * S:(g // 2) * S + S], True, True, t, free, sig=(g == 3))
        es = []
        for j in range(2):
            s_ = col("pool_s", 2 * l + j, 1)
            es.append(ts(pl[:, j * S:(j + 1) * S], ps[:, j * S:(j + 1) * S], s_, None, ALU.mult, None, last))
        put(b, es)
        t_b = split(B[0][:, 2:4, :], B[1][:, 2:4, :], pl.rearrange("p (b s) -> p b s", b=2), es, free_B[0])
        br_tok = {1: t_b}
        b, ps, t = to_T(r3, None, t_r)
        t1 = act(B[0][:, 0:2, :], ps[:, :].rearrange("p (b s) -> p b s", b=2), ACT.Copy, t, free_B[0])
        t2_ = tt(B[1][:, 0:2, :], ps[:, :].rearrange("p (b s) -> p b s", b=2), B[0][:, 0:2, :].bitcast(F32),
                 ALU.subtract, t1)
        put(b, [t1, t2_])
        br_tok[0] = [t1, t2_]
        t_mq = to_T(v3("mq"), tiles["mqT"], qt_tok["mq"], fa)

        bias = T["TB"][:, :].rearrange("p (a s) -> p a s", s=S)
        t_bias = tt(bias, bias, con("mask").unsqueeze(1).broadcast_to([P, 8, S]), ALU.add, t_nab)
        b_used = []
        state = {}
        G3 = G[:, :].rearrange("p (b s) -> p b s", s=S)
        g_tok = {}
        wg = dr["w_gate"][l]
        order = [1, 0, 2, 3]

        def gate_units(n, slot, func):
            g_tok[n] = []
            for i in range(4):
                b, ps, t_p = T_proj(wg, n * D + S * i, H)
                o = G3[:, 8 * slot + 2 * i:8 * slot + 2 * i + 2, :]
                e = act(o, ps[:, :].rearrange("p (b s) -> p b s", b=2), func, t_p, free_G[0], g_used.get(slot))
                put(b, e)
                g_tok[n].append(e)
                free_H[0] = t_p
                yield

        g_used = {}

        def filler():
            for n, slot in ((1, 0), (0, 1)):
                for _ in gate_units(n, slot, ACT.Copy):
                    yield

        pt_free = [ret_all]

        def head(kind, h, i):
            Sb = T1[:, 512 * (i % 4):512 * (i % 4) + 512].rearrange("p (t n) -> p t n", t=2)
            pt = T2[:, 512 * (i % 4):512 * (i % 4) + 512]
            qT, kT, v = (tiles[n] for n in (("nqT", "nkT", "nv") if kind == "n" else ("mqT", "mkT", "mv")))
            tq, tk_, tv_ = (t_nq, t_nk, t_nv) if kind == "n" else (t_mq, t_mkT, t_mv)
            o = 64 * (h % 2)
            blk = h // 2

            def s1():
                b, ps, free = take()
                last = None
                for qt in range(2):
                    last = mm(ps[:, qt * S:(qt + 1) * S], qT[o:o + 64, blk * S + qt * P:blk * S + (qt + 1) * P],
                              kT[o:o + 64, blk * S:(blk + 1) * S], True, True, free, tq, tk_, sig=(qt == 1))
                p3 = ps[:, :].rearrange("p (t s) -> p t s", t=2)
                if kind == "n":
                    b4 = bias.rearrange("p (t h) s -> p t h s", h=4)[:, :, h, :]
                    e = stt(Sb, p3, 0.125, b4, ALU.mult, ALU.add, last, t_bias, state.get(i - 4), t_r, t0,
                            qt_tok["mq"])
                    b_used.append(e)
                    put(b, e)
                    state[("p", i)] = head_softmax(Sb, S, 1.0, e)[1]
                else:
                    es, state[("p", i)] = head_softmax(Sb, S, 0.125, last, p3, state.get(i - 4))
                    put(b, es)
                if kind == "n" and h == 3:
                    free_TB[0] = b_used

            def s2():
                state[("t", i)], state[i] = probs_T(Sb, 1, pt, state[("p", i)], pt_free[0])

            def s3():
                pt_free[0] = pv(h, 1, pt, lambda g, kt: v.rearrange("p (t c) -> p t c", t=2)[:, kt, h * HD:(h + 1) * HD],
                                state[("t", i)], (4 if kind == "n" else 6) + h // 2, tv_)

            return s1, s2, s3

        pipeline([head("n", h, h) for h in range(4)] + [head("m", h, 4 + h) for h in range(4)], filler())
        br_tok[2] = [B_tok[4], B_tok[5]]
        br_tok[3] = [B_tok[6], B_tok[7]]
        free_AR[0] = pt_free[0]

        for n, slot in ((1, 0), (0, 1)):
            v = G[:, 2048 * slot:2048 * slot + 2048]
            for hh in range(2):
                vv = v[:, 1024 * hh:1024 * hh + 1024]
                g_tok[n].append(act(vv, vv, ACT.Sigmoid, g_tok[n][0:4]))
        m_toks = []
        s_done = [state[7], state[6], state[5], state[4]]
        prev = {}
        for z, n in enumerate(order):
            slot = z % 2
            if z >= 2:
                for _ in gate_units(n, slot, ACT.Sigmoid):
                    pass
            u = unit(dr["w_br"][l, n].rearrange("(k p) c -> p k c", p=P), 2, D)
            used = []
            for m in range(4):
                b, ps, free = take()
                last = proj_T(u, B, 2, 2 * m, ps, free, br_tok[n], k0=2 * n)
                gv = G[:, 2048 * slot + 512 * m:2048 * slot + 512 * m + 512]
                tv_ = T1[:, 512 * m:512 * m + 512]
                if z == 0:
                    e = tt(tv_, gv, ps[:, :], ALU.mult, last, g_tok[n], s_done)
                    put(b, e)
                else:
                    e = tt(gv, gv, ps[:, :], ALU.mult, last, g_tok[n])
                    put(b, e)
                    e = tt(tv_, tv_, gv, ALU.add, e, prev[m], eng="pool" if m % 2 else "dve")
                prev[m] = e
                used.append(e)
                if z == 3:
                    m_toks += split(H[0][:, 2 * m:2 * m + 2, :], H[1][:, 2 * m:2 * m + 2, :],
                                    tv_.rearrange("p (k s) -> p k s", k=2), e, free_H[0])
            done(u, last)
            g_used[slot] = used
        free_G[0] = [g_used[0], g_used[1]]
        free_B[0] = last
        B_tok.clear()
        x_t = [None, None]
        xs = [[], []]
        for c in range(2):
            bs, ts_ = tok_proj512(dr["w_out2"][l], 512 * c, 8, H, m_toks)
            for t in range(2):
                xv = x[:, t, 512 * c:512 * c + 512]
                e = tt(xv, xv, bs[t][1][:, :], ALU.add, ts_[t], t_n)
                put(bs[t][0], e)
                xs[t].append(e)
            free_H[0] = ts_[1]
        t_n = [rms(x[:, t, :], xn[:, t, :], T2[:, 1024 * t:1024 * t + 1024], xs[t], m_toks, pt_free[0])
               for t in range(2)]
        h3 = to_H(xn, col("ffn_g", 8 * l, 8), None, t_n, free_H[0], t_n)
        wf, wd = dr["w_ff1"][l], dr["w_ff2"][l]
        acc, y, tu = ffn(11, lambda i: (w_unit8(wf, S * i), 8, S),
                         lambda i: (w_unit8(wf, FF + S * i), 8, S),
                         lambda i: (wd[S * i:S * i + S, :].rearrange("(k p) c -> p k c", p=P), 2, D),
                         None, h3, h3)
        free_H[0] = tu
        out = [[], []]
        for t in range(2):
            for c in range(2):
                xv = x[:, t, 512 * c:512 * c + 512]
                b, ps, _ = acc[2 * t + c]
                e = tt(xv, xv, ps[:, :], ALU.add, y[2 * t + c])
                put(b, e)
                out[t].append(e)
        free_T1[0] = [y, h3]
        free_T2[0] = h3
        return out

    mod_part(0, 1)
    mod_part(0, 0)
    t_gam = decays()
    xt = [tok["x"], tok["x"]]
    for l in range(L):
        xt = first_layer(l, xt)
    for l in range(L):
        xt = second_layer(l, xt, t_gam)
    t_out = []
    for t in range(2):
        dma("sp", "s_out", dr["out"][t * P:(t + 1) * P, :], x[:, t, :], xt[t])
    Q.wait("sp", [("s_out", 32)])
    return Q


def build(nc, dr):
    ctx = ExitStack()
    with ctx:
        def sb(name, shape, dt=F32):
            return ctx.enter_context(nc.sbuf_tensor(name, shape, dt))

        T = {
            "raw": [sb(f"raw{i}", [P, 2048]) for i in range(NRAW)],
            "whi": [sb(f"whi{i}", [P, 2048], F32R) for i in range(NSPL)],
            "wlo": [sb(f"wlo{i}", [P, 2048], F32R) for i in range(NSPL)],
            "Hh": sb("Hh", [P, 8, S], F32R), "Hl": sb("Hl", [P, 8, S], F32R),
            "Bh": sb("Bh", [P, 8, S], F32R), "Bl": sb("Bl", [P, 8, S], F32R),
            "x": sb("xs", [P, 2, D]), "T1": sb("T1", [P, 2048]), "T2": sb("T2", [P, 2048]),
            "G": sb("G", [P, 4096]), "AR": sb("AR", [P, 8704]),
            "cons": sb("cons_s", [P, N_CONS]), "cols": sb("cols_s", [P, N_COLS]), "rows": sb("rows_s", [P, N_ROWS]),
            "csil": sb("csil", [P, 8]), "modT": sb("modT", [P, 96]), "crow": sb("crow", [16, S]), "TB": sb("TB", [P, 2048]), "R": sb("R", [P, 200]), "gam": sb("gam", [P, 16]),
            "small": sb("small", [P, 240]), "mhalf": sb("mhalf", [P, 8]),
            "ps": [ctx.enter_context(nc.psum_tensor(f"ps{i}", [P, 512], F32)) for i in range(8)],
        }
        units = []
        plan(nc, T, dr, units, False)
        Q = plan(nc, T, dr, units, True)
        sems = {}
        for name in sorted({s for q in Q.q.values() for it in q if it[0] == "op" and it[2] for s in [it[2][0]]}):
            sems[name] = ctx.enter_context(nc.semaphore("c_" + name))

        def emit(eng, e):
            for it in Q.q[eng]:
                if it[0] == "wait":
                    e.wait_ge(sems[it[1]], it[2])
                else:
                    ins = it[1](e)
                    if it[2]:
                        ins.then_inc(sems[it[2][0]], it[2][1])

        block = ctx.enter_context(nc.Block())

        @block.sync
        def _(e):
            emit("sp", e)

        @block.gpsimd
        def _(e):
            emit("pool", e)

        @block.scalar
        def _(e):
            emit("act", e)

        @block.tensor
        def _(e):
            emit("pe", e)

        @block.vector
        def _(e):
            emit("dve", e)


def kernel(**inp):
    import concourse.bacc as bacc
    from concourse.bass_utils import run_bass_kernel_spmd

    a = {k: np.ascontiguousarray(np.asarray(v)) for k, v in inp.items()}

    def columns(v):
        return v.reshape(-1, P).T

    pw = a["pool_w_2"].reshape(L, 2, 2, HD, HD).transpose(2, 3, 0, 1, 4).reshape(P, -1)
    router = a["w_router"].reshape(8, P, NE).transpose(1, 0, 2).reshape(P, -1)
    cols = np.concatenate([columns(a["c"]), columns(a["b_ada"]), columns(a["norm_mix_g_2"]),
                           columns(a["norm_mem_g_2"]), columns(a["norm_ffn_g_2"]), columns(a["pool_scale_2"]),
                           router, pw], 1)
    rows = np.concatenate([a[n].reshape(-1) for n in (
        "q_norm_g", "k_norm_g", "na_q_norm_g_2", "na_k_norm_g_2", "mem_q_norm_g_2", "mem_k_norm_g_2",
        "ret_norm_g_2", "router_bias", "ret_decay_fwd_2", "ret_decay_bwd_2")])
    t = np.arange(S)
    r_off = (t[None, :] // 64 - t[:, None] // 64) + 7
    c_off = np.clip(t[None, :] % 64 - t[:, None] % 64, -15, 15) + 15
    na = a["na_rpb_2"][:, :, r_off, c_off]
    na = na.reshape(L, 4, 2, P, S).transpose(3, 0, 2, 1, 4)

    arrays = {
        "x": a["x"][0], "mem": a["mem_2"][0], "cols": cols, "rows": rows, "na_b": na,
        "w_ada": a["w_ada"], "w_in": a["w_in"], "w_pa": a["w_branch_a"], "w_pb": a["w_branch_b"],
        "w_out": a["w_out"], "ln1_g": a["ln1_g"], "ln1_b": a["ln1_b"], "ln2_g": a["ln2_g"], "ln2_b": a["ln2_b"],
        "w_g": a["w_exp_gate"], "w_u": a["w_exp_up"], "w_d": a["w_exp_down"],
        "w_in2": a["w_in_2"], "w_gate": a["w_gate_2"], "w_kv": a["w_mem_kv_2"], "w_br": a["w_branch_2"],
        "w_out2": a["w_out_2"], "w_ff1": a["w_ffn_in_2"], "w_ff2": a["w_ffn_out_2"],
    }
    arrays.update(shape_constants())
    nc = bacc.Bacc("TRN2", target_bir_lowering=False, num_devices=1)
    feed, dr = {}, {}
    for k, v in arrays.items():
        v = np.ascontiguousarray(v)
        feed["in_" + k] = v
        dr[k] = nc.dram_tensor("in_" + k, v.shape, F32, kind="ExternalInput").ap()
    dr["out"] = nc.dram_tensor("out_0", (S, D), F32, kind="ExternalOutput").ap()
    build(nc, dr)
    r = run_bass_kernel_spmd(nc, [feed], core_ids=[0])
    return r.results[0]["out_0"].reshape(1, S, D)
```

```python
import math
from collections import deque
from contextlib import ExitStack

import numpy as np
import concourse.bass as bass
from concourse import mybir

F32 = mybir.dt.float32
F32R = mybir.dt.float32r
ALU = mybir.AluOpType
ACT = mybir.ActivationFunctionType
AX = mybir.AxisListType

P = 128
D = 1024
S = 256
HD = 64
L = 2
NE = 16
FF = 2816
ALPHA = (2.0 * L) ** 0.25
LN_EPS = 1e-5
RMS_EPS = 1e-6
W_IN1 = 5120
NRAW = 4
NSPL = 3

COLS = {}
ROWS = {}
CONS = {}


def _spans(table, items):
    at = 0
    for name, n in items:
        table[name] = (at, at + n)
        at += n
    return at


N_COLS = _spans(COLS, [("c", 8), ("b_ada", 96), ("mix_g", 16), ("mem_g", 16), ("ffn_g", 16),
                       ("pool_s", 4), ("router", 128), ("pool_w", 256)])
N_ROWS = _spans(ROWS, [("qn", 128), ("kn", 128), ("naq", 128), ("nak", 128), ("mq", 128), ("mk", 128),
                       ("ret", 512), ("rb", 16), ("dec", 16)])
N_CONS = _spans(CONS, [("ident", 128), ("cos1", 64), ("sin1", 64), ("cos2", 64), ("sin2", 64),
                       ("mask", 256)])


def shape_constants():
    f = np.float32
    t = np.arange(S)
    cons = np.zeros((P, N_CONS), f)

    def put(name, a):
        cons[:, CONS[name][0]:CONS[name][1]] = a

    def tiles(a):
        return a.reshape(2, P, -1).transpose(1, 0, 2).reshape(P, -1)

    put("ident", np.eye(P, dtype=f))
    inv = (f(10000.0) ** (-np.arange(0, 32, 2, dtype=f) / f(32))).astype(f)
    row, col = (t // 64).astype(f), (t % 64).astype(f)
    ang = np.concatenate([row[:, None] * inv, col[:, None] * inv], -1).astype(f)
    put("cos1", tiles(np.cos(ang)))
    put("sin1", tiles(np.sin(ang)))
    inv = (f(10000.0) ** (-np.arange(32, dtype=f) / f(32))).astype(f)
    ang = (t.astype(f)[:, None] * inv[None, :]).astype(f)
    put("cos2", tiles(np.cos(ang)))
    put("sin2", tiles(np.sin(ang)))
    qc, kc = np.arange(P) % 64, t % 64
    win = np.clip(qc - 8, 0, 48)
    ok = (kc[None, :] >= win[:, None]) & (kc[None, :] < win[:, None] + 16)
    put("mask", np.where(ok, f(0), f(-1e30)))

    dist = np.abs(t[:, None] - t[None, :])
    alibi = np.zeros((S, 3, S), f)
    for g, dil in enumerate((1, 4, 16)):
        seen = (dist % dil == 0) & (dist <= 64 * dil)
        alibi[:, g] = np.where(seen, dist, 1e30)
    alibi = tiles(alibi.reshape(S, -1))

    pool = np.zeros((S, 4, S), f)
    for g, w in enumerate((2, 4, 8, 16)):
        lo, hi = np.clip(t - w // 2, 0, S), np.clip(t + w // 2, 0, S)
        inside = (t[:, None] >= lo[None, :]) & (t[:, None] < hi[None, :])
        pool[:, g] = inside / (hi - lo)[None, :] - np.eye(S)
    pool = tiles(pool.reshape(S, -1))

    k, q = t[:, None], t[None, :]
    decay = np.stack([tiles(np.maximum(q - k, 0).astype(f)), tiles(np.maximum(k - q, 0).astype(f))], 1)
    return {"cons": cons, "alibi": np.ascontiguousarray(alibi), "pool_m": np.ascontiguousarray(pool.astype(f)),
            "decay_m": np.ascontiguousarray(decay.reshape(P, -1).astype(f))}


class Queues:

    def __init__(self):
        self.q = {n: [] for n in ("pe", "act", "dve", "pool", "sp")}
        self.n = {}
        self.seen = {n: {} for n in self.q}
        self.marks = []

    def wait(self, eng, deps):
        for d in deps:
            if d is None:
                continue
            if isinstance(d, list):
                self.wait(eng, d)
                continue
            s, v = d
            if self.seen[eng].get(s, 0) < v:
                self.seen[eng][s] = v
                self.q[eng].append(("wait", s, v))

    def mark(self, label):
        self.marks.append((label, {e: sum(1 for i in q if i[0] == "op") for e, q in self.q.items()}))

    def op(self, eng, fn, *deps, sig=True):
        self.wait(eng, deps)
        if sig:
            self.n[eng] = self.n.get(eng, 0) + 1
        self.q[eng].append(("op", fn, (eng, 1) if sig else None))
        return (eng, self.n.get(eng, 0))

    def dma(self, eng, sem, out, src, *deps):
        self.wait(eng, deps)
        self.n[sem] = self.n.get(sem, 0) + 16
        self.q[eng].append(("op", lambda e: e.dma_start(out, src), (sem, 16)))
        return (sem, self.n[sem])


def plan(nc, T, dr, units, real):
    Q = Queues()
    op, dma = Q.op, Q.dma

    n_unit = len(units)
    st = {"dma": 0, "spl": 0, "use": 0}
    landed, released, prepared = {}, {}, {}
    spl_free = [None] * NSPL
    spl_ids = [i for i, u in enumerate(units) if u[3]]
    spl_no = {u: k for k, u in enumerate(spl_ids)}
    held = {}
    hold = [False]

    def resume():
        hold[0] = False
        pump()

    def pump():
        if not real or hold[0]:
            return
        while True:
            moved = False
            i = st["dma"]
            if i < n_unit and (i < NRAW or (i - NRAW) in released):
                src, a, b, _ = units[i]
                dst = T["raw"][i % NRAW][:, 0:a * b].rearrange("p (a b) -> p a b", a=a)
                landed[i] = dma("sp", f"s_raw{i % NRAW}", dst, src, released.get(i - NRAW))
                st["dma"] += 1
                moved = True
            k = st["spl"]
            if k < len(spl_ids):
                i = spl_ids[k]
                if i in landed and (k < NSPL or held.get(k - NSPL)):
                    _, a, b, _ = units[i]
                    j = k % NSPL
                    raw = T["raw"][i % NRAW][:, 0:a * b]
                    hi, lo = T["whi"][j][:, 0:a * b], T["wlo"][j][:, 0:a * b]
                    t1 = op("act", lambda e, hi=hi, raw=raw: e.activation(hi, raw, ACT.Copy),
                            landed[i], held.get(k - NSPL))
                    t2 = op("dve", lambda e, hi=hi, lo=lo, raw=raw:
                            e.tensor_tensor(lo, raw, hi.bitcast(F32), ALU.subtract), t1)
                    released[i] = [t1, t2]
                    prepared[i] = [t1, t2]
                    st["spl"] += 1
                    moved = True
            if not moved:
                return

    def unit(src, a, b, split=True):
        i = st["use"]
        st["use"] += 1
        hold[0] = False
        if not real:
            units.append((src, a, b, split))
            return (i, None, None, None)
        pump()
        if split:
            j = spl_no[i] % NSPL
            hi = T["whi"][j][:, 0:a * b].rearrange("p (a b) -> p a b", a=a)
            lo = T["wlo"][j][:, 0:a * b].rearrange("p (a b) -> p a b", a=a)
            return (i, hi, lo, prepared[i])
        raw = T["raw"][i % NRAW][:, 0:a * b].rearrange("p (a b) -> p a b", a=a)
        return (i, raw, None, landed[i])

    def done(u, tok):
        i = u[0]
        if real:
            if units[i][3]:
                held[spl_no[i]] = tok
            else:
                released[i] = tok
            pump()

    if not real:
        full = op

        def op(eng, fn, *deps, sig=True):
            return None

        def dma(*a):
            return None

    ring = deque((b, None) for b in range(8))

    def take():
        b, free = ring.popleft()
        return b, T["ps"][b], free

    def put(b, tok):
        ring.append((b, tok))

    def col(name, j=0, n=1):
        a = COLS[name][0] + j
        return T["cols"][:, a:a + n]

    def row(name, j, n):
        a = ROWS[name][0] + j
        return T["rows"][:, a:a + n]

    def con(name):
        a, b = CONS[name]
        return T["cons"][:, a:b]

    ident = con("ident")
    small_at = [0]

    def small(n):
        if small_at[0] + n > T["small"].shape[1]:
            small_at[0] = 0
        a = small_at[0]
        small_at[0] += n
        return T["small"][:, a:a + n]

    H = (T["Hh"], T["Hl"])
    B = (T["Bh"], T["Bl"])
    x, T1, T2, G, AR = T["x"], T["T1"], T["T2"], T["G"], T["AR"]

    def arena(a, n, **k):
        v = AR[:, a:a + n]
        return v

    def mm(out, lhsT, rhs, start, stop, *deps, sig=False):
        return op("pe", lambda e: e.matmul(out, lhsT, rhs, start=start, stop=stop), *deps, sig=sig)

    def mm3(out, lhsT, rhs, start, stop, *deps, sig=False):
        (lh, ll), (rh, rl) = lhsT, rhs
        mm(out, lh, rh, start, False, *deps)
        mm(out, lh, rl, False, False)
        return mm(out, ll, rh, False, stop, sig=sig)

    def tr(out, src, *deps, sig=False):
        return op("pe", lambda e: e.transpose(out, src, ident), *deps, sig=sig)

    def act(out, src, func, *deps, **k):
        return op("act", lambda e: e.activation(out, src, func, **k), *deps)

    def tt(out, a, b, o, *deps, eng="dve"):
        return op(eng, lambda e: e.tensor_tensor(out, a, b, o), *deps)

    def ts(out, a, s1, s2, o0, o1, *deps, eng="dve"):
        if o1 is None:
            return op(eng, lambda e: e.tensor_scalar(out, a, s1, None, o0), *deps)
        return op(eng, lambda e: e.tensor_scalar(out, a, s1, s2, o0, o1), *deps)

    def stt(out, a, s, b, o0, o1, *deps):
        return op("dve", lambda e: e.scalar_tensor_tensor(out=out, in0=a, scalar=s, in1=b, op0=o0, op1=o1), *deps)

    def red(out, a, o, *deps):
        return op("dve", lambda e: e.tensor_reduce(out, a, AX.X, o), *deps)

    def copy(out, a, *deps, eng="act"):
        if eng == "act":
            return act(out, a, ACT.Copy, *deps)
        return op(eng, lambda e: e.tensor_copy(out, a), *deps)

    def split(hi, lo, src, *deps):
        t1 = act(hi, src, ACT.Copy, *deps)
        t2 = tt(lo, src, hi.bitcast(F32), ALU.subtract, t1, *deps)
        return [t1, t2]

    def rsqrt(ap, n, scale, eps, *deps):
        t = ts(ap, ap, scale, eps, ALU.mult, ALU.add, *deps, eng="pool")
        return op("pool", lambda e: e.tensor_tensor(ap, ap, T["mhalf"][:, 0:n], ALU.pow), t, tok["mhalf"])

    def proj_T(u, rhs, n_k, blk0, out, *deps, k0=0):
        last = None
        for j in range(2):
            for k in range(n_k):
                c = (blk0 + j) * P
                last = mm3(out[:, j * S:(j + 1) * S],
                           (u[1][:, k, c:c + P], u[2][:, k, c:c + P]) if real else (0, 0),
                           (rhs[0][:, k0 + k, :], rhs[1][:, k0 + k, :]), k == 0, k == n_k - 1,
                           u[3], *deps, sig=(j == 1 and k == n_k - 1))
        return last

    def proj_tok256(u, lhs, out, *deps):
        last = None
        for t in range(2):
            for k in range(8):
                last = mm3(out[:, t * S:(t + 1) * S],
                           (lhs[0][:, k, t * P:(t + 1) * P], lhs[1][:, k, t * P:(t + 1) * P]),
                           (u[1][:, k, :], u[2][:, k, :]) if real else (0, 0), k == 0, k == 7,
                           u[3], *deps, sig=(t == 1 and k == 7))
        return last

    def w_unit8(w, c0, n=256):
        return w[:, c0:c0 + n].rearrange("(k p) c -> p k c", p=P)

    def tok_proj(w, c0, lhs, *deps):
        u = unit(w_unit8(w, c0), 8, S)
        b, ps, free = take()
        t = proj_tok256(u, lhs, ps, free, *deps)
        done(u, t)
        return b, ps, t

    def T_proj(w, c0, rhs, *deps):
        u = unit(w_unit8(w, c0), 8, S)
        b, ps, free = take()
        t = proj_T(u, rhs, 8, 0, ps, free, *deps)
        done(u, t)
        return b, ps, t

    def tok_proj512(w, rhs_cols, n_kt, lhs, lhs_split, end=False):
        bs = [take() for _ in range(2)]
        us = [unit(w[a * 512:(a + 1) * 512, rhs_cols:rhs_cols + 512].rearrange("(k p) c -> p k c", p=P), 4, 512)
              for a in range(n_kt // 4)]
        toks = []
        for t in range(2):
            for a, u in enumerate(us):
                for k in range(4):
                    kk = 4 * a + k
                    last = mm3(bs[t][1][:, :],
                               (lhs[0][:, kk, t * P:(t + 1) * P], lhs[1][:, kk, t * P:(t + 1) * P]),
                               (u[1][:, k, :], u[2][:, k, :]) if real else (0, 0),
                               kk == 0, kk == n_kt - 1, u[3], bs[t][2], lhs_split[t][kk], sig=(k == 3))
                if t == 1:
                    if end:
                        hold[0] = True
                    done(u, last)
            toks.append(last)
        return bs, toks

    def tok_proj_two(w, cs, lhs, lhs_split):
        us = [unit(w_unit8(w, c), 8, S) for c in cs]
        bs = [take() for _ in cs]
        res = []
        for t in range(2):
            for u, (b, ps, free) in zip(us, bs):
                for k in range(8):
                    last = mm3(ps[:, t * S:(t + 1) * S],
                               (lhs[0][:, k, t * P:(t + 1) * P], lhs[1][:, k, t * P:(t + 1) * P]),
                               (u[1][:, k, :], u[2][:, k, :]) if real else (0, 0), k == 0, k == 7,
                               u[3], lhs_split[t], free, sig=(k == 7))
                if t == 1:
                    done(u, last)
                    res.append((b, ps, last))
        return res

    tok = {}
    tok["mhalf"] = op("pool", lambda e: e.memset(T["mhalf"][:, :], -0.5))
    tok["ones"] = op("pool", lambda e: e.memset(T["ones"][:, :], 1.0))
    tok["cons"] = dma("act", "s_cons", T["cons"][:, :], dr["cons"])
    tok["cols"] = dma("act", "s_cols", T["cols"][:, :], dr["cols"])
    tok["x"] = dma("act", "s_x", x[:, :, :], dr["x"].rearrange("(t p) d -> p t d", p=P))
    tok["rows"] = dma("act", "s_rows", T["rows"][:, :], dr["rows"].partition_broadcast(P))

    csil = T["csil"]
    t_c = act(csil[:, :], col("c", 0, 8), ACT.Silu, tok["cols"])
    modT = T["modT"]
    mod_tok = {}

    mod_list = [(0, 1), (0, 0), (0, 2), (0, 4), (0, 3), (0, 5), (1, 1), (1, 0), (1, 2), (1, 4), (1, 3), (1, 5)]
    mod_work = deque((l, part, h, a) for l, part in mod_list for h in range(2) for a in range(2))
    mod_acc = [AR[:, 7936 + 512 * i:8448 + 512 * i] for i in range(2)]
    mod_free = [None, None]
    mod_pend = []

    def mod_final():
        while mod_pend:
            l, part, h, acc, e = mod_pend.pop(0)
            b, ps, free = take()
            for j in range(4):
                last = mm(ps[:, j:j + 1], acc[:, j * P:(j + 1) * P], T["ones"][:, 0:1], True, True, e, free,
                          tok["ones"], sig=(j == 3))
            mod_free[h] = last
            a = 48 * l + 8 * part + 4 * h
            t = tt(modT[:, a:a + 4], ps[:, 0:4], col("b_ada", a, 4), ALU.add, last, tok["cols"])
            put(b, t)
            if part in (1, 4):
                t = ts(modT[:, a:a + 4], modT[:, a:a + 4], 1.0, None, ALU.add, None, t)
            mod_tok.setdefault((l, part), []).append(t)

    def mod_step(n=1):
        for _ in range(n):
            if not mod_in:
                mod_final()
                return
            l, part, h, a = mod_work.popleft()
            c0 = part * D + h * 512
            slot, t_in = mod_in.popleft()
            acc = mod_acc[h]
            e = mod_run.get(h)
            for k in range(4):
                wk = slot[:, k * 512:(k + 1) * 512]
                c = csil[:, 4 * a + k:4 * a + k + 1]
                if a == 0 and k == 0:
                    e = ts(acc, wk, c, None, ALU.mult, None, t_in, t_c, mod_free[h])
                else:
                    e = stt(acc, wk, c, acc, ALU.mult, ALU.add, t_in, e)
            mod_run[h] = e
            mod_load(slot, e)
            mod_final()
            if a == 1:
                mod_pend.append((l, part, h, acc, e))

    mod_run = {}
    mod_src = deque((l, part, h, a) for l, part in mod_list for h in range(2) for a in range(2))
    mod_in = deque()
    mod_left = [0]
    mod_sem = [0]

    def mod_load(slot, *deps):
        if not mod_left[0]:
            return
        mod_left[0] -= 1
        l, part, h, a = mod_src.popleft()
        c0 = part * D + h * 512
        src = dr["w_ada"][l][a * 512:(a + 1) * 512, c0:c0 + 512].rearrange("(k p) c -> p k c", p=P)
        mod_sem[0] = (mod_sem[0] + 1) % 5
        t = dma("sp", f"s_mod{mod_sem[0]}", slot.rearrange("p (k c) -> p k c", k=4), src, *deps)
        mod_in.append((slot, t))

    def mod_phase(n, slots, *deps):
        assert not mod_in
        mod_left[0] = n
        for v in slots:
            mod_load(v, *deps)

    def mod_until(l, part):
        while any(w_[0:2] == (l, part) for w_ in mod_work):
            assert mod_in
            mod_step()
        mod_final()

    def mod_cols(l, part):
        return modT[:, 48 * l + 8 * part:48 * l + 8 * part + 8]

    def mod_bcast(l, part, out, *deps):
        b, ps, free = take()
        m = mod_cols(l, part)
        t = op("pe", lambda e, o=ps[0:8, 0:P]: e.transpose(o, m, ident), mod_tok[(l, part)], free, tok["cons"])
        t = copy(T["crow"][0:8, 0:P], ps[0:8, 0:P], t)
        put(b, t)
        toks = []
        for h in range(2):
            b, ps, free = take()
            last = None
            for j in range(4):
                kk = 4 * h + j
                last = mm(ps[:, j * P:(j + 1) * P], ident[0:8, kk:kk + 1].broadcast_to([8, P]),
                          T["crow"][0:8, 0:P], True, True, t, free, sig=(j == 3))
            e = copy(out[:, h * 512:(h + 1) * 512], ps[:, :], last, *deps)
            put(b, e)
            toks.append(e)
        return toks

    def ln(src, dst, *deps):
        sb = small(12)
        for h in range(2):
            t = op("dve", lambda e, h=h: e.bn_stats(sb[:, 6 * h:6 * h + 6], src[:, 512 * h:512 * h + 512]), *deps)
        mv = small(2)
        t = op("dve", lambda e: e.bn_aggr(mv, sb), t)
        t = rsqrt(mv[:, 1:2], 1, 1.0, LN_EPS, t)
        return ts(dst, src, mv[:, 0:1], mv[:, 1:2], ALU.subtract, ALU.mult, t)

    def rms(src, dst, junk, *deps, dve=False):
        ss = small(1)
        t = act(junk, src, ACT.Square, *deps, accum_out=ss)
        t = rsqrt(ss, 1, 1.0 / D, RMS_EPS, t)
        if dve:
            return ts(dst, src, ss, None, ALU.mult, None, t)
        return act(dst, src, ACT.Copy, t, scale=ss)

    def ln_act(src, dst, *deps):
        sm, ss = small(1), small(1)
        t = act(dst, src, ACT.Copy, *deps, accum_out=sm)
        t = ts(sm, sm, -1.0 / D, None, ALU.mult, None, t, eng="pool")
        t1 = act(dst, src, ACT.Square, t, bias=sm, accum_out=ss)
        t = rsqrt(ss, 1, 1.0 / D, LN_EPS, t1)
        t = tt(sm, sm, ss, ALU.mult, t, t1, eng="pool")
        return act(dst, src, ACT.Identity, t, scale=ss, bias=sm)

    def to_H(src, scale, bias, src_toks, scr, *deps):
        toks = []
        f3 = scr.rearrange("p (k s) -> p k s", s=S)
        for t in range(2):
            mine = []
            for kq in range(2):
                b, ps, free = take()
                for j in range(4):
                    k = 4 * kq + j
                    last = tr(ps[:, j * P:(j + 1) * P], src[:, t, k * P:(k + 1) * P], src_toks[t], free,
                              tok["cons"], sig=(j == 3))
                es = []
                for j in range(4):
                    k = 4 * kq + j
                    o, i = f3[:, k, t * P:(t + 1) * P], ps[:, j * P:(j + 1) * P]
                    if bias is None:
                        e = ts(o, i, scale[:, k:k + 1], None, ALU.mult, None, last, *deps)
                    else:
                        e = ts(o, i, scale[:, k:k + 1], bias[:, k:k + 1], ALU.mult, ALU.add, last, *deps)
                    es.append(e)
                put(b, es)
                v = (slice(None), slice(4 * kq, 4 * kq + 4), slice(t * P, (t + 1) * P))
                e = act(H[0][v], f3[v], ACT.Copy, es)
                mine += es + [e, tt(H[1][v], f3[v], H[0][v].bitcast(F32), ALU.subtract, e,
                                    eng="pool" if kq == 0 else "dve")]
            toks.append(mine)
        return toks

    def head_rms(src, dst, g, tmp, n, *deps):
        t0 = act(tmp, src, ACT.Square, *deps)
        ss = small(n)
        t = red(ss, tmp, ALU.add, t0)
        t = rsqrt(ss, n, 1.0 / HD, RMS_EPS, t)
        t_src = tt(dst, src, ss.unsqueeze(2).broadcast_to([P, n, HD]), ALU.mult, t, *deps)
        t = tt(dst, dst, g, ALU.mult, t_src, tok["rows"], eng="pool")
        return t, t_src

    def rotate(x0, x1, o0, o1, c, s, t4, *deps):
        a = tt(t4[0], x0, c, ALU.mult, *deps, tok["cons"], eng="pool")
        b = tt(t4[1], x1, s, ALU.mult, *deps, eng="pool")
        cc = tt(t4[2], x0, s, ALU.mult, *deps, eng="pool")
        d = tt(t4[3], x1, c, ALU.mult, *deps, eng="pool")
        e = tt(o0, t4[0], t4[1], ALU.subtract, b, d, eng="pool")
        f = tt(o1, t4[2], t4[3], ALU.add, d, eng="pool")
        return f

    def head_softmax(Sb, n, qscale, toks_in, src=None, *deps):
        frm = Sb if src is None else src
        mx = small(2)
        t = red(mx, frm, ALU.max, toks_in, *deps)
        t = ts(mx, mx, -qscale, None, ALU.mult, None, t)
        sm = small(2)
        es = [act(Sb[:, i, :], frm[:, i, :], ACT.Exp, t, bias=mx[:, i:i + 1], scale=qscale,
                  accum_out=sm[:, i:i + 1]) for i in range(2)]
        t = op("dve", lambda e: e.reciprocal(sm, sm), es)
        rs = [ts(Sb[:, i, :], Sb[:, i, :], sm[:, i:i + 1], None, ALU.mult, None, t) for i in range(2)]
        return es, rs

    def probs_T(Sb, n_g, PT, toks, free_pt):
        outs = []
        for g in range(n_g):
            b, ps, free = take()
            last = None
            for kt in range(2):
                for qt in range(2):
                    last = tr(ps[:, kt * S + qt * P:kt * S + (qt + 1) * P],
                              Sb[:, qt, g * S + kt * P:g * S + (kt + 1) * P], toks[qt], free,
                              sig=(kt == 1 and qt == 1))
            e = copy(PT[:, g * 512:(g + 1) * 512], ps[:, :], last, free_pt, eng="act" if g % 2 == 0 else "dve")
            put(b, e)
            outs.append(e)
        return outs, last

    pair = {}

    def pv(h, n_g, PT, v, toks, dst_blk, v_tok):
        half = h % 2
        if half == 0:
            pair["b"] = take()
        b, ps, free = pair["b"]
        last = None
        n = 2 * n_g
        for g in range(n_g):
            for kt in range(2):
                i = 2 * g + kt
                last = mm(ps[64 * half:64 * half + 64, 0:S], v(g, kt), PT[:, i * S:(i + 1) * S],
                          i == 0, i == n - 1, toks, free, v_tok, sig=(i == n - 1))
        res = last
        if half == 1:
            t1 = act(B[0][:, dst_blk, :], ps[:, 0:S], ACT.Copy, last, free_B[0])
            t2 = tt(B[1][:, dst_blk, :], ps[:, 0:S], B[0][:, dst_blk, :].bitcast(F32), ALU.subtract, t1, free_B[0])
            put(b, [t1, t2])
            B_tok[dst_blk] = [t1, t2]
        return res

    free_B = [None]
    B_tok = {}

    def pipeline(heads, filler, per=1):
        n = len(heads)
        for i in range(n + 2):
            if i < n:
                heads[i][0]()
            for _ in range(per):
                next(filler, None)
            if 0 <= i - 2 < n:
                heads[i - 2][2]()
            if 0 <= i - 1 < n:
                heads[i - 1][1]()
        for _ in filler:
            pass

    def ffn(n, ug, uu, ud, comb, h_toks, hook, tail, *deps, hook2=lambda i: None):
        acc = []
        act_done, pe_done, half_done = {}, {}, {}
        y = []

        def down(*ii):
            if not acc:
                acc.extend(take() for _ in range(4))
            us = [unit(*ud(i)) for i in ii]
            last = None
            for t in range(2):
                for i, u in zip(ii, us):
                    for c in range(2):
                        for f in range(2):
                            a = (i % 4) * 2 + f
                            last = mm3(acc[2 * t + c][1][:, :],
                                       (B[0][:, a, t * P:(t + 1) * P], B[1][:, a, t * P:(t + 1) * P]),
                                       (u[1][:, f, c * 512:(c + 1) * 512], u[2][:, f, c * 512:(c + 1) * 512])
                                       if real else (0, 0),
                                       i == 0 and f == 0, i == n - 1 and f == 1, u[3], act_done[i],
                                       acc[2 * t + c][2], sig=(f == 1))
                        if i == n - 1:
                            y.append(last)
                    if t == 1:
                        if i >= n - 2:
                            hold[0] = True
                        done(u, last)
                        pe_done[i] = last

        def finish(i):
            s = T1[:, (i % 2) * 512:(i % 2) * 512 + 512]
            s3 = s.rearrange("p (f t) -> p f t", f=2)
            e = half_done[i]
            if comb is not None:
                cb, ct = comb(i)
                e = tt(s3, s3, cb.unsqueeze(1).broadcast_to([P, 2, S]), ALU.mult, e, ct, eng="pool")
            a = (i % 4) * 2
            act_done[i] = split(B[0][:, a:a + 2, :], B[1][:, a:a + 2, :], s3, e, pe_done.get(i - 4), free_B[0])

        lag = 2 if comb is not None else 1
        tu = None
        for i in range(n):
            ug_ = unit(*ug(i))
            bg, pg, fg = take()
            tg = proj_T(ug_, H, 8, 0, pg, fg, h_toks)
            done(ug_, tg)
            uu_ = unit(*uu(i))
            bu, pu, fu = take()
            tu = proj_T(uu_, H, 8, 0, pu, fu)
            done(uu_, tu)
            s = T1[:, (i % 2) * 512:(i % 2) * 512 + 512]
            e = act(s, pg[:, :], ACT.Silu, tg, act_done.get(i - 2), *deps)
            put(bg, e)
            e = tt(s, s, pu[:, :], ALU.mult, e, tu)
            put(bu, e)
            half_done[i] = e
            hook(i)
            if lag == 2 and i == 0:
                continue
            if lag == 2 and i == 1:
                finish(0)
            finish(i)
            if i == n - 1:
                tail(tu)
            if 1 <= i < n - 1:
                down(i - 1)
                hook2(i)
        down(n - 2, n - 1)
        free_B[0] = pe_done[n - 1]
        return acc, y, tu

    def first_layer(l, x_toks):
        w = dr["w_in"][l]
        xn = T1[:, :].rearrange("p (t d) -> p t d", t=2)
        t_n = [(ln if t else ln_act)(x[:, t, :], xn[:, t, :], x_toks[t], free_T1[0]) for t in range(2)]
        mod_until(l, 1)
        mod_until(l, 0)
        h_t = to_H(xn, mod_cols(l, 1), mod_cols(l, 0), t_n, T2, mod_tok[(l, 0)], mod_tok[(l, 1)],
                   free_H[0], free_T2[0])
        h_toks = h_t[0] + h_t[1]

        Q.mark(f"A{l} proj")
        qd, kd = arena(0, 1536), arena(1536, 1536)
        qd3 = qd.rearrange("p (b s) -> p b s", s=S)
        kd3 = kd.rearrange("p (b s) -> p b s", s=S)
        vd = arena(3072, 1536).rearrange("p (t c) -> p t c", t=2)
        PT = arena(4608, 1536)
        qaT = arena(6144, 1024).rearrange("p (j s) -> p j s", j=4)
        kaT = arena(7168, 256)
        va = arena(7424, 256).rearrange("p (t c) -> p t c", t=2)
        ka = arena(7680, 256).rearrange("p (t c) -> p t c", t=2)
        qa = arena(4608, 1024).rearrange("p (t c) -> p t c", t=2)
        fa = free_AR[0]

        bs, ts_ = tok_proj512(w, 0, 8, H, [[h_t[t]] * 8 for t in range(2)])
        feed = mod_feed(l)
        next(feed, None)
        qa_t = []
        for t in range(2):
            tmp = T1[:, 512 * t:512 * t + 512].rearrange("p (h d) -> p h d", d=HD)
            dst = qa[:, t, :].rearrange("p (h d) -> p h d", d=HD)
            gq = row("qn", 64 * l, 64).unsqueeze(1).broadcast_to([P, 8, HD])
            tc_ = copy(qa[:, t, :].rearrange("p (j a d) -> p j a d", a=2, j=4),
                       bs[t][1][:, :].rearrange("p (a j d) -> p j a d", a=2, j=4), ts_[t], fa)
            put(bs[t][0], tc_)
            tq, _ = head_rms(dst, dst, gq, tmp, 8, tc_, h_toks)
            c = con("cos1")[:, 32 * t:32 * t + 32].unsqueeze(1).broadcast_to([P, 8, 32])
            s = con("sin1")[:, 32 * t:32 * t + 32].unsqueeze(1).broadcast_to([P, 8, 32])
            v = dst.rearrange("p h (i two) -> p h i two", two=2)
            t4 = [T1[:, 1024 + 256 * i:1280 + 256 * i].rearrange("p (h i) -> p h i", h=8) for i in range(4)]
            qa_t.append(rotate(v[:, :, :, 0], v[:, :, :, 1], v[:, :, :, 0], v[:, :, :, 1], c, s, t4, tq,
                               qa_t[-1] if qa_t else None))
        next(feed, None)
        b, ps, t_p = tok_proj(w, 512, H, h_toks)
        next(feed, None)
        p3 = ps[:, :].rearrange("p (t c) -> p t c", t=2)
        t1 = copy(ka, p3[:, :, 0:128], t_p, fa)
        t_va = copy(va, p3[:, :, 128:256], t_p, fa)
        put(b, [t1, t_va])
        kav = ka.rearrange("p t (h d) -> p (t h) d", d=HD)
        gk = row("kn", 64 * l, 64).unsqueeze(1).broadcast_to([P, 4, HD])
        tk, _ = head_rms(kav, kav, gk, T2[:, 0:256].rearrange("p (h d) -> p h d", d=HD), 4, t1, h_toks)
        for t in range(2):
            c = con("cos1")[:, 32 * t:32 * t + 32].unsqueeze(1).broadcast_to([P, 2, 32])
            s = con("sin1")[:, 32 * t:32 * t + 32].unsqueeze(1).broadcast_to([P, 2, 32])
            v = ka[:, t, :].rearrange("p (h i two) -> p h i two", h=2, two=2)
            t4 = [T2[:, 512 + 256 * t + 64 * i:576 + 256 * t + 64 * i].rearrange("p (h i) -> p h i", h=2)
                  for i in range(4)]
            tk = rotate(v[:, :, :, 0], v[:, :, :, 1], v[:, :, :, 0], v[:, :, :, 1], c, s, t4, tk)
        t_vd, t_qd, t_kd = [], [], []
        for i in range(3):
            b, ps, t_p = tok_proj(w, 2304 + S * i, H)
            e = copy(vd[:, :, S * i:S * i + S], ps[:, :].rearrange("p (t c) -> p t c", t=2), t_p, fa,
                     eng="dve" if i % 2 else "act")
            put(b, e)
            t_vd.append(e)
            next(feed, None)
        for dst, c0, lst in ((qd, 768, t_qd), (kd, 1536, t_kd)):
            for i in range(3):
                b, ps, t_p = T_proj(w, c0 + S * i, H)
                e = copy(dst[:, 512 * i:512 * i + 512], ps[:, :], t_p, fa, eng="dve" if i % 2 else "act")
                put(b, e)
                lst.append(e)
                next(feed, None)
        Q.mark(f"A{l} qkT")
        t_qa = []
        for jp in range(2):
            b, ps, free = take()
            last = None
            for j in range(2):
                for t in range(2):
                    jj = 2 * jp + j
                    v = qa[:, t, jj * P:(jj + 1) * P]
                    last = tr(ps[:, j * S + t * P:j * S + t * P + P], v, qa_t[t], free, sig=(j == 1 and t == 1))
            e = copy(qaT[:, 2 * jp:2 * jp + 2, :], ps[:, :].rearrange("p (j s) -> p j s", j=2), last, fa)
            put(b, e)
            t_qa.append(e)
        b, ps, free = take()
        for t in range(2):
            last = tr(ps[:, t * P:t * P + P], ka[:, t, :], tk, free, sig=(t == 1))
        t_ka = copy(kaT, ps[:, 0:S], last, fa)
        put(b, t_ka)

        G3 = G[:, :].rearrange("p (b s) -> p b s", s=S)
        g_tok = []
        for _ in feed:
            pass
        mod_g = [mod_run.get(0), mod_run.get(1)]

        def gates():
            for i in range(8):
                b, ps, t_p = T_proj(w, 3072 + S * i, H)
                e = copy(G3[:, 2 * i:2 * i + 2, :], ps[:, :].rearrange("p (b s) -> p b s", b=2), t_p, free_G[0], mod_g,
                         eng="dve" if i % 2 else "act")
                put(b, e)
                g_tok.append(e)
                free_H[0] = t_p
                next(feed, None)
                yield

        if l == 0:
            tok["alibi"] = dma("pool", "s_tab", T["TB"][:, 0:1536], dr["alibi"])
        t_al = tok["alibi"]
        al = T["TB"][:, 0:1536].rearrange("p (t g s) -> p t g s", t=2, g=3)
        bufs = [T1[:, 0:1536], T2[:, 0:1536]]
        state = {}
        pt_free = [[fa, t_qa]]
        al_used = []

        def dilated(j, i):
            Sb = bufs[i % 2].rearrange("p (t n) -> p t n", t=2)

            def s1():
                toks = []
                for g in range(3):
                    n = 4 * g + j
                    b, ps, free = take()
                    last = None
                    o = 64 * (n % 2)
                    for qt in range(2):
                        last = mm(ps[:, qt * S:(qt + 1) * S], qd3[o:o + 64, n // 2, qt * P:(qt + 1) * P],
                                  kd3[o:o + 64, n // 2, :], True, True, free, t_qd, t_kd, sig=(qt == 1))
                    slope = float(np.float32(2.0) ** np.float32(-8.0 * (n + 1) / 12))
                    a3 = al[:, :, g, :]
                    e = stt(Sb[:, :, g * S:(g + 1) * S], a3, -8.0 * slope,
                            ps[:, :].rearrange("p (t s) -> p t s", t=2), ALU.mult, ALU.add, last, t_al,
                            state.get(i - 2), qa_t, tk, h_toks)
                    put(b, e)
                    toks.append(e)
                al_used.append(toks[-1])
                state[("p", i)] = head_softmax(Sb, 768, 0.125, toks)[1]

            def s2():
                state[("t", i)], state[i] = probs_T(Sb, 3, PT, state[("p", i)], pt_free[0])

            def s3():
                r = pv(j, 3, PT, lambda g, kt: vd[:, kt, (4 * g + j) * HD:(4 * g + j + 1) * HD],
                       state[("t", i)], 4 + j // 2, t_vd)
                pt_free[0] = r

            return s1, s2, s3

        Q.mark(f"A{l} dilated")
        pipeline([dilated(j, j) for j in range(4)], gates(), per=2)
        free_TB[0] = al_used

        def globl(h, i):
            Sb = bufs[i % 2][:, 512 * (i // 2 % 3):512 * (i // 2 % 3) + 512].rearrange("p (t n) -> p t n", t=2)
            pt = PT[:, 512 * (i % 3):512 * (i % 3) + 512]

            def s1():
                b, ps, free = take()
                last = None
                o = 64 * (h // 4)
                for qt in range(2):
                    last = mm(ps[:, qt * S:(qt + 1) * S], qaT[o:o + 64, h % 4, qt * P:(qt + 1) * P],
                              kaT[o:o + 64, :], True, True, free, t_qa, t_ka, sig=(qt == 1))
                es, state[("p", i)] = head_softmax(Sb, S, 0.125, last, ps[:, :].rearrange("p (t s) -> p t s", t=2),
                                                   state.get(i - 2), state.get(i - 6))
                put(b, es)

            def s2():
                state[("t", i)], state[i] = probs_T(Sb, 1, pt, state[("p", i)], pt_free[0])

            def s3():
                pt_free[0] = pv(h, 1, pt, lambda g, kt: va[:, kt, 64 * (h // 4):64 * (h // 4) + 64],
                                state[("t", i)], h // 2, t_va)

            return s1, s2, s3

        pipeline([globl(h, 4 + h) for h in range(8)], feed)
        free_AR[0] = pt_free[0]

        Q.mark(f"A{l} merge")
        sg = [None] * 4
        for i in (2, 3, 0, 1):
            v = G[:, 1024 * i:1024 * (i + 1)]
            sg[i] = act(v, v, ACT.Sigmoid, g_tok)
        u = unit(dr["w_pb"][l].rearrange("(k p) c -> p k c", p=P), 2, D)
        last = None
        tb = []
        for m in range(4):
            b, ps, free = take()
            last = proj_T(u, B, 2, 2 * m, ps, free, B_tok[4], B_tok[5], k0=4)
            v = G[:, 2048 + 512 * m:2048 + 512 * m + 512]
            e = tt(v, v, ps[:, :], ALU.mult, last, sg[2 + m // 2])
            put(b, e)
            tb.append(e)
        done(u, last)
        m_toks = []
        for uu in range(2):
            u = unit(dr["w_pa"][l][:, uu * 512:uu * 512 + 512].rearrange("(k p) c -> p k c", p=P), 4, 512)
            for mm_ in range(2):
                m = 2 * uu + mm_
                b, ps, free = take()
                last = proj_T(u, B, 4, 2 * mm_, ps, free, [B_tok[i] for i in range(4)])
                v = G[:, 512 * m:512 * m + 512]
                vb = G[:, 2048 + 512 * m:2048 + 512 * m + 512]
                e = tt(v, v, ps[:, :], ALU.mult, last, sg[m // 2])
                put(b, e)
                e = tt(v, v, vb, ALU.add, e, tb[m], eng="pool")
                v3 = v.rearrange("p (k s) -> p k s", k=2)
                m_toks.append(split(H[0][:, 2 * m:2 * m + 2, :], H[1][:, 2 * m:2 * m + 2, :], v3, e, free_H[0]))
            done(u, last)
        free_B[0] = last
        B_tok.clear()
        Q.mark(f"A{l} wout")
        mod_until(l, 2)
        lg = dma("pool", "s_lng", G[:, 1024:2048], dr["ln1_g"][l].partition_broadcast(P), m_toks)
        lb = dma("pool", "s_lnb", G[:, 2048:3072], dr["ln1_b"][l].partition_broadcast(P), m_toks)
        ys = [[None, None], [None, None]]
        for c in range(2):
            bs, ts_ = tok_proj512(dr["w_out"][l], 512 * c, 8, H, [[m_toks[k // 2] for k in range(8)]] * 2, c == 1)
            if c == 0:
                gb = mod_bcast(l, 2, G[:, 0:1024], m_toks)
            for t in range(2):
                ys[t][c] = (bs[t][0], bs[t][1], ts_[t])
            free_H[0] = ts_[1]
        t_n = []
        x_toks = residual_ln(ys, G[:, 0:1024], G[:, 1024:2048], G[:, 2048:3072], gb, lg, lb,
                             lambda t: T1[:, 1024 * t:1024 * t + 1024], [state[11], state[10], state[9], state[8]],
                             lambda e: t_n.append(ln_act(x[:, 0, :], xn[:, 0, :], e)))
        free_G[0] = x_toks

        Q.mark(f"A{l} ln2+router")
        t_n.append(ln(x[:, 1, :], xn[:, 1, :], x_toks[1]))
        mod_until(l, 4)
        mod_until(l, 3)
        h_t = to_H(xn, mod_cols(l, 4), mod_cols(l, 3), t_n, T2, mod_tok[(l, 3)], mod_tok[(l, 4)], free_H[0],
                   [state[11], state[10]])
        h_toks = h_t[0] + h_t[1]
        t_rank, r_used = router_scores(h_toks)
        late = {}
        lg = dma("pool", "s_lng", T2[:, 0:1024], dr["ln2_g"][l].partition_broadcast(P), h_toks, r_used)
        lb = dma("pool", "s_lnb", T2[:, 1024:2048], dr["ln2_b"][l].partition_broadcast(P), h_toks, r_used)
        Q.mark(f"A{l} experts")
        CB = G[:, :].rearrange("p (e s) -> p e s", s=S)

        mod_phase(24 if l == 0 else 4, [AR[:, 2048 * i:2048 * i + 2048] for i in range(3)], free_AR[0])

        def hook(i):
            if i == 0:
                late["row"] = comb_rows(t_rank)
            if i == 1:
                late["comb"] = comb_bcast(late["row"])
            if l == 0 and i < 15:
                mod_step()
            if l == 1 and i < 4:
                mod_step()
            if i == 12:
                mod_until(l, 5)
                if l == 1:
                    mem_norm(0)
                late["g2"] = mod_bcast(l, 5, T1[:, 1024:2048], h_toks)

        acc, y, tu = ffn(NE,
                         lambda i: (w_unit8(dr["w_g"][l, i], 0), 8, S),
                         lambda i: (w_unit8(dr["w_u"][l, i], 0), 8, S),
                         lambda i: (dr["w_d"][l, i].rearrange("(k p) c -> p k c", p=P), 2, D),
                         lambda i: (CB[:, i, :], late["comb"]), h_toks, hook,
                         (lambda tok_: None) if l == 0 else (lambda tok_: mem_turn(0, tok_)), h_toks,
                         hook2=lambda i: mod_step() if l == 0 and 2 <= i <= 10 else None)
        Q.mark(f"A{l} end")
        g2 = late["g2"]
        free_H[0] = tu
        ys = [[(acc[2 * t + c][0], acc[2 * t + c][1], y[2 * t + c]) for c in range(2)] for t in range(2)]
        x_toks = residual_ln(ys, T1[:, 1024:2048], T2[:, 0:1024], T2[:, 1024:2048], g2, lg, lb,
                             lambda t: G[:, 1024 * t:1024 * t + 1024], None, lambda e: None)
        free_G[0] = x_toks
        free_T1[0] = x_toks
        free_T2[0] = x_toks
        return x_toks

    def mod_feed(l):
        for _ in range(12 if l == 0 else 0):
            mod_step()
            yield
        mod_step(0)
        mod_final()
        yield

    free_TB = [None]
    free_T1, free_T2, free_G, free_H, free_AR = [None], [None], [None], [None], [None]

    def residual_ln(ys, gate, lng, lnb, g_tok, lg_tok, lb_tok, tmp, deps, first):
        out = []
        for t in range(2):
            v = tmp(t)
            es = []
            for c in range(2):
                b, ps, ty = ys[t][c]
                e = tt(v[:, 512 * c:512 * c + 512], ps[:, :], gate[:, 512 * c:512 * c + 512], ALU.mult, ty,
                       g_tok, deps)
                put(b, e)
                es.append(e)
            e = stt(x[:, t, :], x[:, t, :], ALPHA, v, ALU.mult, ALU.add, es)
            sb = small(12)
            for hh in range(2):
                e1 = op("dve", lambda e_, hh=hh, sb=sb, xv=x[:, t, :]: e_.bn_stats(
                    sb[:, 6 * hh:6 * hh + 6], xv[:, 512 * hh:512 * hh + 512]), e)
            mv = small(2)
            e1 = op("dve", lambda e_, sb=sb, mv=mv: e_.bn_aggr(mv, sb), e1)
            r = rsqrt(mv[:, 1:2], 1, 1.0, LN_EPS, e1)
            e = stt(v, x[:, t, :], mv[:, 0:1], lng, ALU.subtract, ALU.mult, e1, lg_tok)
            e = stt(x[:, t, :], v, mv[:, 1:2], lnb, ALU.mult, ALU.add, e, r, lb_tok)
            out.append(e)
            if t == 0:
                first(e)
        resume()
        return out

    def router_scores(h_toks):
        Hf = T2[:, :].rearrange("p (k s) -> p k s", k=8)
        b, ps, free = take()
        last = None
        for t in range(2):
            for k in range(8):
                last = mm(ps[:, 16 * t:16 * t + 16], Hf[:, k, t * P:(t + 1) * P],
                          col("router", 16 * k, 16), k == 0, k == 7, h_toks, free, sig=(t == 1 and k == 7))
        R = T["R"]

        def r(a, n):
            return R[:, a:a + n]

        sc, sel = r(0, 32), r(32, 32)
        r_used = last
        e = act(sc, ps[:, 0:32], ACT.Sigmoid, last)
        put(b, e)
        rb = row("rb", 0, 16).unsqueeze(1).broadcast_to([P, 2, 16])
        e_sc = e
        e = tt(sel.rearrange("p (t e) -> p t e", t=2), sc.rearrange("p (t e) -> p t e", t=2), rb, ALU.add, e,
               tok["rows"])
        s4 = sel.rearrange("p (g e) -> p g e", e=4)
        rank, cmp_ = r(64, 32), r(96, 32)
        rk4, c4 = rank.rearrange("p (g e) -> p g e", e=4), cmp_.rearrange("p (g e) -> p g e", e=4)
        e = op("dve", lambda e_: e_.memset(rank, 0.0), e)
        pr = r(128, 8 * 6)
        n = 0
        ps_t = []
        for a in range(4):
            for b_ in range(a + 1, 4):
                sa, sb = s4[:, :, a:a + 1], s4[:, :, b_:b_ + 1]
                ps_t.append(tt(pr[:, 8 * n:8 * n + 8].unsqueeze(2), sa, sb, ALU.add, e))
                e = tt(c4[:, :, 0:1], sb, sa, ALU.is_gt, e)
                e = tt(rk4[:, :, a:a + 1], rk4[:, :, a:a + 1], c4[:, :, 0:1], ALU.add, e)
                e = tt(c4[:, :, 1:2], sa, sb, ALU.is_ge, e)
                e = tt(rk4[:, :, b_:b_ + 1], rk4[:, :, b_:b_ + 1], c4[:, :, 1:2], ALU.add, e)
                n += 1
        gs = r(176, 8)
        e = red(gs, pr.rearrange("p (n g) -> p g n", n=6), ALU.max, ps_t, e)
        g4 = gs.rearrange("p (t g) -> p t g", g=4)
        gr = r(184, 8)
        gr4 = gr.rearrange("p (t g) -> p t g", g=4)
        e = op("dve", lambda e_: e_.memset(gr, 0.0), e)
        c2 = cmp_.rearrange("p (t g) -> p t g", t=2)
        for a in range(4):
            for b_ in range(a + 1, 4):
                e = tt(c2[:, :, 0:1], g4[:, :, b_:b_ + 1], g4[:, :, a:a + 1], ALU.is_gt, e)
                e = tt(gr4[:, :, a:a + 1], gr4[:, :, a:a + 1], c2[:, :, 0:1], ALU.add, e)
                e = tt(c2[:, :, 1:2], g4[:, :, a:a + 1], g4[:, :, b_:b_ + 1], ALU.is_ge, e)
                e = tt(gr4[:, :, b_:b_ + 1], gr4[:, :, b_:b_ + 1], c2[:, :, 1:2], ALU.add, e)
        e = ts(gr, gr, 0.5, None, ALU.is_lt, None, e)
        e = ts(rank, rank, 1.5, None, ALU.is_lt, None, e)
        e = tt(rk4, rk4, gr.unsqueeze(2).broadcast_to([P, 8, 4]), ALU.mult, e)
        e = tt(rank, rank, sc, ALU.mult, e)
        tot = r(192, 2)
        e = red(tot, rank.rearrange("p (t e) -> p t e", t=2), ALU.add, e)
        e = op("dve", lambda e_: e_.reciprocal(tot, tot), e)
        e = tt(rank.rearrange("p (t e) -> p t e", t=2), rank.rearrange("p (t e) -> p t e", t=2),
               tot.unsqueeze(2).broadcast_to([P, 2, 16]), ALU.mult, e)
        return e, r_used

    def comb_rows(e):
        rank = T["R"][:, 64:96]
        b, ps, free = take()
        for t in range(2):
            last = op("pe", lambda e_, t=t, ps=ps: e_.transpose(ps[0:16, t * P:(t + 1) * P], rank[:, 16 * t:16 * t + 16], ident),
                      e, free)
        e = copy(T["crow"][0:16, :], ps[0:16, 0:S], last)
        put(b, e)
        return e

    def comb_bcast(e):
        outs = []
        for m in range(8):
            b, ps, free = take()
            for j in range(2):
                k = 2 * m + j
                last = mm(ps[:, j * S:(j + 1) * S], ident[0:16, k:k + 1].broadcast_to([16, P]),
                          T["crow"][0:16, :], True, True, e, free, sig=(j == 1))
            c = copy(G[:, 512 * m:512 * m + 512], ps[:, :], last, free_G[0], eng="act" if m % 2 else "dve")
            put(b, c)
            outs.append(c)
        return outs

    mem_state = {}

    def mem_norm(l):
        mn = AR[:, 0:2048].rearrange("p (t d) -> p t d", t=2)
        where = AR[:, 6144:8192] if l == 0 else G[:, 0:2048]
        where = where.rearrange("p (t d) -> p t d", t=2)
        t_m = dma("sp", "s_mem", where, dr["mem"].rearrange("(t p) d -> p t d", p=P), free_AR[0], free_G[0],
                  mod_run.get(0), mod_run.get(1))
        t_n = []
        for t in range(2):
            t_n.append(rms(where[:, t, :], mn[:, t, :], AR[:, 4096 + 1024 * t:5120 + 1024 * t], t_m, free_AR[0],
                           mod_run.get(0), mod_run.get(1)))
        if l:
            free_G[0] = [free_G[0], t_n]
        mem_state["n"] = t_n

    def mem_turn(l, last_H):
        mn = AR[:, 0:2048].rearrange("p (t d) -> p t d", t=2)
        mem_state["h"] = to_H(mn, col("mem_g", 8 * l, 8), None, mem_state["n"], AR[:, 2048:4096], last_H,
                              tok["cols"])

    gam = T["gam"]

    def decays():
        z, a, u, w, d, r_, m = (T["R"][:, 16 * i:16 * i + 16] for i in range(7))
        src = row("dec", 0, 16)
        e = ts(z, src, -1.0, None, ALU.mult, None, tok["rows"])
        e = tt(a, z, src, ALU.min, e)
        e = act(u, a, ACT.Exp, e)
        e1 = ts(w, u, 1.0, None, ALU.add, None, e)
        e2 = act(m, w, ACT.Ln, e1)
        e = ts(d, w, -1.0, None, ALU.add, None, e1)
        e = ts(r_, d, 1e-30, None, ALU.max, None, e)
        e = op("dve", lambda e_: e_.reciprocal(r_, r_), e)
        e = tt(r_, r_, u, ALU.mult, e)
        e = tt(r_, r_, m, ALU.mult, e, e2)
        e = stt(m, d, 0.0, u, ALU.is_equal, ALU.mult, e)
        e = tt(r_, r_, m, ALU.add, e)
        e = ts(a, src, 0.0, None, ALU.min, None, e)
        return tt(gam[:, :], a, r_, ALU.subtract, e)

    def to_T(src, dst, toks, *deps):
        b, ps, free = take()
        last = None
        for blk in range(2):
            for t in range(2):
                last = tr(ps[:, blk * S + t * P:blk * S + t * P + P], src[:, t, blk * P:(blk + 1) * P], toks, free,
                          sig=(blk == 1 and t == 1))
        if dst is None:
            return b, ps, last
        e = copy(dst, ps[:, :], last, *deps)
        put(b, e)
        return e

    def second_layer(l, x_toks, t_gam):
        w = dr["w_in2"][l]
        xn = T1[:, :].rearrange("p (t d) -> p t d", t=2)

        def t2(a):
            return arena(a * 512, 512)

        fa = free_AR[0]
        tiles = {}
        names = ["rq", "rk", "rv", "rg", "rqT", "rkT", "pv", "nq", "nk", "nv", "nqT", "nkT", "mq", "mqT",
                 "mk", "mkT", "mv"]
        for i, n in enumerate(names):
            tiles[n] = t2(i)

        def v3(n):
            return tiles[n].rearrange("p (t c) -> p t c", t=2)

        def vh(ap):
            return ap.rearrange("p (h d) -> p h d", d=HD)

        t_nab = dma("pool", "s_tab", T["TB"][:, :], dr["na_b"][:, l].rearrange("p t h s -> p (t h s)"), free_TB[0])
        ms = dict(mem_state)
        t_dec = dma("sp", "s_dec", G[:, 0:1024], dr["decay_m"], free_G[0])
        t_pm = dma("sp", "s_pm", G[:, 2048:4096], dr["pool_m"], free_G[0])
        Q.mark(f"B{l} x")
        t_n = [rms(x[:, t, :], xn[:, t, :], T2[:, 1024 * t:1024 * t + 1024], x_toks[t], free_T1[0], free_T2[0],
                   dve=t == 1) for t in range(2)]
        (bk, pk, tk), (bv, pvs, tv) = tok_proj_two(dr["w_kv"][l], (0, S), H, ms["h"])
        t_mem = ms["h"][0] + ms["h"][1]
        h_t = to_H(xn, col("mix_g", 8 * l, 8), None, t_n, T2, tv, t_n)
        h2 = h_t[0] + h_t[1]
        fa = [fa, t_mem, ms["n"]]

        hr_last = [None]

        def hr(src_ps, name, g, t_in):
            t, ts_ = head_rms(vh(src_ps), vh(tiles[name]), row(g, 64 * l, 64).unsqueeze(1).broadcast_to([P, 8, HD]),
                              vh(T1[:, 512:1024]), 8, t_in, fa, h2, hr_last[0])
            hr_last[0] = ts_
            return t, ts_

        Q.mark(f"B{l} proj")
        t_mk, t_s = hr(pk[:, :], "mk", "mk", tk)
        put(bk, t_s)
        t_mv = copy(tiles["mv"], pvs[:, :], tv, fa)
        put(bv, t_mv)

        (b, ps, t_p), rq_p = tok_proj_two(w, (3 * S, 0), H, h_t)
        t_rg = act(tiles["rg"], ps[:, :], ACT.Silu, t_p, fa)
        put(b, t_rg)
        rot = {}
        prev = None
        for n, name in enumerate(("rq", "rk")):
            b, ps, t_p = rq_p if n == 0 else tok_proj(w, n * S, H)
            e = copy(tiles[name], ps[:, :], t_p, fa)
            put(b, e)
            for t in range(2):
                c = con("cos2")[:, 32 * t:32 * t + 32].unsqueeze(1).broadcast_to([P, 4, 32])
                s = con("sin2")[:, 32 * t:32 * t + 32].unsqueeze(1).broadcast_to([P, 4, 32])
                v = v3(name)[:, t, :].rearrange("p (h two i) -> p h two i", two=2, i=32)
                t4 = [T1[:, 1024 + 128 * i:1152 + 128 * i].rearrange("p (h i) -> p h i", h=4) for i in range(4)]
                prev = rotate(v[:, :, 0, :], v[:, :, 1, :], v[:, :, 0, :], v[:, :, 1, :], c, s, t4, e, prev, h2)
            rot[name] = prev
        b, ps, t_p = tok_proj(w, 2 * S, H)
        t_rv = copy(tiles["rv"], ps[:, :], t_p, fa, eng="dve")
        put(b, t_rv)
        DT = T2
        t_D = []
        for h in range(4):
            o = DT[:, 512 * h:512 * h + 512]
            a_, b_ = G[:, 0:512], G[:, 512:1024]
            e = ts(o, a_, gam[:, 4 * l + h:4 * l + h + 1], None, ALU.mult, None, t_dec, t_gam, h2)
            e = stt(o, b_, gam[:, 8 + 4 * l + h:8 + 4 * l + h + 1], o, ALU.mult, ALU.add, e)
            e_dec = e
            t_D.append(act(o, o, ACT.Exp, e))
        b, ps, t_p = tok_proj(w, 4 * S, H)
        t_pv = copy(tiles["pv"], ps[:, :], t_p, fa)
        put(b, t_pv)
        t_rq = to_T(v3("rq"), tiles["rqT"], rot["rq"], fa)
        t_rk = to_T(v3("rk"), tiles["rkT"], rot["rk"], fa)

        qt_tok = {}

        def nh(name, c0, g):
            b, ps, t_p = tok_proj(w, c0, H)
            qt_tok[name], t_s = hr(ps[:, :], name, g, t_p)
            put(b, t_s)

        nh("nq", 5 * S, "naq")
        rqT = tiles["rqT"].rearrange("p (b s) -> p b s", b=2)
        rkT = tiles["rkT"].rearrange("p (b s) -> p b s", b=2)
        bo, po, fo = take()
        t_sd = {}
        t_ret = {}

        def ret_s(h):
            b, ps, free = take()
            o = 64 * (h % 2)
            last = None
            for kt in range(2):
                last = mm(ps[:, kt * S:(kt + 1) * S], rkT[o:o + 64, h // 2, kt * P:(kt + 1) * P],
                          rqT[o:o + 64, h // 2, :], True, True, t_rq, t_rk, free, sig=(kt == 1))
            d = DT[:, 512 * h:512 * h + 512]
            t_sd[h] = stt(d, ps[:, :], 0.125, d, ALU.mult, ALU.mult, last, t_D[h])
            put(b, t_sd[h])

        def ret_o(h):
            for qt in range(2):
                for kt in range(2):
                    o = qt * S + h * HD
                    t_ret[h] = mm(po[:, o:o + HD],
                                  DT[:, 512 * h + kt * S + qt * P:512 * h + kt * S + qt * P + P],
                                  v3("rv")[:, kt, h * HD:(h + 1) * HD], kt == 0, kt == 1, t_sd[h], t_rv, fo,
                                  sig=(kt == 1 and qt == 1))

        ret_s(0)
        ret_s(1)
        nh("nk", 6 * S, "nak")
        ret_o(0)
        ret_s(2)
        ret_o(1)
        ret_s(3)
        b, ps, t_p = tok_proj(w, 7 * S, H)
        t_nv = copy(tiles["nv"], ps[:, :], t_p, fa, eng="dve")
        put(b, t_nv)
        ret_o(2)
        ret_o(3)
        ret_all = list(t_ret.values())
        rt = tiles["rq"]
        tmp = vh(T1[:, 512:1024])
        t0 = act(tmp, vh(po[:, :]), ACT.Square, ret_all, hr_last[0])
        ss = small(8)
        t = red(ss, tmp, ALU.add, t0)
        hr_last[0] = t
        t = rsqrt(ss, 8, 1.0 / HD, RMS_EPS, t)
        t = tt(vh(rt), vh(po[:, :]), ss.unsqueeze(2).broadcast_to([P, 8, HD]), ALU.mult, t, t_rq)
        put(bo, t)
        r3 = rt.rearrange("p (t c) -> p t c", t=2)
        t = tt(r3, r3, row("ret", S * l, S).unsqueeze(1).broadcast_to([P, 2, S]), ALU.mult, t, eng="pool")
        t_r = tt(rt, rt, tiles["rg"], ALU.mult, t, t_rg, eng="pool")
        nh("mq", 8 * S, "mq")
        t_nq = to_T(v3("nq"), tiles["nqT"], qt_tok["nq"], fa)
        t_nk = to_T(v3("nk"), tiles["nkT"], qt_tok["nk"], fa)
        t_mkT = to_T(v3("mk"), tiles["mkT"], t_mk, fa)

        Q.mark(f"B{l} pool")
        pm = G[:, 2048:4096].rearrange("p (a s) -> p a s", s=S)
        b, ps, free = take()
        last = None
        for g in range(4):
            for kt in range(2):
                last = mm(ps[64 * (g % 2):64 * (g % 2) + 64, (g // 2) * S:(g // 2) * S + S],
                          v3("pv")[:, kt, g * HD:(g + 1) * HD], pm[:, 4 * kt + g, :],
                          kt == 0, kt == 1, t_pm, t_pv, free, sig=(g == 3 and kt == 1))
        free_G[0] = [last, e_dec]
        pl = tiles["rk"]
        t = copy(pl, ps[:, :], last, t_rk)
        put(b, t)
        b, ps, free = take()
        for g in range(4):
            o = 64 * (g % 2)
            a = 128 * l + 64 * (g // 2)
            c0 = COLS["pool_w"][0] + a
            last = mm(ps[o:o + 64, (g // 2) * S:(g // 2) * S + S], T["cols"][o:o + 64, c0:c0 + 64],
                      pl[o:o + 64, (g // 2) * S:(g // 2) * S + S], True, True, t, free, sig=(g == 3))
        es = []
        for j in range(2):
            s_ = col("pool_s", 2 * l + j, 1)
            es.append(ts(pl[:, j * S:(j + 1) * S], ps[:, j * S:(j + 1) * S], s_, None, ALU.mult, None, last))
        put(b, es)
        t_b = split(B[0][:, 2:4, :], B[1][:, 2:4, :], pl.rearrange("p (b s) -> p b s", b=2), es, free_B[0])
        br_tok = {1: t_b}
        b, ps, t = to_T(r3, None, t_r)
        t1 = act(B[0][:, 0:2, :], ps[:, :].rearrange("p (b s) -> p b s", b=2), ACT.Copy, t, free_B[0])
        t2_ = tt(B[1][:, 0:2, :], ps[:, :].rearrange("p (b s) -> p b s", b=2), B[0][:, 0:2, :].bitcast(F32),
                 ALU.subtract, t1)
        put(b, [t1, t2_])
        br_tok[0] = [t1, t2_]
        t_mq = to_T(v3("mq"), tiles["mqT"], qt_tok["mq"], fa)

        Q.mark(f"B{l} heads")
        bias = T["TB"][:, :].rearrange("p (a s) -> p a s", s=S)
        t_bias = tt(bias, bias, con("mask").unsqueeze(1).broadcast_to([P, 8, S]), ALU.add, t_nab)
        b_used = []
        state = {}
        G3 = G[:, :].rearrange("p (b s) -> p b s", s=S)
        g_tok = {}
        wg = dr["w_gate"][l]
        order = [1, 0, 2, 3]

        def gate_units(n, slot, func):
            g_tok[n] = []
            for i in range(4):
                b, ps, t_p = T_proj(wg, n * D + S * i, H)
                o = G3[:, 8 * slot + 2 * i:8 * slot + 2 * i + 2, :]
                e = act(o, ps[:, :].rearrange("p (b s) -> p b s", b=2), func, t_p, free_G[0], g_used.get(slot))
                put(b, e)
                g_tok[n].append(e)
                free_H[0] = t_p
                yield

        g_used = {}

        def filler():
            for n, slot in ((1, 0), (0, 1)):
                for _ in gate_units(n, slot, ACT.Copy):
                    yield

        pt_free = [ret_all]

        def head(kind, h, i):
            Sb = T1[:, 512 * (i % 4):512 * (i % 4) + 512].rearrange("p (t n) -> p t n", t=2)
            pt = T2[:, 512 * (i % 4):512 * (i % 4) + 512]
            qT, kT, v = (tiles[n] for n in (("nqT", "nkT", "nv") if kind == "n" else ("mqT", "mkT", "mv")))
            tq, tk_, tv_ = (t_nq, t_nk, t_nv) if kind == "n" else (t_mq, t_mkT, t_mv)
            o = 64 * (h % 2)
            blk = h // 2

            def s1():
                b, ps, free = take()
                last = None
                for qt in range(2):
                    last = mm(ps[:, qt * S:(qt + 1) * S], qT[o:o + 64, blk * S + qt * P:blk * S + (qt + 1) * P],
                              kT[o:o + 64, blk * S:(blk + 1) * S], True, True, free, tq, tk_, sig=(qt == 1))
                p3 = ps[:, :].rearrange("p (t s) -> p t s", t=2)
                if kind == "n":
                    b4 = bias.rearrange("p (t h) s -> p t h s", h=4)[:, :, h, :]
                    e = stt(Sb, p3, 0.125, b4, ALU.mult, ALU.add, last, t_bias, state.get(i - 4), t_r, t0,
                            qt_tok["mq"])
                    b_used.append(e)
                    put(b, e)
                    state[("p", i)] = head_softmax(Sb, S, 1.0, e)[1]
                else:
                    es, state[("p", i)] = head_softmax(Sb, S, 0.125, last, p3, state.get(i - 4))
                    put(b, es)
                if kind == "n" and h == 3:
                    free_TB[0] = b_used

            def s2():
                state[("t", i)], state[i] = probs_T(Sb, 1, pt, state[("p", i)], pt_free[0])

            def s3():
                pt_free[0] = pv(h, 1, pt, lambda g, kt: v.rearrange("p (t c) -> p t c", t=2)[:, kt, h * HD:(h + 1) * HD],
                                state[("t", i)], (4 if kind == "n" else 6) + h // 2, tv_)

            return s1, s2, s3

        pipeline([head("n", h, h) for h in range(4)] + [head("m", h, 4 + h) for h in range(4)], filler())
        br_tok[2] = [B_tok[4], B_tok[5]]
        br_tok[3] = [B_tok[6], B_tok[7]]
        free_AR[0] = pt_free[0]

        Q.mark(f"B{l} up")
        for n, slot in ((1, 0), (0, 1)):
            v = G[:, 2048 * slot:2048 * slot + 2048]
            for hh in range(2):
                vv = v[:, 1024 * hh:1024 * hh + 1024]
                g_tok[n].append(act(vv, vv, ACT.Sigmoid, g_tok[n][0:4]))
        m_toks = []
        s_done = [state[7], state[6], state[5], state[4]]
        prev = {}
        for z, n in enumerate(order):
            slot = z % 2
            if z >= 2:
                for _ in gate_units(n, slot, ACT.Sigmoid):
                    pass
            u = unit(dr["w_br"][l, n].rearrange("(k p) c -> p k c", p=P), 2, D)
            used = []
            for m in range(4):
                b, ps, free = take()
                last = proj_T(u, B, 2, 2 * m, ps, free, br_tok[n], k0=2 * n)
                gv = G[:, 2048 * slot + 512 * m:2048 * slot + 512 * m + 512]
                tv_ = T1[:, 512 * m:512 * m + 512]
                if z == 0:
                    e = tt(tv_, gv, ps[:, :], ALU.mult, last, g_tok[n], s_done)
                    put(b, e)
                else:
                    e = tt(gv, gv, ps[:, :], ALU.mult, last, g_tok[n])
                    put(b, e)
                    e = tt(tv_, tv_, gv, ALU.add, e, prev[m], eng="pool" if m % 2 else "dve")
                prev[m] = e
                used.append(e)
                if z == 3:
                    m_toks.append(split(H[0][:, 2 * m:2 * m + 2, :], H[1][:, 2 * m:2 * m + 2, :],
                                        tv_.rearrange("p (k s) -> p k s", k=2), e, free_H[0]))
            done(u, last)
            g_used[slot] = used
        free_G[0] = [g_used[0], g_used[1]]
        free_B[0] = last
        B_tok.clear()
        Q.mark(f"B{l} wout")
        x_t = [None, None]
        xs = [[], []]
        for c in range(2):
            bs, ts_ = tok_proj512(dr["w_out2"][l], 512 * c, 8, H, [[m_toks[k // 2] for k in range(8)]] * 2, c == 1)
            for t in range(2):
                xv = x[:, t, 512 * c:512 * c + 512]
                e = tt(xv, xv, bs[t][1][:, :], ALU.add, ts_[t], t_n)
                put(bs[t][0], e)
                xs[t].append(e)
            free_H[0] = ts_[1]
        t_n = [rms(x[:, t, :], xn[:, t, :], T2[:, 1024 * t:1024 * t + 1024], xs[t], m_toks, pt_free[0], dve=t == 1)
               for t in range(2)]
        resume()
        h3 = to_H(xn, col("ffn_g", 8 * l, 8), None, t_n, T2, free_H[0], t_n)
        h3 = h3[0] + h3[1]
        Q.mark(f"B{l} ffn")
        wf, wd = dr["w_ff1"][l], dr["w_ff2"][l]
        acc, y, tu = ffn(11, lambda i: (w_unit8(wf, S * i), 8, S),
                         lambda i: (w_unit8(wf, FF + S * i), 8, S),
                         lambda i: (wd[S * i:S * i + S, :].rearrange("(k p) c -> p k c", p=P), 2, D),
                         None, h3, lambda i: mem_norm(1) if l == 0 and i == 6 else None,
                         (lambda tok_: mem_turn(1, tok_)) if l == 0 else (lambda tok_: None), h3)
        Q.mark(f"B{l} end")
        free_H[0] = tu
        out = [[], []]
        for t in range(2):
            for c in range(2):
                xv = x[:, t, 512 * c:512 * c + 512]
                b, ps, _ = acc[2 * t + c]
                e = tt(xv, xv, ps[:, :], ALU.add, y[2 * t + c])
                put(b, e)
                out[t].append(e)
        resume()
        free_T1[0] = [y, h3]
        free_T2[0] = h3
        return out

    mod_phase(8, [AR[:, 2048 * i:2048 * i + 2048] for i in range(3)] + [G[:, 0:2048], G[:, 2048:4096]])
    mod_until(0, 1)
    mod_until(0, 0)
    free_AR[0] = [mod_run.get(0), mod_run.get(1)]
    mod_phase(12, [G[:, 0:2048], G[:, 2048:4096]], free_AR[0])
    t_gam = decays()
    xt = [tok["x"], tok["x"]]
    for l in range(L):
        xt = first_layer(l, xt)
    for l in range(L):
        xt = second_layer(l, xt, t_gam)
    t_out = []
    for t in range(2):
        dma("sp", "s_out", dr["out"][t * P:(t + 1) * P, :], x[:, t, :], xt[t])
    Q.wait("sp", [("s_out", 32)])
    return Q


def build(nc, dr):
    ctx = ExitStack()
    with ctx:
        def sb(name, shape, dt=F32):
            return ctx.enter_context(nc.sbuf_tensor(name, shape, dt))

        T = {
            "raw": [sb(f"raw{i}", [P, 2048]) for i in range(NRAW)],
            "whi": [sb(f"whi{i}", [P, 2048], F32R) for i in range(NSPL)],
            "wlo": [sb(f"wlo{i}", [P, 2048], F32R) for i in range(NSPL)],
            "Hh": sb("Hh", [P, 8, S], F32R), "Hl": sb("Hl", [P, 8, S], F32R),
            "Bh": sb("Bh", [P, 8, S], F32R), "Bl": sb("Bl", [P, 8, S], F32R),
            "x": sb("xs", [P, 2, D]), "T1": sb("T1", [P, 2048]), "T2": sb("T2", [P, 2048]),
            "G": sb("G", [P, 4096]), "AR": sb("AR", [P, 8960]),
            "cons": sb("cons_s", [P, N_CONS]), "cols": sb("cols_s", [P, N_COLS]), "rows": sb("rows_s", [P, N_ROWS]),
            "csil": sb("csil", [P, 8]), "modT": sb("modT", [P, 96]), "crow": sb("crow", [16, S]), "TB": sb("TB", [P, 2048]), "R": sb("R", [P, 200]), "gam": sb("gam", [P, 16]),
            "small": sb("small", [P, 200]), "ones": sb("ones", [P, 2]), "mhalf": sb("mhalf", [P, 8]),
            "ps": [ctx.enter_context(nc.psum_tensor(f"ps{i}", [P, 512], F32)) for i in range(8)],
        }
        units = []
        plan(nc, T, dr, units, False)
        Q = plan(nc, T, dr, units, True)
        sems = {}
        for name in sorted({s for q in Q.q.values() for it in q if it[0] == "op" and it[2] for s in [it[2][0]]}):
            sems[name] = ctx.enter_context(nc.semaphore("c_" + name))

        def emit(eng, e):
            for it in Q.q[eng]:
                if it[0] == "wait":
                    e.wait_ge(sems[it[1]], it[2])
                else:
                    ins = it[1](e)
                    if it[2]:
                        ins.then_inc(sems[it[2][0]], it[2][1])

        block = ctx.enter_context(nc.Block())

        @block.sync
        def _(e):
            emit("sp", e)

        @block.gpsimd
        def _(e):
            emit("pool", e)

        @block.scalar
        def _(e):
            emit("act", e)

        @block.tensor
        def _(e):
            emit("pe", e)

        @block.vector
        def _(e):
            emit("dve", e)


def kernel(**inp):
    import concourse.bacc as bacc
    from concourse.bass_utils import run_bass_kernel_spmd

    a = {k: np.ascontiguousarray(np.asarray(v)) for k, v in inp.items()}

    def columns(v):
        return v.reshape(-1, P).T

    pw = a["pool_w_2"].reshape(L, 2, 2, HD, HD).transpose(2, 3, 0, 1, 4).reshape(P, -1)
    router = a["w_router"].reshape(8, P, NE).transpose(1, 0, 2).reshape(P, -1)
    cols = np.concatenate([columns(a["c"]), columns(a["b_ada"]), columns(a["norm_mix_g_2"]),
                           columns(a["norm_mem_g_2"]), columns(a["norm_ffn_g_2"]), columns(a["pool_scale_2"]),
                           router, pw], 1)
    rows = np.concatenate([a[n].reshape(-1) for n in (
        "q_norm_g", "k_norm_g", "na_q_norm_g_2", "na_k_norm_g_2", "mem_q_norm_g_2", "mem_k_norm_g_2",
        "ret_norm_g_2", "router_bias", "ret_decay_fwd_2", "ret_decay_bwd_2")])
    t = np.arange(S)
    r_off = (t[None, :] // 64 - t[:, None] // 64) + 7
    c_off = np.clip(t[None, :] % 64 - t[:, None] % 64, -15, 15) + 15
    na = a["na_rpb_2"][:, :, r_off, c_off]
    na = na.reshape(L, 4, 2, P, S).transpose(3, 0, 2, 1, 4)

    arrays = {
        "x": a["x"][0], "mem": a["mem_2"][0], "cols": cols, "rows": rows, "na_b": na,
        "w_ada": a["w_ada"], "w_in": a["w_in"], "w_pa": a["w_branch_a"], "w_pb": a["w_branch_b"],
        "w_out": a["w_out"], "ln1_g": a["ln1_g"], "ln1_b": a["ln1_b"], "ln2_g": a["ln2_g"], "ln2_b": a["ln2_b"],
        "w_g": a["w_exp_gate"], "w_u": a["w_exp_up"], "w_d": a["w_exp_down"],
        "w_in2": a["w_in_2"], "w_gate": a["w_gate_2"], "w_kv": a["w_mem_kv_2"], "w_br": a["w_branch_2"],
        "w_out2": a["w_out_2"], "w_ff1": a["w_ffn_in_2"], "w_ff2": a["w_ffn_out_2"],
    }
    arrays.update(shape_constants())
    nc = bacc.Bacc("TRN2", target_bir_lowering=False, num_devices=1)
    feed, dr = {}, {}
    for k, v in arrays.items():
        v = np.ascontiguousarray(v)
        feed["in_" + k] = v
        dr[k] = nc.dram_tensor("in_" + k, v.shape, F32, kind="ExternalInput").ap()
    dr["out"] = nc.dram_tensor("out_0", (S, D), F32, kind="ExternalOutput").ap()
    build(nc, dr)
    r = run_bass_kernel_spmd(nc, [feed], core_ids=[0])
    return r.results[0]["out_0"].reshape(1, S, D)
```

```python
import math
from collections import deque
from contextlib import ExitStack

import numpy as np
import concourse.bass as bass
from concourse import mybir

F32 = mybir.dt.float32
F32R = mybir.dt.float32r
ALU = mybir.AluOpType
ACT = mybir.ActivationFunctionType
AX = mybir.AxisListType

P = 128
D = 1024
S = 256
HD = 64
L = 2
NE = 16
FF = 2816
ALPHA = (2.0 * L) ** 0.25
LN_EPS = 1e-5
RMS_EPS = 1e-6
W_IN1 = 5120
NRAW = 4
NSPL = 3

COLS = {}
ROWS = {}
CONS = {}


def _spans(table, items):
    at = 0
    for name, n in items:
        table[name] = (at, at + n)
        at += n
    return at


N_COLS = _spans(COLS, [("c", 8), ("b_ada", 96), ("mix_g", 16), ("mem_g", 16), ("ffn_g", 16),
                       ("pool_s", 4), ("router", 128), ("pool_w", 256)])
N_ROWS = _spans(ROWS, [("qn", 128), ("kn", 128), ("naq", 128), ("nak", 128), ("mq", 128), ("mk", 128),
                       ("ret", 512), ("rb", 16), ("dec", 16)])
N_CONS = _spans(CONS, [("ident", 128), ("cos1", 64), ("sin1", 64), ("cos2", 64), ("sin2", 64),
                       ("mask", 256)])


def shape_constants():
    f = np.float32
    t = np.arange(S)
    cons = np.zeros((P, N_CONS), f)

    def put(name, a):
        cons[:, CONS[name][0]:CONS[name][1]] = a

    def tiles(a):
        return a.reshape(2, P, -1).transpose(1, 0, 2).reshape(P, -1)

    put("ident", np.eye(P, dtype=f))
    inv = (f(10000.0) ** (-np.arange(0, 32, 2, dtype=f) / f(32))).astype(f)
    row, col = (t // 64).astype(f), (t % 64).astype(f)
    ang = np.concatenate([row[:, None] * inv, col[:, None] * inv], -1).astype(f)
    put("cos1", tiles(np.cos(ang)))
    put("sin1", tiles(np.sin(ang)))
    inv = (f(10000.0) ** (-np.arange(32, dtype=f) / f(32))).astype(f)
    ang = (t.astype(f)[:, None] * inv[None, :]).astype(f)
    put("cos2", tiles(np.cos(ang)))
    put("sin2", tiles(np.sin(ang)))
    qc, kc = np.arange(P) % 64, t % 64
    win = np.clip(qc - 8, 0, 48)
    ok = (kc[None, :] >= win[:, None]) & (kc[None, :] < win[:, None] + 16)
    put("mask", np.where(ok, f(0), f(-1e30)))

    dist = np.abs(t[:, None] - t[None, :])
    alibi = np.zeros((S, 3, S), f)
    for g, dil in enumerate((1, 4, 16)):
        seen = (dist % dil == 0) & (dist <= 64 * dil)
        alibi[:, g] = np.where(seen, dist, 1e30)
    alibi = tiles(alibi.reshape(S, -1))

    pool = np.zeros((S, 4, S), f)
    for g, w in enumerate((2, 4, 8, 16)):
        lo, hi = np.clip(t - w // 2, 0, S), np.clip(t + w // 2, 0, S)
        inside = (t[:, None] >= lo[None, :]) & (t[:, None] < hi[None, :])
        pool[:, g] = inside / (hi - lo)[None, :] - np.eye(S)
    pool = tiles(pool.reshape(S, -1))

    k, q = t[:, None], t[None, :]
    decay = np.stack([tiles(np.maximum(q - k, 0).astype(f)), tiles(np.maximum(k - q, 0).astype(f))], 1)
    return {"cons": cons, "alibi": np.ascontiguousarray(alibi), "pool_m": np.ascontiguousarray(pool.astype(f)),
            "decay_m": np.ascontiguousarray(decay.reshape(P, -1).astype(f))}


class Queues:

    def __init__(self):
        self.q = {n: [] for n in ("pe", "act", "dve", "pool", "sp")}
        self.n = {}
        self.seen = {n: {} for n in self.q}

    def wait(self, eng, deps):
        for d in deps:
            if d is None:
                continue
            if isinstance(d, list):
                self.wait(eng, d)
                continue
            s, v = d
            if self.seen[eng].get(s, 0) < v:
                self.seen[eng][s] = v
                self.q[eng].append(("wait", s, v))

    def op(self, eng, fn, *deps, sig=True):
        self.wait(eng, deps)
        if sig:
            self.n[eng] = self.n.get(eng, 0) + 1
        self.q[eng].append(("op", fn, (eng, 1) if sig else None))
        return (eng, self.n.get(eng, 0))

    def dma(self, eng, sem, out, src, *deps):
        self.wait(eng, deps)
        self.n[sem] = self.n.get(sem, 0) + 16
        self.q[eng].append(("op", lambda e: e.dma_start(out, src), (sem, 16)))
        return (sem, self.n[sem])


def plan(nc, T, dr, units, real):
    Q = Queues()
    op, dma = Q.op, Q.dma

    n_unit = len(units)
    st = {"dma": 0, "spl": 0, "use": 0}
    landed, released, prepared = {}, {}, {}
    spl_free = [None] * NSPL
    spl_ids = [i for i, u in enumerate(units) if u[3]]
    spl_no = {u: k for k, u in enumerate(spl_ids)}
    held = {}
    hold = [False]
    low = ["dve"]

    def resume():
        low[0] = "pool"
        hold[0] = False
        pump(1)
        hold[0] = True
        low[0] = "dve"

    def pump(most=None):
        if not real or hold[0]:
            return
        while True:
            moved = False
            i = st["dma"]
            if i < n_unit and (i < NRAW or (i - NRAW) in released):
                src, a, b, _ = units[i]
                dst = T["raw"][i % NRAW][:, 0:a * b].rearrange("p (a b) -> p a b", a=a)
                landed[i] = dma("sp", f"s_raw{i % NRAW}", dst, src, released.get(i - NRAW))
                st["dma"] += 1
                moved = True
            k = st["spl"]
            if k < len(spl_ids) and most != 0:
                i = spl_ids[k]
                if i in landed and (k < NSPL or held.get(k - NSPL)):
                    _, a, b, _ = units[i]
                    j = k % NSPL
                    raw = T["raw"][i % NRAW][:, 0:a * b]
                    hi, lo = T["whi"][j][:, 0:a * b], T["wlo"][j][:, 0:a * b]
                    t1 = op("act", lambda e, hi=hi, raw=raw: e.activation(hi, raw, ACT.Copy),
                            landed[i], held.get(k - NSPL))
                    t2 = op(low[0], lambda e, hi=hi, lo=lo, raw=raw:
                            e.tensor_tensor(lo, raw, hi.bitcast(F32), ALU.subtract), t1)
                    released[i] = [t1, t2]
                    prepared[i] = [t1, t2]
                    st["spl"] += 1
                    most = None if most is None else most - 1
                    moved = True
            if not moved:
                return

    def unit(src, a, b, split=True):
        i = st["use"]
        st["use"] += 1
        if hold[0]:
            hold[0] = False
        if not real:
            units.append((src, a, b, split))
            return (i, None, None, None)
        pump()
        if split:
            j = spl_no[i] % NSPL
            hi = T["whi"][j][:, 0:a * b].rearrange("p (a b) -> p a b", a=a)
            lo = T["wlo"][j][:, 0:a * b].rearrange("p (a b) -> p a b", a=a)
            return (i, hi, lo, prepared[i])
        raw = T["raw"][i % NRAW][:, 0:a * b].rearrange("p (a b) -> p a b", a=a)
        return (i, raw, None, landed[i])

    def done(u, tok):
        i = u[0]
        if real:
            if units[i][3]:
                held[spl_no[i]] = tok
            else:
                released[i] = tok
            pump()

    if not real:
        full = op

        def op(eng, fn, *deps, sig=True):
            return None

        def dma(*a):
            return None

    ring = deque((b, None) for b in range(8))

    def take():
        b, free = ring.popleft()
        return b, T["ps"][b], free

    def put(b, tok):
        ring.append((b, tok))

    def col(name, j=0, n=1):
        a = COLS[name][0] + j
        return T["cols"][:, a:a + n]

    def row(name, j, n):
        a = ROWS[name][0] + j
        return T["rows"][:, a:a + n]

    def con(name):
        a, b = CONS[name]
        return T["cons"][:, a:b]

    ident = con("ident")
    small_at = [0]

    def small(n):
        if small_at[0] + n > T["small"].shape[1]:
            small_at[0] = 0
        a = small_at[0]
        small_at[0] += n
        return T["small"][:, a:a + n]

    H = (T["Hh"], T["Hl"])
    B = (T["Bh"], T["Bl"])
    x, T1, T2, G, AR = T["x"], T["T1"], T["T2"], T["G"], T["AR"]

    def arena(a, n, **k):
        v = AR[:, a:a + n]
        return v

    def mm(out, lhsT, rhs, start, stop, *deps, sig=False):
        return op("pe", lambda e: e.matmul(out, lhsT, rhs, start=start, stop=stop), *deps, sig=sig)

    def mm3(out, lhsT, rhs, start, stop, *deps, sig=False):
        (lh, ll), (rh, rl) = lhsT, rhs
        mm(out, lh, rh, start, False, *deps)
        mm(out, lh, rl, False, False)
        return mm(out, ll, rh, False, stop, sig=sig)

    def tr(out, src, *deps, sig=False):
        return op("pe", lambda e: e.transpose(out, src, ident), *deps, sig=sig)

    def act(out, src, func, *deps, **k):
        return op("act", lambda e: e.activation(out, src, func, **k), *deps)

    def tt(out, a, b, o, *deps, eng="dve"):
        return op(eng, lambda e: e.tensor_tensor(out, a, b, o), *deps)

    def ts(out, a, s1, s2, o0, o1, *deps, eng="dve"):
        if o1 is None:
            return op(eng, lambda e: e.tensor_scalar(out, a, s1, None, o0), *deps)
        return op(eng, lambda e: e.tensor_scalar(out, a, s1, s2, o0, o1), *deps)

    def stt(out, a, s, b, o0, o1, *deps):
        return op("dve", lambda e: e.scalar_tensor_tensor(out=out, in0=a, scalar=s, in1=b, op0=o0, op1=o1), *deps)

    def red(out, a, o, *deps):
        return op("dve", lambda e: e.tensor_reduce(out, a, AX.X, o), *deps)

    def copy(out, a, *deps, eng="act"):
        if eng == "act":
            return act(out, a, ACT.Copy, *deps)
        return op(eng, lambda e: e.tensor_copy(out, a), *deps)

    def split(hi, lo, src, *deps):
        t1 = act(hi, src, ACT.Copy, *deps)
        t2 = tt(lo, src, hi.bitcast(F32), ALU.subtract, t1, *deps)
        return [t1, t2]

    def rsqrt(ap, n, scale, eps, *deps):
        t = ts(ap, ap, scale, eps, ALU.mult, ALU.add, *deps, eng="pool")
        return op("pool", lambda e: e.tensor_tensor(ap, ap, T["mhalf"][:, 0:n], ALU.pow), t, tok["mhalf"])

    def proj_T(u, rhs, n_k, blk0, out, *deps, k0=0, by_k=None):
        last = None
        for j in range(2):
            for k in range(n_k):
                c = (blk0 + j) * P
                last = mm3(out[:, j * S:(j + 1) * S],
                           (u[1][:, k, c:c + P], u[2][:, k, c:c + P]) if real else (0, 0),
                           (rhs[0][:, k0 + k, :], rhs[1][:, k0 + k, :]), k == 0, k == n_k - 1,
                           u[3], *deps, *(by_k[k] if by_k else ()), sig=(j == 1 and k == n_k - 1))
        return last

    def proj_tok256(u, lhs, out, *deps):
        last = None
        for t in range(2):
            for k in range(8):
                last = mm3(out[:, t * S:(t + 1) * S],
                           (lhs[0][:, k, t * P:(t + 1) * P], lhs[1][:, k, t * P:(t + 1) * P]),
                           (u[1][:, k, :], u[2][:, k, :]) if real else (0, 0), k == 0, k == 7,
                           u[3], *deps, sig=(t == 1 and k == 7))
        return last

    def w_unit8(w, c0, n=256):
        return w[:, c0:c0 + n].rearrange("(k p) c -> p k c", p=P)

    def tok_proj(w, c0, lhs, *deps):
        u = unit(w_unit8(w, c0), 8, S)
        b, ps, free = take()
        t = proj_tok256(u, lhs, ps, free, *deps)
        done(u, t)
        return b, ps, t

    def T_proj(w, c0, rhs, *deps):
        u = unit(w_unit8(w, c0), 8, S)
        b, ps, free = take()
        t = proj_T(u, rhs, 8, 0, ps, free, *deps)
        done(u, t)
        return b, ps, t

    def tok_tile(u, t, bank, lhs, lhs_split):
        last = None
        for k in range(8):
            last = mm3(bank[1][:, t * S:(t + 1) * S],
                       (lhs[0][:, k, t * P:(t + 1) * P], lhs[1][:, k, t * P:(t + 1) * P]),
                       (u[1][:, k, :], u[2][:, k, :]) if real else (0, 0), k == 0, k == 7,
                       u[3], lhs_split[k], bank[2], sig=(k == 7))
        return last

    def w_unit4(w, a, c0):
        return w[a * 512:(a + 1) * 512, c0:c0 + 512].rearrange("(k p) c -> p k c", p=P)

    def tok_part(u, a, t, bank, lhs, lhs_split, n_kt):
        last = None
        for k in range(4):
            kk = 4 * a + k
            last = mm3(bank[1][:, :],
                       (lhs[0][:, kk, t * P:(t + 1) * P], lhs[1][:, kk, t * P:(t + 1) * P]),
                       (u[1][:, k, :], u[2][:, k, :]) if real else (0, 0),
                       kk == 0, kk == n_kt - 1, u[3], bank[2], lhs_split[kk], sig=(k == 3))
        return last

    def out_proj(w, lhs, lhs_split):
        bs = [[take() for _ in range(2)] for _ in range(2)]
        us = [unit(w_unit4(w, i % 2, 512 * (i // 2)), 4, 512) for i in range(3)]
        res = [[None, None], [None, None]]

        def part(i, t):
            c = i // 2
            last = tok_part(us[i], i % 2, t, bs[t][c], lhs, lhs_split, 8)
            if i % 2:
                res[t][c] = (bs[t][c][0], bs[t][c][1], last)
            if t == 1:
                done(us[i], last)

        part(0, 0)
        part(0, 1)
        us.append(unit(w_unit4(w, 1, 512), 4, 512))
        hold[0] = True
        for t in range(2):
            for i in range(1, 4):
                part(i, t)
        return res

    def tok_projs(w, cs, lhs, lhs_split, end=False):
        us = [unit(w_unit8(w, c), 8, S) for c in cs]
        bs = [take() for _ in cs]
        res = []
        for t in range(2):
            for u, (b, ps, free) in zip(us, bs):
                last = tok_tile(u, t, (b, ps, free), lhs, lhs_split[t])
                if t == 1:
                    if end:
                        hold[0] = True
                    done(u, last)
                    res.append((b, ps, last))
        return res

    tok = {}
    tok["mhalf"] = op("pool", lambda e: e.memset(T["mhalf"][:, :], -0.5))
    tok["ones"] = op("pool", lambda e: e.memset(T["ones"][:, :], 1.0))
    tok["cons"] = dma("act", "s_cons", T["cons"][:, :], dr["cons"])
    tok["cols"] = dma("act", "s_cols", T["cols"][:, :], dr["cols"])
    tok["x"] = dma("act", "s_x", x[:, :, :], dr["x"].rearrange("(t p) d -> p t d", p=P))

    tok["idr"] = act(T["idr"][:, :], ident[0:16, 0:16], ACT.Copy, tok["cons"])

    csil = T["csil"]
    t_c = act(csil[:, :], col("c", 0, 8), ACT.Silu, tok["cols"])
    modT = T["modT"]
    mod_tok = {}

    mod_list = [(0, 1), (0, 0), (0, 2), (0, 4), (0, 3), (0, 5), (1, 1), (1, 0), (1, 2), (1, 4), (1, 3), (1, 5)]
    mod_steps = [(l, part, h, a) for l, part in mod_list[:2] for a in range(2) for h in range(2)]
    mod_steps += [(l, part, h, a) for l, part in mod_list[2:] for h in range(2) for a in range(2)]
    mod_work = deque(mod_steps)
    mod_acc = [AR[:, 7936 + 512 * i:8448 + 512 * i] for i in range(2)]
    mod_free = [None, None]
    mod_pend = []

    def mod_final(half=None):
        while mod_pend and (half is None or any(m[2] == half for m in mod_pend)):
            l, part, h, acc, e = mod_pend.pop(0)
            b, ps, free = take()
            for j in range(4):
                last = mm(ps[:, j:j + 1], acc[:, j * P:(j + 1) * P], T["ones"][:, 0:1], True, True, e, free,
                          tok["ones"], sig=(j == 3))
            mod_free[h] = last
            a = 48 * l + 8 * part + 4 * h
            t = tt(modT[:, a:a + 4], ps[:, 0:4], col("b_ada", a, 4), ALU.add, last, tok["cols"])
            put(b, t)
            if part in (1, 4):
                t = ts(modT[:, a:a + 4], modT[:, a:a + 4], 1.0, None, ALU.add, None, t)
            mod_tok.setdefault((l, part), []).append(t)

    def mod_step(n=1):
        for _ in range(n):
            if not mod_in:
                mod_final()
                return
            l, part, h, a = mod_work.popleft()
            slot, t_in = mod_in.popleft()
            acc = mod_acc[h]
            e = mod_run.get(h)
            if a == 0:
                mod_final(h)
            for k in range(4):
                wk = slot[:, k * 512:(k + 1) * 512]
                c = csil[:, 4 * a + k:4 * a + k + 1]
                if a == 0 and k == 0:
                    e = ts(acc, wk, c, None, ALU.mult, None, t_in, t_c, mod_free[h])
                else:
                    e = stt(acc, wk, c, acc, ALU.mult, ALU.add, t_in, e)
            mod_run[h] = e
            if slot is mod_once.get("slot"):
                mod_once["used"] = e
            else:
                mod_load(slot, e)
            if a == 1:
                mod_pend.append((l, part, h, acc, e))

    def mod_pair(acc, *deps):
        two = [(mod_work.popleft(), mod_in.popleft()) for _ in range(2)]
        for k in range(4):
            for (l, part, h, a), (slot, t_in) in two:
                wk = slot[:, k * 512:(k + 1) * 512]
                c = csil[:, 4 * a + k:4 * a + k + 1]
                if a == 0 and k == 0:
                    mod_run[h] = ts(acc[h], wk, c, None, ALU.mult, None, t_in, t_c)
                else:
                    mod_run[h] = stt(acc[h], wk, c, acc[h], ALU.mult, ALU.add, t_in, mod_run[h])
        for (l, part, h, a), (slot, t_in) in two:
            mod_load(slot, mod_run[h])
            if a == 1:
                mod_pend.append((l, part, h, acc[h], mod_run[h]))

    mod_run = {}
    mod_once = {}
    mod_src = deque(mod_steps)
    mod_in = deque()
    mod_left = [0]
    mod_sem = [0]

    def mod_load(slot, *deps):
        if not mod_left[0]:
            return
        mod_left[0] -= 1
        l, part, h, a = mod_src.popleft()
        c0 = part * D + h * 512
        src = dr["w_ada"][l][a * 512:(a + 1) * 512, c0:c0 + 512].rearrange("(k p) c -> p k c", p=P)
        mod_sem[0] = (mod_sem[0] + 1) % 8
        t = dma("sp", f"s_mod{mod_sem[0]}", slot.rearrange("p (k c) -> p k c", k=4), src, *deps)
        mod_in.append((slot, t))

    def mod_phase(n, slots, *deps, once=None):
        assert not mod_in
        mod_once["slot"] = None if once is None else slots[once]
        mod_left[0] = n
        for v in slots:
            mod_load(v, *deps)

    def mod_until(l, part):
        while any(w_[0:2] == (l, part) for w_ in mod_work):
            assert mod_in
            mod_step()
        mod_final()

    def mod_cols(l, part):
        return modT[:, 48 * l + 8 * part:48 * l + 8 * part + 8]

    def mod_rows(l, part):
        b, ps, free = take()
        m = mod_cols(l, part)
        t = op("pe", lambda e, o=ps[0:8, 0:P]: e.transpose(o, m, ident), mod_tok[(l, part)], free, tok["cons"])
        t = copy(T["crow"][0:8, 0:P], ps[0:8, 0:P], t)
        put(b, t)
        return t

    def mod_bcast(part, out, t, *deps):
        toks = []
        for h in range(2):
            b, ps, free = take()
            last = None
            for j in range(4):
                kk = 4 * h + j
                last = mm(ps[:, j * P:(j + 1) * P], ident[0:8, kk:kk + 1].broadcast_to([8, P]),
                          T["crow"][0:8, 0:P], True, True, t, free, sig=(j == 3))
            e = copy(out[:, h * 512:(h + 1) * 512], ps[:, :], last, *deps)
            put(b, e)
            toks.append(e)
        return toks

    def ln(src, dst, *deps):
        sb = small(12)
        for h in range(2):
            t = op("dve", lambda e, h=h: e.bn_stats(sb[:, 6 * h:6 * h + 6], src[:, 512 * h:512 * h + 512]), *deps)
        mv = small(2)
        t = op("dve", lambda e: e.bn_aggr(mv, sb), t)
        t = rsqrt(mv[:, 1:2], 1, 1.0, LN_EPS, t)
        return ts(dst, src, mv[:, 0:1], mv[:, 1:2], ALU.subtract, ALU.mult, t)

    def rms(src, dst, junk, *deps, dve=False):
        ss = small(1)
        t = act(junk, src, ACT.Square, *deps, accum_out=ss)
        t = rsqrt(ss, 1, 1.0 / D, RMS_EPS, t)
        if dve:
            return ts(dst, src, ss, None, ALU.mult, None, t)
        return act(dst, src, ACT.Copy, t, scale=ss)

    def ln_act(src, dst, *deps):
        sm, ss = small(1), small(1)
        t = act(dst, src, ACT.Copy, *deps, accum_out=sm)
        t = ts(sm, sm, -1.0 / D, None, ALU.mult, None, t, eng="pool")
        t1 = act(dst, src, ACT.Square, t, bias=sm, accum_out=ss)
        t = rsqrt(ss, 1, 1.0 / D, LN_EPS, t1)
        t = tt(sm, sm, ss, ALU.mult, t, t1, eng="pool")
        return act(dst, src, ACT.Identity, t, scale=ss, bias=sm)

    def H_turn(src, src_toks, t):
        out = []
        for kq in range(2):
            b, ps, free = take()
            for j in range(4):
                k = 4 * kq + j
                last = tr(ps[:, j * P:(j + 1) * P], src[:, t, k * P:(k + 1) * P], src_toks[t], free,
                          tok["cons"], sig=(j == 3))
            out.append((b, ps, last))
        return out

    def blocks(tile):
        return [tile[9]] * 4 + [tile[11]] * 4

    def to_H(src, scale, bias, src_toks, scr, *deps, slow=False, turned=None):
        toks, parts = [], []
        f3 = scr.rearrange("p (k s) -> p k s", s=S)
        for t in range(2):
            mine = []
            mine_ps = turned[2 * t:2 * t + 2] if turned else H_turn(src, src_toks, t)
            for kq in range(2):
                b, ps, last = mine_ps[kq]
                es = []
                for j in range(4):
                    k = 4 * kq + j
                    o, i = f3[:, k, t * P:(t + 1) * P], ps[:, j * P:(j + 1) * P]
                    sc, bi = scale[:, k:k + 1], None if bias is None else bias[:, k:k + 1]
                    if (t == 0 and slow) or kq == 1:
                        e = (act(o, i, ACT.Copy, last, *deps, scale=sc) if bias is None else
                             act(o, i, ACT.Identity, last, *deps, scale=sc, bias=bi))
                    elif bias is None:
                        e = ts(o, i, sc, None, ALU.mult, None, last, *deps)
                    else:
                        e = ts(o, i, sc, bi, ALU.mult, ALU.add, last, *deps)
                    es.append(e)
                put(b, es)
                mine += es
                parts.append((t, kq, es))
            for kq in range(2):
                v = (slice(None), slice(4 * kq, 4 * kq + 4), slice(t * P, (t + 1) * P))
                e = act(H[0][v], f3[v], ACT.Copy, parts[2 * t + kq][2])
                mine += [e, tt(H[1][v], f3[v], H[0][v].bitcast(F32), ALU.subtract, e)]
            toks.append(mine)
        return toks

    def head_scale(src, tmp, n, *deps):
        t = act(tmp, src, ACT.Square, *deps)
        ss = small(n)
        t = red(ss, tmp, ALU.add, t)
        return ss, rsqrt(ss, n, 1.0 / HD, RMS_EPS, t)

    def head_apply(src, dst, g, scaled, n, *deps):
        ss, t = scaled
        t_src = tt(dst, src, ss.unsqueeze(2).broadcast_to([P, n, HD]), ALU.mult, t, *deps)
        t = tt(dst, dst, g, ALU.mult, t_src, tok["rows"], eng="pool")
        return t, t_src

    def head_rms(src, dst, g, tmp, n, *deps):
        return head_apply(src, dst, g, head_scale(src, tmp, n, *deps), n, *deps)

    def rotate(x0, x1, o0, o1, c, s, t4, *deps):
        a = tt(t4[0], x0, c, ALU.mult, *deps, tok["cons"], eng="pool")
        b = tt(t4[1], x1, s, ALU.mult, *deps, eng="pool")
        cc = tt(t4[2], x0, s, ALU.mult, *deps, eng="pool")
        d = tt(t4[3], x1, c, ALU.mult, *deps, eng="pool")
        e = tt(o0, t4[0], t4[1], ALU.subtract, b, d, eng="pool")
        f = tt(o1, t4[2], t4[3], ALU.add, d, eng="pool")
        return f

    def head_softmax(Sb, n, qscale, toks_in, src=None, *deps):
        frm = Sb if src is None else src
        mx = small(2)
        t = red(mx, frm, ALU.max, toks_in, *deps)
        t = ts(mx, mx, -qscale, None, ALU.mult, None, t)
        sm = small(2)
        es = [act(Sb[:, i, :], frm[:, i, :], ACT.Exp, t, bias=mx[:, i:i + 1], scale=qscale,
                  accum_out=sm[:, i:i + 1]) for i in range(2)]
        t = op("dve", lambda e: e.reciprocal(sm, sm), es)
        rs = [ts(Sb[:, i, :], Sb[:, i, :], sm[:, i:i + 1], None, ALU.mult, None, t) for i in range(2)]
        return es, rs

    def probs_T(Sb, n_g, PT, toks, free_pt):
        outs = []
        for g in range(n_g):
            b, ps, free = take()
            last = None
            for kt in range(2):
                for qt in range(2):
                    last = tr(ps[:, kt * S + qt * P:kt * S + (qt + 1) * P],
                              Sb[:, qt, g * S + kt * P:g * S + (kt + 1) * P], toks[qt], free,
                              sig=(kt == 1 and qt == 1))
            e = copy(PT[:, g * 512:(g + 1) * 512], ps[:, :], last, free_pt, eng="act" if g % 2 == 0 else "dve")
            put(b, e)
            outs.append(e)
        return outs, last

    pair = {}

    def pv(h, n_g, PT, v, toks, dst_blk, v_tok):
        half = h % 2
        if half == 0:
            pair["b"] = take()
        b, ps, free = pair["b"]
        last = None
        n = 2 * n_g
        for g in range(n_g):
            for kt in range(2):
                i = 2 * g + kt
                last = mm(ps[64 * half:64 * half + 64, 0:S], v(g, kt), PT[:, i * S:(i + 1) * S],
                          i == 0, i == n - 1, toks, free, v_tok, sig=(i == n - 1))
        res = last
        if half == 1:
            t1 = act(B[0][:, dst_blk, :], ps[:, 0:S], ACT.Copy, last, free_B[0])
            t2 = tt(B[1][:, dst_blk, :], ps[:, 0:S], B[0][:, dst_blk, :].bitcast(F32), ALU.subtract, t1, free_B[0])
            put(b, [t1, t2])
            B_tok[dst_blk] = [t1, t2]
        return res

    free_B = [None]
    B_tok = {}

    def pipeline(heads, filler, per=(1,)):
        n = len(heads)
        for i in range(n + 2):
            if i < n:
                heads[i][0]()
            for _ in range(per[min(i, len(per) - 1)]):
                next(filler, None)
            if 0 <= i - 2 < n:
                heads[i - 2][2]()
            if 0 <= i - 1 < n:
                heads[i - 1][1]()
        for _ in filler:
            pass

    def ffn(n, ug, uu, ud, comb, h_t, hook, tail, *deps, hook2=lambda i: None, mid=lambda i: None,
            keep=True):
        acc = []
        act_done, pe_done, half_done = {}, {}, {}
        y = []

        def down(*ii):
            if not acc:
                acc.extend(take() for _ in range(4))
            us = [unit(*ud(i)) for i in ii]
            last = None
            for t in range(2):
                for i, u in zip(ii, us):
                    for c in range(2):
                        for f in range(2):
                            a = (i % 4) * 2 + f
                            last = mm3(acc[2 * t + c][1][:, :],
                                       (B[0][:, a, t * P:(t + 1) * P], B[1][:, a, t * P:(t + 1) * P]),
                                       (u[1][:, f, c * 512:(c + 1) * 512], u[2][:, f, c * 512:(c + 1) * 512])
                                       if real else (0, 0),
                                       i == 0 and f == 0, i == n - 1 and f == 1, u[3], act_done[i],
                                       acc[2 * t + c][2], sig=(f == 1))
                        if i == n - 1:
                            y.append(last)
                    if t == 1:
                        hold[0] = i == n - 1 or (keep and i >= n - 3)
                        low[0] = "dve" if keep or i < n - 3 else "pool"
                        done(u, last)
                        low[0] = "dve"
                        pe_done[i] = last

        def finish(i):
            s = T1[:, (i % 2) * 512:(i % 2) * 512 + 512]
            s3 = s.rearrange("p (f t) -> p f t", f=2)
            e = half_done[i]
            if comb is not None:
                cb, ct = comb(i)
                e = tt(s3, s3, cb.unsqueeze(1).broadcast_to([P, 2, S]), ALU.mult, e, ct, eng="pool")
            a = (i % 4) * 2
            act_done[i] = split(B[0][:, a:a + 2, :], B[1][:, a:a + 2, :], s3, e, pe_done.get(i - 4), free_B[0])

        lag = 2 if comb is not None else 1
        tu = None
        for i in range(n):
            ug_ = unit(*ug(i))
            bg, pg, fg = take()
            tg = proj_T(ug_, H, 8, 0, pg, fg, by_k=list(zip(blocks(h_t[0]), blocks(h_t[1]))))
            done(ug_, tg)
            mid(i)
            if lag == 2 and i == 2:
                finish(0)
            if lag == 2 and i in (3, 4):
                down(2 * (i - 3))
            uu_ = unit(*uu(i))
            bu, pu, fu = take()
            tu = proj_T(uu_, H, 8, 0, pu, fu)
            done(uu_, tu)
            s = T1[:, (i % 2) * 512:(i % 2) * 512 + 512]
            e = act(s, pg[:, :], ACT.Silu, tg, act_done.get(i - 2), *deps)
            put(bg, e)
            e = tt(s, s, pu[:, :], ALU.mult, e, tu)
            put(bu, e)
            half_done[i] = e
            hook(i)
            if lag == 2 and i < 2:
                continue
            if lag == 2 and i == 2:
                finish(1)
            finish(i)
            if i == n - 1:
                tail(tu)
            if lag == 2 and i in (3, 4):
                down(2 * i - 5)
            elif (5 if lag == 2 else 1) <= i < n - 2:
                down(i - 1)
            hook2(i)
        down(n - 3, n - 2, n - 1)
        free_B[0] = pe_done[n - 1]
        return acc, y, tu

    def first_layer(l, x_toks):
        w = dr["w_in"][l]
        xn = T1[:, :].rearrange("p (t d) -> p t d", t=2)
        turned = None
        if l == 0:
            t_n = [ln_act(x[:, t, :], xn[:, t, :], x_toks[t]) for t in range(2)]
            tok["rows"] = dma("act", "s_rows", T["rows"][:, :], dr["rows"].partition_broadcast(P))
            turned = H_turn(xn, t_n, 0) + H_turn(xn, t_n, 1)
            for acc in ([AR[:, 6144:6656], AR[:, 6656:7168]], mod_acc):
                mod_pair(acc)
                mod_pair(acc)
            mod_final()
            free_AR[0] = [mod_run.get(0), mod_run.get(1)]
            pump(0)
            mod_phase(12, mod_more + [AR[:, 0:2048]], free_AR[0], once=3)
            resume()

        else:
            t_n = [(ln if t else ln_act)(x[:, t, :], xn[:, t, :], x_toks[t], free_T1[t]) for t in range(2)]
            resume()
            mod_until(l, 1)
            mod_until(l, 0)
        h_t = to_H(xn, mod_cols(l, 1), mod_cols(l, 0), t_n, T2, mod_tok[(l, 0)], mod_tok[(l, 1)],
                   free_H[0], free_T2[0], slow=l > 0, turned=turned)
        h_toks = h_t[0] + h_t[1]
        qd, kd = arena(0, 1536), arena(1536, 1536)
        qd3 = qd.rearrange("p (b s) -> p b s", s=S)
        kd3 = kd.rearrange("p (b s) -> p b s", s=S)
        vd = arena(3072, 1536).rearrange("p (t c) -> p t c", t=2)
        PT = arena(4608, 1536)
        qaT = arena(6144, 1024).rearrange("p (j s) -> p j s", j=4)
        kaT = arena(7168, 256)
        va = arena(7424, 256).rearrange("p (t c) -> p t c", t=2)
        ka = arena(7680, 256).rearrange("p (t c) -> p t c", t=2)
        qa = arena(4608, 1024).rearrange("p (t c) -> p t c", t=2)
        fa = free_AR[0]

        us = [unit(w_unit4(w, a, 0), 4, 512) for a in range(2)]
        bs = [take() for _ in range(2)]
        ts_ = []
        for t in range(2):
            for a in range(2):
                last = tok_part(us[a], a, t, bs[t], H, blocks(h_t[t]), 8)
                if t == 1:
                    done(us[a], last)
            ts_.append(last)
        feed = mod_feed(l)
        next(feed, None)
        qa_t = []
        tq = []
        for t in range(2):
            tq.append(copy(qa[:, t, :].rearrange("p (j a d) -> p j a d", a=2, j=4),
                           bs[t][1][:, :].rearrange("p (a j d) -> p j a d", a=2, j=4), ts_[t], fa))
            put(bs[t][0], tq[t])
        next(feed, None)
        b, ps, t_p = tok_proj(w, 512, H, h_toks)
        next(feed, None)
        p3 = ps[:, :].rearrange("p (t c) -> p t c", t=2)
        t1 = copy(ka, p3[:, :, 0:128], t_p, fa)
        t_va = copy(va, p3[:, :, 128:256], t_p, fa)
        put(b, [t1, t_va])
        q_heads = [qa[:, t, :].rearrange("p (h d) -> p h d", d=HD) for t in range(2)]
        kav = ka.rearrange("p t (h d) -> p (t h) d", d=HD)
        sc_q = [head_scale(q_heads[t], T1[:, 512 * t:512 * t + 512].rearrange("p (h d) -> p h d", d=HD), 8, tq[t],
                           h_toks) for t in range(2)]
        sc_k = head_scale(kav, T2[:, 0:256].rearrange("p (h d) -> p h d", d=HD), 4, t1, h_toks)
        gq = row("qn", 64 * l, 64).unsqueeze(1).broadcast_to([P, 8, HD])
        gk = row("kn", 64 * l, 64).unsqueeze(1).broadcast_to([P, 4, HD])
        for t in range(2):
            tq[t], _ = head_apply(q_heads[t], q_heads[t], gq, sc_q[t], 8, tq[t])
        tk, _ = head_apply(kav, kav, gk, sc_k, 4, t1)
        for t in range(2):
            c = con("cos1")[:, 32 * t:32 * t + 32].unsqueeze(1).broadcast_to([P, 8, 32])
            s = con("sin1")[:, 32 * t:32 * t + 32].unsqueeze(1).broadcast_to([P, 8, 32])
            v = qa[:, t, :].rearrange("p (h i two) -> p h i two", h=8, two=2)
            t4 = [T1[:, 1024 + 256 * i:1280 + 256 * i].rearrange("p (h i) -> p h i", h=8) for i in range(4)]
            qa_t.append(rotate(v[:, :, :, 0], v[:, :, :, 1], v[:, :, :, 0], v[:, :, :, 1], c, s, t4, tq[t],
                               qa_t[-1] if qa_t else None))
        next(feed, None)
        for t in range(2):
            c = con("cos1")[:, 32 * t:32 * t + 32].unsqueeze(1).broadcast_to([P, 2, 32])
            s = con("sin1")[:, 32 * t:32 * t + 32].unsqueeze(1).broadcast_to([P, 2, 32])
            v = ka[:, t, :].rearrange("p (h i two) -> p h i two", h=2, two=2)
            t4 = [T2[:, 512 + 256 * t + 64 * i:576 + 256 * t + 64 * i].rearrange("p (h i) -> p h i", h=2)
                  for i in range(4)]
            tk = rotate(v[:, :, :, 0], v[:, :, :, 1], v[:, :, :, 0], v[:, :, :, 1], c, s, t4, tk)
        t_vd, t_qd, t_kd = [], [], []
        for i in range(3):
            b, ps, t_p = tok_proj(w, 2304 + S * i, H)
            e = copy(vd[:, :, S * i:S * i + S], ps[:, :].rearrange("p (t c) -> p t c", t=2), t_p, fa,
                     eng="dve" if i % 2 else "act")
            put(b, e)
            t_vd.append(e)
            next(feed, None)
        for dst, c0, lst in ((qd, 768, t_qd), (kd, 1536, t_kd)):
            for i in range(3):
                b, ps, t_p = T_proj(w, c0 + S * i, H)
                e = copy(dst[:, 512 * i:512 * i + 512], ps[:, :], t_p, fa, mod_once.get("used") if l == 0 else None, eng="dve" if i % 2 else "act")
                put(b, e)
                lst.append(e)
                next(feed, None)
        t_qa = []
        for jp in range(2):
            b, ps, free = take()
            last = None
            for j in range(2):
                for t in range(2):
                    jj = 2 * jp + j
                    v = qa[:, t, jj * P:(jj + 1) * P]
                    last = tr(ps[:, j * S + t * P:j * S + t * P + P], v, qa_t[t], free, sig=(j == 1 and t == 1))
            e = copy(qaT[:, 2 * jp:2 * jp + 2, :], ps[:, :].rearrange("p (j s) -> p j s", j=2), last, fa)
            put(b, e)
            t_qa.append(e)
        b, ps, free = take()
        for t in range(2):
            last = tr(ps[:, t * P:t * P + P], ka[:, t, :], tk, free, sig=(t == 1))
        t_ka = copy(kaT, ps[:, 0:S], last, fa)
        put(b, t_ka)

        G3 = G[:, :].rearrange("p (b s) -> p b s", s=S)
        g_tok = []
        for _ in feed:
            pass
        mod_g = [mod_run.get(0), mod_run.get(1)]

        def gates():
            for i in (4, 5, 6, 7, 0, 1, 2, 3):
                if i == 3:
                    for j in (2, 3):
                        v = G[:, 1024 * j:1024 * (j + 1)]
                        sg[j] = act(v, v, ACT.Sigmoid, g_tok)
                b, ps, t_p = T_proj(w, 3072 + S * i, H)
                e = copy(G3[:, 2 * i:2 * i + 2, :], ps[:, :].rearrange("p (b s) -> p b s", b=2), t_p, free_G[0], mod_g,
                         eng="dve" if i % 2 else "act")
                put(b, e)
                g_tok.append(e)
                free_H[0] = t_p
                next(feed, None)
                yield

        if l == 0:
            tok["alibi"] = dma("pool", "s_tab", T["TB"][:, 0:1536], dr["alibi"], mod_g)
        t_al = tok["alibi"]
        al = T["TB"][:, 0:1536].rearrange("p (t g s) -> p t g s", t=2, g=3)
        bufs = [T1[:, 0:1536], T2[:, 0:1536]]
        state = {}
        pt_free = [[fa, t_qa]]
        al_used = []

        def dilated(j, i):
            Sb = bufs[i % 2].rearrange("p (t n) -> p t n", t=2)

            def s1():
                toks = []
                for g in range(3):
                    n = 4 * g + j
                    b, ps, free = take()
                    last = None
                    o = 64 * (n % 2)
                    for qt in range(2):
                        last = mm(ps[:, qt * S:(qt + 1) * S], qd3[o:o + 64, n // 2, qt * P:(qt + 1) * P],
                                  kd3[o:o + 64, n // 2, :], True, True, free, t_qd, t_kd, sig=(qt == 1))
                    slope = float(np.float32(2.0) ** np.float32(-8.0 * (n + 1) / 12))
                    a3 = al[:, :, g, :]
                    e = stt(Sb[:, :, g * S:(g + 1) * S], a3, -8.0 * slope,
                            ps[:, :].rearrange("p (t s) -> p t s", t=2), ALU.mult, ALU.add, last, t_al,
                            state.get(i - 2), qa_t, tk, h_toks)
                    put(b, e)
                    toks.append(e)
                al_used.append(toks[-1])
                state[("p", i)] = head_softmax(Sb, 768, 0.125, toks)[1]

            def s2():
                state[("t", i)], state[i] = probs_T(Sb, 3, PT, state[("p", i)], pt_free[0])

            def s3():
                r = pv(j, 3, PT, lambda g, kt: vd[:, kt, (4 * g + j) * HD:(4 * g + j + 1) * HD],
                       state[("t", i)], 4 + j // 2, t_vd)
                pt_free[0] = r

            return s1, s2, s3
        def globl(h, i):
            Sb = bufs[i % 2][:, 512 * (i // 2 % 3):512 * (i // 2 % 3) + 512].rearrange("p (t n) -> p t n", t=2)
            pt = PT[:, 512 * (i % 3):512 * (i % 3) + 512]

            def s1():
                b, ps, free = take()
                last = None
                o = 64 * (h // 4)
                for qt in range(2):
                    last = mm(ps[:, qt * S:(qt + 1) * S], qaT[o:o + 64, h % 4, qt * P:(qt + 1) * P],
                              kaT[o:o + 64, :], True, True, free, t_qa, t_ka, sig=(qt == 1))
                es, state[("p", i)] = head_softmax(Sb, S, 0.125, last, ps[:, :].rearrange("p (t s) -> p t s", t=2),
                                                   state.get(i - 2), state.get(i - 6))
                put(b, es)

            def s2():
                state[("t", i)], state[i] = probs_T(Sb, 1, pt, state[("p", i)], pt_free[0])

            def s3():
                pt_free[0] = pv(h, 1, pt, lambda g, kt: va[:, kt, 64 * (h // 4):64 * (h // 4) + 64],
                                state[("t", i)], h // 2, t_va)

            return s1, s2, s3

        sg = [None] * 4
        tb = []

        def fillers():
            yield from gates()
            u = unit(dr["w_pb"][l].rearrange("(k p) c -> p k c", p=P), 2, D)
            for m in range(4):
                b, ps, free = take()
                last = proj_T(u, B, 2, 2 * m, ps, free, B_tok[4], B_tok[5], k0=4)
                if m == 3:
                    done(u, last)
                v = G[:, 2048 + 512 * m:2048 + 512 * m + 512]
                e = tt(v, v, ps[:, :], ALU.mult, last, sg[2 + m // 2])
                put(b, e)
                tb.append(e)
                yield

        pipeline([dilated(j, j) for j in range(4)] + [globl(h, 4 + h) for h in range(8)], fillers(),
                 (1, 1, 1, 1, 1, 1, 1, 0, 1, 1))
        free_TB[0] = al_used
        free_AR[0] = pt_free[0]
        mod_until(l, 2)
        row2 = mod_rows(l, 2)
        for i in (0, 1):
            v = G[:, 1024 * i:1024 * (i + 1)]
            sg[i] = act(v, v, ACT.Sigmoid, g_tok)
        m_toks = []
        for uu in range(2):
            u = unit(dr["w_pa"][l][:, uu * 512:uu * 512 + 512].rearrange("(k p) c -> p k c", p=P), 4, 512)
            for mm_ in range(2):
                m = 2 * uu + mm_
                b, ps, free = take()
                last = proj_T(u, B, 4, 2 * mm_, ps, free, [B_tok[i] for i in range(4)])
                v = G[:, 512 * m:512 * m + 512]
                vb = G[:, 2048 + 512 * m:2048 + 512 * m + 512]
                e = tt(v, v, ps[:, :], ALU.mult, last, sg[m // 2])
                put(b, e)
                e = tt(v, v, vb, ALU.add, e, tb[m], eng="pool")
                v3 = v.rearrange("p (k s) -> p k s", k=2)
                m_toks.append(split(H[0][:, 2 * m:2 * m + 2, :], H[1][:, 2 * m:2 * m + 2, :], v3, e, free_H[0]))
            done(u, last)
        free_B[0] = last
        B_tok.clear()
        lg = dma("pool", "s_lng", G[:, 1024:2048], dr["ln1_g"][l].partition_broadcast(P), m_toks)
        lb = dma("pool", "s_lnb", G[:, 2048:3072], dr["ln1_b"][l].partition_broadcast(P), m_toks)
        gb = mod_bcast(2, G[:, 0:1024], row2, m_toks)
        ys = out_proj(dr["w_out"][l], H, [m_toks[k // 2] for k in range(8)])
        free_H[0] = ys[1][1][2]
        t_n = []
        x_toks = residual_ln(ys, G[:, 0:1024], G[:, 1024:2048], G[:, 2048:3072], gb, lg, lb,
                             lambda t: T1[:, 1024 * t:1024 * t + 1024], [state[11], state[10], state[9], state[8]],
                             lambda e: t_n.append(ln_act(x[:, 0, :], xn[:, 0, :], e)))
        free_G[0] = x_toks
        t_n.append(ln(x[:, 1, :], xn[:, 1, :], x_toks[1]))
        resume()
        mod_until(l, 4)
        mod_until(l, 3)
        h_t = to_H(xn, mod_cols(l, 4), mod_cols(l, 3), t_n, T2, mod_tok[(l, 3)], mod_tok[(l, 4)], free_H[0],
                   [state[11], state[10]], slow=True)
        h_toks = h_t[0] + h_t[1]
        late = {}
        CB = G[:, :].rearrange("p (e s) -> p e s", s=S)

        mod_phase(24 if l == 0 else 4, [AR[:, 2048 * i:2048 * i + 2048] for i in range(3)], free_AR[0])

        def hook(i):
            if i == 1:
                late["row"] = comb_rows(late["rank"])
            if l == 0 and i < 15:
                mod_step()
            if l == 1 and i < 4:
                mod_step()
            if l == 1 and i == 5:
                mod_until(l, 5)
                mem_load(0)
            if i == 11:
                mod_until(l, 5)
            if i == 8 and l == 1:
                tok["gam"] = decays()
            if i == 12:
                if l == 1:
                    mem_norm(0)
                late["g2"] = mod_bcast(5, T1[:, 1024:2048], late["row"], h_toks)

        def mid(i):
            if i == 0:
                late["rank"], r_used = router_scores(h_toks)
                late["lg"] = dma("pool", "s_lng", T2[:, 0:1024], dr["ln2_g"][l].partition_broadcast(P),
                                 h_toks, r_used)
                late["lb"] = dma("pool", "s_lnb", T2[:, 1024:2048], dr["ln2_b"][l].partition_broadcast(P),
                                 h_toks, r_used)
            if i == 2:
                late["comb"] = comb_bcast(late["row"])
            if i == 12:
                late["row"] = mod_rows(l, 5)

        acc, y, tu = ffn(NE,
                         lambda i: (w_unit8(dr["w_g"][l, i], 0), 8, S),
                         lambda i: (w_unit8(dr["w_u"][l, i], 0), 8, S),
                         lambda i: (dr["w_d"][l, i].rearrange("(k p) c -> p k c", p=P), 2, D),
                         lambda i: (CB[:, i, :], late["comb"]), h_t, hook,
                         (lambda tok_: None) if l == 0 else (lambda tok_: mem_turn(0, tok_)), h_toks,
                         hook2=lambda i: mod_step() if l == 0 and 2 <= i <= 10 else None, mid=mid, keep=l == 0)
        g2 = late["g2"]
        free_H[0] = tu
        ys = [[(acc[2 * t + c][0], acc[2 * t + c][1], y[2 * t + c]) for c in range(2)] for t in range(2)]
        x_toks = residual_ln(ys, T1[:, 1024:2048], T2[:, 0:1024], T2[:, 1024:2048], g2, late["lg"], late["lb"],
                             lambda t: G[:, 1024 * t:1024 * t + 1024], None, lambda e: None)
        free_G[0] = x_toks
        free_T1[:] = x_toks
        free_T2[0] = x_toks
        return x_toks

    def mod_feed(l):
        for _ in range(12 if l == 0 else 0):
            mod_step()
            yield
        mod_step(0)
        mod_final()
        yield

    free_TB = [None]
    free_T1, free_T2, free_G, free_H, free_AR = [None, None], [None], [None], [None], [None]

    def residual_ln(ys, gate, lng, lnb, g_tok, lg_tok, lb_tok, tmp, deps, first):
        out = []
        for t in range(2):
            v = tmp(t)
            sb = small(12)
            e1 = []
            for c in range(2):
                b, ps, ty = ys[t][c]
                half = slice(512 * c, 512 * c + 512)
                e = tt(v[:, half], ps[:, :], gate[:, half], ALU.mult, ty, g_tok, deps)
                put(b, e)
                e = stt(x[:, t, half], x[:, t, half], ALPHA, v[:, half], ALU.mult, ALU.add, e)
                e1.append(op("dve", lambda e_, sb=sb[:, 6 * c:6 * c + 6], xv=x[:, t, half]: e_.bn_stats(sb, xv), e))
            mv = small(2)
            e1 = op("dve", lambda e_, sb=sb, mv=mv: e_.bn_aggr(mv, sb), e1)
            r = rsqrt(mv[:, 1:2], 1, 1.0, LN_EPS, e1)
            e = stt(v, x[:, t, :], mv[:, 0:1], lng, ALU.subtract, ALU.mult, e1, lg_tok)
            e = stt(x[:, t, :], v, mv[:, 1:2], lnb, ALU.mult, ALU.add, e, r, lb_tok)
            out.append(e)
            if t == 0:
                first(e)
        return out

    def router_scores(h_toks):
        Hf = T2[:, :].rearrange("p (k s) -> p k s", k=8)
        b, ps, free = take()
        last = None
        for t in range(2):
            for k in range(8):
                last = mm(ps[:, 16 * t:16 * t + 16], Hf[:, k, t * P:(t + 1) * P],
                          col("router", 16 * k, 16), k == 0, k == 7, h_toks, free, sig=(t == 1 and k == 7))
        R = T["R"]

        def r(a, n):
            return R[:, a:a + n]

        sc, sel = r(0, 32), r(32, 32)
        r_used = last
        e = act(sc, ps[:, 0:32], ACT.Sigmoid, last)
        put(b, e)
        rb = row("rb", 0, 16).unsqueeze(1).broadcast_to([P, 2, 16])
        e_sc = e
        e = tt(sel.rearrange("p (t e) -> p t e", t=2), sc.rearrange("p (t e) -> p t e", t=2), rb, ALU.add, e,
               tok["rows"])
        s4 = sel.rearrange("p (g e) -> p g e", e=4)
        rank, cmp_ = r(64, 32), r(96, 32)
        rk4, c4 = rank.rearrange("p (g e) -> p g e", e=4), cmp_.rearrange("p (g e) -> p g e", e=4)
        e = op("dve", lambda e_: e_.memset(rank, 0.0), e)
        pr = r(128, 8 * 6)
        n = 0
        ps_t = []
        for a in range(4):
            for b_ in range(a + 1, 4):
                sa, sb = s4[:, :, a:a + 1], s4[:, :, b_:b_ + 1]
                ps_t.append(tt(pr[:, 8 * n:8 * n + 8].unsqueeze(2), sa, sb, ALU.add, e, eng="pool"))
                e = tt(c4[:, :, 0:1], sb, sa, ALU.is_gt, e)
                e = tt(rk4[:, :, a:a + 1], rk4[:, :, a:a + 1], c4[:, :, 0:1], ALU.add, e)
                e = tt(c4[:, :, 1:2], sa, sb, ALU.is_ge, e)
                e = tt(rk4[:, :, b_:b_ + 1], rk4[:, :, b_:b_ + 1], c4[:, :, 1:2], ALU.add, e)
                n += 1
        gs = r(176, 8)
        e = red(gs, pr.rearrange("p (n g) -> p g n", n=6), ALU.max, ps_t, e)
        g4 = gs.rearrange("p (t g) -> p t g", g=4)
        gr = r(184, 8)
        gr4 = gr.rearrange("p (t g) -> p t g", g=4)
        e = op("dve", lambda e_: e_.memset(gr, 0.0), e)
        c2 = cmp_.rearrange("p (t g) -> p t g", t=2)
        for a in range(4):
            for b_ in range(a + 1, 4):
                e = tt(c2[:, :, 0:1], g4[:, :, b_:b_ + 1], g4[:, :, a:a + 1], ALU.is_gt, e)
                e = tt(gr4[:, :, a:a + 1], gr4[:, :, a:a + 1], c2[:, :, 0:1], ALU.add, e)
                e = tt(c2[:, :, 1:2], g4[:, :, a:a + 1], g4[:, :, b_:b_ + 1], ALU.is_ge, e)
                e = tt(gr4[:, :, b_:b_ + 1], gr4[:, :, b_:b_ + 1], c2[:, :, 1:2], ALU.add, e)
        e = ts(gr, gr, 0.5, None, ALU.is_lt, None, e)
        e = ts(rank, rank, 1.5, None, ALU.is_lt, None, e)
        e = tt(rk4, rk4, gr.unsqueeze(2).broadcast_to([P, 8, 4]), ALU.mult, e)
        e = tt(rank, rank, sc, ALU.mult, e)
        tot = r(192, 2)
        e = red(tot, rank.rearrange("p (t e) -> p t e", t=2), ALU.add, e)
        e = op("dve", lambda e_: e_.reciprocal(tot, tot), e)
        e = tt(rank.rearrange("p (t e) -> p t e", t=2), rank.rearrange("p (t e) -> p t e", t=2),
               tot.unsqueeze(2).broadcast_to([P, 2, 16]), ALU.mult, e)
        return e, r_used

    def comb_rows(e):
        rank = T["R"][:, 64:96]
        b, ps, free = take()
        for t in range(2):
            last = op("pe", lambda e_, t=t, ps=ps: e_.transpose(ps[0:16, t * P:(t + 1) * P], rank[:, 16 * t:16 * t + 16], ident),
                      e, free)
        e = split(B[0][0:16, 7, :], B[1][0:16, 7, :], ps[0:16, 0:S], last, free_B[0])
        put(b, e)
        return e

    def comb_bcast(e):
        outs = []
        for m in range(8):
            b, ps, free = take()
            for j in range(2):
                k = 2 * m + j
                one = T["idr"][:, k:k + 1].broadcast_to([16, P])
                mm(ps[:, j * S:(j + 1) * S], one, B[0][0:16, 7, :], True, False, e, free, tok["idr"])
                last = mm(ps[:, j * S:(j + 1) * S], one, B[1][0:16, 7, :], False, True, sig=(j == 1))
            c = copy(G[:, 512 * m:512 * m + 512], ps[:, :], last, free_G[0])
            put(b, c)
            outs.append(c)
        return outs

    mem_state = {}

    def mem_load(l):
        where = AR[:, 6144:8192] if l == 0 else G[:, 0:2048]
        where = where.rearrange("p (t d) -> p t d", t=2)
        mem_state["in"] = where, dma("sp", "s_mem", where, dr["mem"].rearrange("(t p) d -> p t d", p=P),
                                     free_AR[0], free_G[0], mod_run.get(0), mod_run.get(1), mod_free)

    def mem_norm(l):
        where, t_m = mem_state["in"]
        mn = AR[:, 0:2048].rearrange("p (t d) -> p t d", t=2)
        t_n = []
        for t in range(2):
            t_n.append(rms(where[:, t, :], mn[:, t, :], AR[:, 4096 + 1024 * t:5120 + 1024 * t], t_m, free_AR[0],
                           mod_run.get(0), mod_run.get(1)))
        if l:
            free_G[0] = [free_G[0], t_n]
        mem_state["n"] = t_n

    def mem_turn(l, last_H):
        mn = AR[:, 0:2048].rearrange("p (t d) -> p t d", t=2)
        mem_state["h"] = to_H(mn, col("mem_g", 8 * l, 8), None, mem_state["n"], AR[:, 2048:4096], last_H,
                              tok["cols"])

    gam = T["gam"]

    def decays():
        z, a, u, w, d, r_, m = (T["R"][:, 16 * i:16 * i + 16] for i in range(7))
        src = row("dec", 0, 16)
        e = ts(z, src, -1.0, None, ALU.mult, None, tok["rows"])
        e = tt(a, z, src, ALU.min, e)
        e = act(u, a, ACT.Exp, e)
        e1 = ts(w, u, 1.0, None, ALU.add, None, e)
        e2 = act(m, w, ACT.Ln, e1)
        e = ts(d, w, -1.0, None, ALU.add, None, e1)
        e = ts(r_, d, 1e-30, None, ALU.max, None, e)
        e = op("dve", lambda e_: e_.reciprocal(r_, r_), e)
        e = tt(r_, r_, u, ALU.mult, e)
        e = tt(r_, r_, m, ALU.mult, e, e2)
        e = stt(m, d, 0.0, u, ALU.is_equal, ALU.mult, e)
        e = tt(r_, r_, m, ALU.add, e)
        e = ts(a, src, 0.0, None, ALU.min, None, e)
        return tt(gam[:, :], a, r_, ALU.subtract, e)

    def to_T(src, dst, toks, *deps):
        b, ps, free = take()
        last = None
        for blk in range(2):
            for t in range(2):
                last = tr(ps[:, blk * S + t * P:blk * S + t * P + P], src[:, t, blk * P:(blk + 1) * P], toks, free,
                          sig=(blk == 1 and t == 1))
        if dst is None:
            return b, ps, last
        e = copy(dst, ps[:, :], last, *deps)
        put(b, e)
        return e

    def second_layer(l, x_toks, t_gam):
        w = dr["w_in2"][l]
        xn = T1[:, :].rearrange("p (t d) -> p t d", t=2)

        def t2(a):
            return arena(a * 512, 512)

        fa = free_AR[0]
        tiles = {}
        names = ["rq", "rk", "rv", "rg", "rqT", "rkT", "pv", "nq", "nk", "nv", "nqT", "nkT", "mq", "mqT",
                 "mk", "mkT", "mv"]
        for i, n in enumerate(names):
            tiles[n] = t2(i)

        def v3(n):
            return tiles[n].rearrange("p (t c) -> p t c", t=2)

        def vh(ap):
            return ap.rearrange("p (h d) -> p h d", d=HD)

        t_nab = dma("pool", "s_tab", T["TB"][:, :], dr["na_b"][:, l].rearrange("p t h s -> p (t h s)"), free_TB[0])
        ms = dict(mem_state)
        t_dec = dma("sp", "s_dec", G[:, 0:1024], dr["decay_m"], free_G[0])
        t_pm = dma("sp", "s_pm", G[:, 2048:4096], dr["pool_m"], free_G[0])
        t_n = [rms(x[:, t, :], xn[:, t, :], xn[:, t, :], x_toks[t], free_T1[t],
                   dve=t == 1) for t in range(2)]
        (bk, pk, tk), (bv, pvs, tv) = tok_projs(dr["w_kv"][l], (0, S), H, [blocks(ms["h"][t]) for t in range(2)], end=True)
        resume()
        t_mem = ms["h"][0] + ms["h"][1]
        h_t = to_H(xn, col("mix_g", 8 * l, 8), None, t_n, T2, tv, t_n, free_T2[0])
        h2 = h_t[0] + h_t[1]
        fa = [fa, t_mem, ms["n"]]

        hr_last = [None]

        def hr(src_ps, name, g, t_in):
            t, ts_ = head_rms(vh(src_ps), vh(tiles[name]), row(g, 64 * l, 64).unsqueeze(1).broadcast_to([P, 8, HD]),
                              vh(T1[:, 512:1024]), 8, t_in, fa, h2, hr_last[0])
            hr_last[0] = ts_
            return t, ts_
        t_mk, t_s = hr(pk[:, :], "mk", "mk", tk)
        put(bk, t_s)
        t_mv = copy(tiles["mv"], pvs[:, :], tv, fa)
        put(bv, t_mv)

        (b, ps, t_p), rq_p = tok_projs(w, (3 * S, 0), H, [blocks(h_t[t]) for t in range(2)])
        t_rg = act(tiles["rg"], ps[:, :], ACT.Silu, t_p, fa)
        put(b, t_rg)
        rot = {}
        prev = None
        for n, name in enumerate(("rq", "rk")):
            b, ps, t_p = rq_p if n == 0 else tok_proj(w, n * S, H)
            e = copy(tiles[name], ps[:, :], t_p, fa)
            put(b, e)
            for t in range(2):
                c = con("cos2")[:, 32 * t:32 * t + 32].unsqueeze(1).broadcast_to([P, 4, 32])
                s = con("sin2")[:, 32 * t:32 * t + 32].unsqueeze(1).broadcast_to([P, 4, 32])
                v = v3(name)[:, t, :].rearrange("p (h two i) -> p h two i", two=2, i=32)
                t4 = [T1[:, 1024 + 128 * i:1152 + 128 * i].rearrange("p (h i) -> p h i", h=4) for i in range(4)]
                prev = rotate(v[:, :, 0, :], v[:, :, 1, :], v[:, :, 0, :], v[:, :, 1, :], c, s, t4, e, prev, h2)
            rot[name] = prev
        b, ps, t_p = tok_proj(w, 2 * S, H)
        t_rv = copy(tiles["rv"], ps[:, :], t_p, fa, eng="dve")
        put(b, t_rv)
        DT = T2
        t_D = []
        for h in range(4):
            o = DT[:, 512 * h:512 * h + 512]
            a_, b_ = G[:, 0:512], G[:, 512:1024]
            e = ts(o, a_, gam[:, 4 * l + h:4 * l + h + 1], None, ALU.mult, None, t_dec, t_gam, h2)
            e = stt(o, b_, gam[:, 8 + 4 * l + h:8 + 4 * l + h + 1], o, ALU.mult, ALU.add, e)
            e_dec = e
            t_D.append(act(o, o, ACT.Exp, e))
        b, ps, t_p = tok_proj(w, 4 * S, H)
        t_pv = copy(tiles["pv"], ps[:, :], t_p, fa)
        put(b, t_pv)
        t_rq = to_T(v3("rq"), tiles["rqT"], rot["rq"], fa)
        t_rk = to_T(v3("rk"), tiles["rkT"], rot["rk"], fa)

        qt_tok = {}

        def nh(name, c0, g):
            b, ps, t_p = tok_proj(w, c0, H)
            qt_tok[name], t_s = hr(ps[:, :], name, g, t_p)
            put(b, t_s)

        nh("nq", 5 * S, "naq")
        rqT = tiles["rqT"].rearrange("p (b s) -> p b s", b=2)
        rkT = tiles["rkT"].rearrange("p (b s) -> p b s", b=2)
        bo, po, fo = take()
        t_sd = {}
        t_ret = {}

        def ret_s(h):
            b, ps, free = take()
            o = 64 * (h % 2)
            last = None
            for kt in range(2):
                last = mm(ps[:, kt * S:(kt + 1) * S], rkT[o:o + 64, h // 2, kt * P:(kt + 1) * P],
                          rqT[o:o + 64, h // 2, :], True, True, t_rq, t_rk, free, sig=(kt == 1))
            d = DT[:, 512 * h:512 * h + 512]
            t_sd[h] = stt(d, ps[:, :], 0.125, d, ALU.mult, ALU.mult, last, t_D[h])
            put(b, t_sd[h])

        def ret_o(h):
            for qt in range(2):
                for kt in range(2):
                    o = qt * S + h * HD
                    t_ret[h] = mm(po[:, o:o + HD],
                                  DT[:, 512 * h + kt * S + qt * P:512 * h + kt * S + qt * P + P],
                                  v3("rv")[:, kt, h * HD:(h + 1) * HD], kt == 0, kt == 1, t_sd[h], t_rv, fo,
                                  sig=(kt == 1 and qt == 1))

        ret_s(0)
        ret_s(1)
        nh("nk", 6 * S, "nak")
        ret_o(0)
        ret_s(2)
        ret_o(1)
        ret_s(3)
        b, ps, t_p = tok_proj(w, 7 * S, H)
        t_nv = copy(tiles["nv"], ps[:, :], t_p, fa, eng="dve")
        put(b, t_nv)
        ret_o(2)
        ret_o(3)
        ret_all = list(t_ret.values())
        rt = tiles["rq"]
        tmp = vh(T1[:, 512:1024])
        t0 = act(tmp, vh(po[:, :]), ACT.Square, ret_all, hr_last[0])
        ss = small(8)
        t = red(ss, tmp, ALU.add, t0)
        hr_last[0] = t
        t = rsqrt(ss, 8, 1.0 / HD, RMS_EPS, t)
        t = tt(vh(rt), vh(po[:, :]), ss.unsqueeze(2).broadcast_to([P, 8, HD]), ALU.mult, t, t_rq)
        put(bo, t)
        r3 = rt.rearrange("p (t c) -> p t c", t=2)
        t = tt(r3, r3, row("ret", S * l, S).unsqueeze(1).broadcast_to([P, 2, S]), ALU.mult, t, eng="pool")
        t_r = tt(rt, rt, tiles["rg"], ALU.mult, t, t_rg, eng="pool")
        nh("mq", 8 * S, "mq")
        t_nq = to_T(v3("nq"), tiles["nqT"], qt_tok["nq"], fa)
        t_nk = to_T(v3("nk"), tiles["nkT"], qt_tok["nk"], fa)
        t_mkT = to_T(v3("mk"), tiles["mkT"], t_mk, fa)
        pm = G[:, 2048:4096].rearrange("p (a s) -> p a s", s=S)
        b, ps, free = take()
        last = None
        for g in range(4):
            for kt in range(2):
                last = mm(ps[64 * (g % 2):64 * (g % 2) + 64, (g // 2) * S:(g // 2) * S + S],
                          v3("pv")[:, kt, g * HD:(g + 1) * HD], pm[:, 4 * kt + g, :],
                          kt == 0, kt == 1, t_pm, t_pv, free, sig=(g == 3 and kt == 1))
        free_G[0] = [last, e_dec]
        pl = tiles["rk"]
        t = copy(pl, ps[:, :], last, t_rk)
        put(b, t)
        b, ps, free = take()
        for g in range(4):
            o = 64 * (g % 2)
            a = 128 * l + 64 * (g // 2)
            c0 = COLS["pool_w"][0] + a
            last = mm(ps[o:o + 64, (g // 2) * S:(g // 2) * S + S], T["cols"][o:o + 64, c0:c0 + 64],
                      pl[o:o + 64, (g // 2) * S:(g // 2) * S + S], True, True, t, free, sig=(g == 3))
        es = []
        for j in range(2):
            s_ = col("pool_s", 2 * l + j, 1)
            es.append(ts(pl[:, j * S:(j + 1) * S], ps[:, j * S:(j + 1) * S], s_, None, ALU.mult, None, last))
        put(b, es)
        t_b = split(B[0][:, 2:4, :], B[1][:, 2:4, :], pl.rearrange("p (b s) -> p b s", b=2), es, free_B[0])
        br_tok = {1: t_b}
        b, ps, t = to_T(r3, None, t_r)
        t1 = act(B[0][:, 0:2, :], ps[:, :].rearrange("p (b s) -> p b s", b=2), ACT.Copy, t, free_B[0])
        t2_ = tt(B[1][:, 0:2, :], ps[:, :].rearrange("p (b s) -> p b s", b=2), B[0][:, 0:2, :].bitcast(F32),
                 ALU.subtract, t1)
        put(b, [t1, t2_])
        br_tok[0] = [t1, t2_]
        t_mq = to_T(v3("mq"), tiles["mqT"], qt_tok["mq"], fa)
        bias = T["TB"][:, :].rearrange("p (a s) -> p a s", s=S)
        t_bias = tt(bias, bias, con("mask").unsqueeze(1).broadcast_to([P, 8, S]), ALU.add, t_nab)
        b_used = []
        state = {}
        G3 = G[:, :].rearrange("p (b s) -> p b s", s=S)
        g_tok = {}
        wg = dr["w_gate"][l]
        order = [1, 0, 2, 3]

        def gate_units(n, slot, func):
            g_tok[n] = []
            for i in range(4):
                b, ps, t_p = T_proj(wg, n * D + S * i, H)
                o = G3[:, 8 * slot + 2 * i:8 * slot + 2 * i + 2, :]
                e = act(o, ps[:, :].rearrange("p (b s) -> p b s", b=2), func, t_p, free_G[0], g_used.get(slot))
                put(b, e)
                g_tok[n].append(e)
                free_H[0] = t_p
                yield

        g_used = {}

        def filler():
            for n, slot in ((1, 0), (0, 1)):
                for _ in gate_units(n, slot, ACT.Copy):
                    yield

        pt_free = [ret_all]

        def head(kind, h, i):
            Sb = T1[:, 512 * (i % 4):512 * (i % 4) + 512].rearrange("p (t n) -> p t n", t=2)
            pt = T2[:, 512 * (i % 4):512 * (i % 4) + 512]
            qT, kT, v = (tiles[n] for n in (("nqT", "nkT", "nv") if kind == "n" else ("mqT", "mkT", "mv")))
            tq, tk_, tv_ = (t_nq, t_nk, t_nv) if kind == "n" else (t_mq, t_mkT, t_mv)
            o = 64 * (h % 2)
            blk = h // 2

            def s1():
                b, ps, free = take()
                last = None
                for qt in range(2):
                    last = mm(ps[:, qt * S:(qt + 1) * S], qT[o:o + 64, blk * S + qt * P:blk * S + (qt + 1) * P],
                              kT[o:o + 64, blk * S:(blk + 1) * S], True, True, free, tq, tk_, sig=(qt == 1))
                p3 = ps[:, :].rearrange("p (t s) -> p t s", t=2)
                if kind == "n":
                    b4 = bias.rearrange("p (t h) s -> p t h s", h=4)[:, :, h, :]
                    e = stt(Sb, p3, 0.125, b4, ALU.mult, ALU.add, last, t_bias, state.get(i - 4), t_r, t0,
                            qt_tok["mq"])
                    b_used.append(e)
                    put(b, e)
                    state[("p", i)] = head_softmax(Sb, S, 1.0, e)[1]
                else:
                    es, state[("p", i)] = head_softmax(Sb, S, 0.125, last, p3, state.get(i - 4))
                    put(b, es)
                if kind == "n" and h == 3:
                    free_TB[0] = b_used

            def s2():
                state[("t", i)], state[i] = probs_T(Sb, 1, pt, state[("p", i)], pt_free[0])

            def s3():
                pt_free[0] = pv(h, 1, pt, lambda g, kt: v.rearrange("p (t c) -> p t c", t=2)[:, kt, h * HD:(h + 1) * HD],
                                state[("t", i)], (4 if kind == "n" else 6) + h // 2, tv_)

            return s1, s2, s3

        pipeline([head("n", h, h) for h in range(4)] + [head("m", h, 4 + h) for h in range(4)], filler())
        br_tok[2] = [B_tok[4], B_tok[5]]
        br_tok[3] = [B_tok[6], B_tok[7]]
        free_AR[0] = pt_free[0]
        for n, slot in ((1, 0), (0, 1)):
            v = G[:, 2048 * slot:2048 * slot + 2048]
            for hh in range(2):
                vv = v[:, 1024 * hh:1024 * hh + 1024]
                g_tok[n].append(act(vv, vv, ACT.Sigmoid, g_tok[n][0:4]))
        m_toks = []
        s_done = [state[7], state[6], state[5], state[4]]
        prev = {}
        for z, n in enumerate(order):
            slot = z % 2
            if z >= 2:
                for _ in gate_units(n, slot, ACT.Sigmoid):
                    pass
            u = unit(dr["w_br"][l, n].rearrange("(k p) c -> p k c", p=P), 2, D)
            used = []
            for m in range(4):
                b, ps, free = take()
                last = proj_T(u, B, 2, 2 * m, ps, free, br_tok[n], k0=2 * n)
                gv = G[:, 2048 * slot + 512 * m:2048 * slot + 512 * m + 512]
                tv_ = T1[:, 512 * m:512 * m + 512]
                if z == 0:
                    e = tt(tv_, gv, ps[:, :], ALU.mult, last, g_tok[n], s_done)
                    put(b, e)
                else:
                    e = tt(gv, gv, ps[:, :], ALU.mult, last, g_tok[n])
                    put(b, e)
                    e = tt(tv_, tv_, gv, ALU.add, e, prev[m], eng="pool" if m % 2 else "dve")
                prev[m] = e
                used.append(e)
                if z == 3:
                    m_toks.append(split(H[0][:, 2 * m:2 * m + 2, :], H[1][:, 2 * m:2 * m + 2, :],
                                        tv_.rearrange("p (k s) -> p k s", k=2), e, free_H[0]))
            done(u, last)
            g_used[slot] = used
        free_G[0] = [g_used[0], g_used[1]]
        free_B[0] = last
        B_tok.clear()
        x_t = [None, None]
        xs = [[], []]
        ys = out_proj(dr["w_out2"][l], H, [m_toks[k // 2] for k in range(8)])
        for t in range(2):
            for c in range(2):
                xv = x[:, t, 512 * c:512 * c + 512]
                e = tt(xv, xv, ys[t][c][1][:, :], ALU.add, ys[t][c][2], t_n)
                put(ys[t][c][0], e)
                xs[t].append(e)
        free_H[0] = ys[1][1][2]
        t_n = [rms(x[:, t, :], xn[:, t, :], xn[:, t, :], xs[t], m_toks, pt_free[0], dve=t == 1)
               for t in range(2)]
        resume()
        h3_t = to_H(xn, col("ffn_g", 8 * l, 8), None, t_n, T2, free_H[0], t_n)
        h3 = h3_t[0] + h3_t[1]
        wf, wd = dr["w_ff1"][l], dr["w_ff2"][l]

        def hook(i):
            if l == 0 and i == 2:
                mem_load(1)
            if l == 0 and i == 6:
                mem_norm(1)

        acc, y, tu = ffn(11, lambda i: (w_unit8(wf, S * i), 8, S),
                         lambda i: (w_unit8(wf, FF + S * i), 8, S),
                         lambda i: (wd[S * i:S * i + S, :].rearrange("(k p) c -> p k c", p=P), 2, D),
                         None, h3_t, hook,
                         (lambda tok_: mem_turn(1, tok_)) if l == 0 else (lambda tok_: None), h3, keep=l == 1)
        free_H[0] = tu
        out = [[], []]
        for t in range(2):
            for c in range(2):
                xv = x[:, t, 512 * c:512 * c + 512]
                b, ps, _ = acc[2 * t + c]
                e = tt(xv, xv, ps[:, :], ALU.add, y[2 * t + c])
                put(b, e)
                out[t].append(e)
        resume()
        free_T1[:] = [[y, h3]] * 2
        free_T2[0] = h3
        return out

    mod_more = [T["TB"][:, :], G[:, 0:2048], G[:, 2048:4096]]
    mod_phase(8, mod_more + [AR[:, 2048 * i:2048 * i + 2048] for i in range(3)] + [T2[:, :]])
    xt = [tok["x"], tok["x"]]
    for l in range(L):
        xt = first_layer(l, xt)
    for l in range(L):
        xt = second_layer(l, xt, tok["gam"])
    t_out = []
    for t in range(2):
        dma("sp", "s_out", dr["out"][t * P:(t + 1) * P, :], x[:, t, :], xt[t])
    Q.wait("sp", [("s_out", 32)])
    return Q


def build(nc, dr):
    ctx = ExitStack()
    with ctx:
        def sb(name, shape, dt=F32):
            return ctx.enter_context(nc.sbuf_tensor(name, shape, dt))

        T = {
            "raw": [sb(f"raw{i}", [P, 2048]) for i in range(NRAW)],
            "whi": [sb(f"whi{i}", [P, 2048], F32R) for i in range(NSPL)],
            "wlo": [sb(f"wlo{i}", [P, 2048], F32R) for i in range(NSPL)],
            "Hh": sb("Hh", [P, 8, S], F32R), "Hl": sb("Hl", [P, 8, S], F32R),
            "Bh": sb("Bh", [P, 8, S], F32R), "Bl": sb("Bl", [P, 8, S], F32R),
            "x": sb("xs", [P, 2, D]), "T1": sb("T1", [P, 2048]), "T2": sb("T2", [P, 2048]),
            "G": sb("G", [P, 4096]), "AR": sb("AR", [P, 8960]),
            "cons": sb("cons_s", [P, N_CONS]), "cols": sb("cols_s", [P, N_COLS]), "rows": sb("rows_s", [P, N_ROWS]),
            "csil": sb("csil", [P, 8]), "modT": sb("modT", [P, 96]), "crow": sb("crow", [8, P]),
            "idr": sb("idr", [16, 16], F32R),
            "TB": sb("TB", [P, 2048]), "R": sb("R", [P, 200]), "gam": sb("gam", [P, 16]),
            "small": sb("small", [P, 200]), "ones": sb("ones", [P, 2]), "mhalf": sb("mhalf", [P, 8]),
            "ps": [ctx.enter_context(nc.psum_tensor(f"ps{i}", [P, 512], F32)) for i in range(8)],
        }
        units = []
        plan(nc, T, dr, units, False)
        Q = plan(nc, T, dr, units, True)
        sems = {}
        for name in sorted({s for q in Q.q.values() for it in q if it[0] == "op" and it[2] for s in [it[2][0]]}):
            sems[name] = ctx.enter_context(nc.semaphore("c_" + name))

        def emit(eng, e):
            for it in Q.q[eng]:
                if it[0] == "wait":
                    e.wait_ge(sems[it[1]], it[2])
                else:
                    ins = it[1](e)
                    if it[2]:
                        ins.then_inc(sems[it[2][0]], it[2][1])

        block = ctx.enter_context(nc.Block())

        @block.sync
        def _(e):
            emit("sp", e)

        @block.gpsimd
        def _(e):
            emit("pool", e)

        @block.scalar
        def _(e):
            emit("act", e)

        @block.tensor
        def _(e):
            emit("pe", e)

        @block.vector
        def _(e):
            emit("dve", e)


def kernel(**inp):
    import concourse.bacc as bacc
    from concourse.bass_utils import run_bass_kernel_spmd

    a = {k: np.ascontiguousarray(np.asarray(v)) for k, v in inp.items()}

    def columns(v):
        return v.reshape(-1, P).T

    pw = a["pool_w_2"].reshape(L, 2, 2, HD, HD).transpose(2, 3, 0, 1, 4).reshape(P, -1)
    router = a["w_router"].reshape(8, P, NE).transpose(1, 0, 2).reshape(P, -1)
    cols = np.concatenate([columns(a["c"]), columns(a["b_ada"]), columns(a["norm_mix_g_2"]),
                           columns(a["norm_mem_g_2"]), columns(a["norm_ffn_g_2"]), columns(a["pool_scale_2"]),
                           router, pw], 1)
    rows = np.concatenate([a[n].reshape(-1) for n in (
        "q_norm_g", "k_norm_g", "na_q_norm_g_2", "na_k_norm_g_2", "mem_q_norm_g_2", "mem_k_norm_g_2",
        "ret_norm_g_2", "router_bias", "ret_decay_fwd_2", "ret_decay_bwd_2")])
    t = np.arange(S)
    r_off = (t[None, :] // 64 - t[:, None] // 64) + 7
    c_off = np.clip(t[None, :] % 64 - t[:, None] % 64, -15, 15) + 15
    na = a["na_rpb_2"][:, :, r_off, c_off]
    na = na.reshape(L, 4, 2, P, S).transpose(3, 0, 2, 1, 4)

    arrays = {
        "x": a["x"][0], "mem": a["mem_2"][0], "cols": cols, "rows": rows, "na_b": na,
        "w_ada": a["w_ada"], "w_in": a["w_in"], "w_pa": a["w_branch_a"], "w_pb": a["w_branch_b"],
        "w_out": a["w_out"], "ln1_g": a["ln1_g"], "ln1_b": a["ln1_b"], "ln2_g": a["ln2_g"], "ln2_b": a["ln2_b"],
        "w_g": a["w_exp_gate"], "w_u": a["w_exp_up"], "w_d": a["w_exp_down"],
        "w_in2": a["w_in_2"], "w_gate": a["w_gate_2"], "w_kv": a["w_mem_kv_2"], "w_br": a["w_branch_2"],
        "w_out2": a["w_out_2"], "w_ff1": a["w_ffn_in_2"], "w_ff2": a["w_ffn_out_2"],
    }
    arrays.update(shape_constants())
    nc = bacc.Bacc("TRN2", target_bir_lowering=False, num_devices=1)
    feed, dr = {}, {}
    for k, v in arrays.items():
        v = np.ascontiguousarray(v)
        feed["in_" + k] = v
        dr[k] = nc.dram_tensor("in_" + k, v.shape, F32, kind="ExternalInput").ap()
    dr["out"] = nc.dram_tensor("out_0", (S, D), F32, kind="ExternalOutput").ap()
    build(nc, dr)
    r = run_bass_kernel_spmd(nc, [feed], core_ids=[0])
    return r.results[0]["out_0"].reshape(1, S, D)
```
